# Optimizing a Trainium2 kernel written in Bass

```python
import jax, jax.numpy as jnp
from jax import lax
import numpy as np

D_MODEL = 1024
BATCH = 1
SEQ = 512
DEPTH = 1

CHUNK = 64
N_META = 16
PAD = CHUNK - N_META
A_KDIM = 128
A_HEADS = D_MODEL // A_KDIM
A_FDIM = A_HEADS * A_KDIM
A_WIDTH = D_MODEL // 2
A_VDIM = A_WIDTH // A_HEADS
POOL_WINDOWS = (2, 4, 8, 16)
B_GROUPS = 4
B_WIDTH = D_MODEL // 2
B_GDIM = B_WIDTH // B_GROUPS
N_BRANCH = 2
SPLITS = (A_FDIM, 2 * A_FDIM, 2 * A_FDIM + A_WIDTH, 2 * A_FDIM + 2 * A_WIDTH,
          2 * A_FDIM + 2 * A_WIDTH + B_WIDTH, 2 * A_FDIM + 2 * A_WIDTH + B_WIDTH + D_MODEL)
IN_COLS = 2 * A_FDIM + 2 * A_WIDTH + B_WIDTH + N_BRANCH * D_MODEL
D_FF = ((8 * D_MODEL // 3 + 127) // 128) * 128
CONV_W = 3
EPS = 1e-6


def rmsnorm(x, g):
    xf = x.astype(jnp.float32)
    y = xf * lax.rsqrt(jnp.mean(xf * xf, axis=-1, keepdims=True) + EPS)
    return (y * g.astype(jnp.float32)).astype(x.dtype)

def hgrn2_mixer(q, f_logit, i, og, lb, head_g):
    dt = i.dtype
    f32 = jnp.float32
    B_, T, _ = q.shape
    n_chunks = (T + PAD) // CHUNK
    lbf = lb.astype(f32)
    f = lbf + (1.0 - lbf) * jax.nn.sigmoid(f_logit.astype(f32))
    k = 1.0 - f
    logf = jnp.log(f)
    qf = jax.nn.silu(q.astype(f32))
    vf = i.astype(f32)

    def to_chunks(t, d):
        t = jnp.pad(t, ((0, 0), (PAD, 0), (0, 0)))
        return t.reshape(B_, n_chunks, CHUNK, A_HEADS, d).transpose(1, 0, 3, 2, 4)

    qc = to_chunks(qf, A_KDIM)
    kc = to_chunks(k, A_KDIM)
    vc = to_chunks(vf, A_VDIM)
    ac = jnp.cumsum(to_chunks(logf, A_KDIM), axis=3)
    causal = jnp.tril(jnp.ones((CHUNK, CHUNK), dtype=bool))[:, :, None]

    def step(S, inp):
        q_, k_, v_, a_ = inp
        o_inter = jnp.einsum('bhtk,bhkv->bhtv', q_ * jnp.exp(a_), S)
        diff = a_[:, :, :, None, :] - a_[:, :, None, :, :]
        decay = jnp.exp(jnp.where(causal, diff, -jnp.inf))
        scores = jnp.einsum('bhtsk,bhsk->bhts', q_[:, :, :, None, :] * decay, k_)
        o = o_inter + jnp.einsum('bhts,bhsv->bhtv', scores, v_)
        a_last = a_[:, :, -1:, :]
        S = jnp.exp(a_last[:, :, 0, :])[..., None] * S + jnp.einsum(
            'bhsk,bhsv->bhkv', k_ * jnp.exp(a_last - a_), v_)
        return S, o

    S0 = jnp.zeros((B_, A_HEADS, A_KDIM, A_VDIM), f32)
    _, o = lax.scan(step, S0, (qc, kc, vc, ac))
    o = o.transpose(1, 0, 3, 2, 4).reshape(B_, n_chunks * CHUNK, A_HEADS, A_VDIM)[:, PAD:]
    o = o * lax.rsqrt(jnp.mean(o * o, axis=-1, keepdims=True) + EPS)
    o = o * head_g.astype(f32).reshape(A_HEADS, A_VDIM)
    o = o.reshape(B_, T, A_WIDTH) * jax.nn.silu(og.astype(f32))
    return o.astype(dt)

def pool_mixer(p, w_group, scale):
    dt = p.dtype
    B_, T, _ = p.shape
    pf = p.astype(jnp.float32).reshape(B_, T, B_GROUPS, B_GDIM)
    cs = jnp.cumsum(pf, axis=1)
    pos = jnp.arange(1, T + 1, dtype=jnp.float32)
    outs = []
    for gi, w in enumerate(POOL_WINDOWS):
        c = cs[:, :, gi]
        lag = jnp.pad(c[:, :-w], ((0, 0), (w, 0), (0, 0)))
        mean = (c - lag) / jnp.minimum(pos, float(w))[None, :, None]
        outs.append(mean - pf[:, :, gi])
    d = jnp.stack(outs, axis=2)
    y = jnp.einsum('btgc,gcd->btgd', d, w_group.astype(jnp.float32)).reshape(B_, T, B_WIDTH)
    return (y * scale.astype(jnp.float32)).astype(dt)

def causal_dwconv(u, w, b):
    C = u.shape[-1]
    up = jnp.pad(u, ((0, 0), (CONV_W - 1, 0), (0, 0)))
    y = lax.conv_general_dilated(up, w[:, None, :].astype(u.dtype), window_strides=(1,), padding='VALID',
                                 dimension_numbers=('NWC', 'WIO', 'NWC'), feature_group_count=C)
    return y + b

def first_inputs(seed: int = 0) -> dict:
    key = jax.random.key(seed)
    ks = jax.random.split(key, 20)
    f32 = jnp.float32
    nrm = lambda k, shape, s: jax.random.normal(k, shape, f32) * s
    L = DEPTH
    return {
        "x": nrm(ks[0], (BATCH, SEQ, D_MODEL), 1.0),
        "meta_tokens": nrm(ks[1], (N_META, D_MODEL), 1.0),
        "lb_logits": nrm(ks[2], (DEPTH + 1, A_FDIM), 1.0),
        "norm1_g": 1.0 + nrm(ks[3], (L, D_MODEL), 0.05),
        "w_in": nrm(ks[4], (L, D_MODEL, IN_COLS), D_MODEL ** -0.5),
        "b_f": nrm(ks[5], (L, A_FDIM), 0.1),
        "head_norm_g": 1.0 + nrm(ks[6], (L, A_WIDTH), 0.05),
        "w_pool": nrm(ks[7], (L, B_GROUPS, B_GDIM, B_GDIM), B_GDIM ** -0.5),
        "pool_scale": 1.0 + nrm(ks[8], (L, B_WIDTH), 0.1),
        "w_branch_a": nrm(ks[9], (L, A_WIDTH, D_MODEL), A_WIDTH ** -0.5),
        "w_branch_b": nrm(ks[10], (L, B_WIDTH, D_MODEL), B_WIDTH ** -0.5),
        "w_out": nrm(ks[11], (L, D_MODEL, D_MODEL), D_MODEL ** -0.5),
        "norm2_g": 1.0 + nrm(ks[12], (L, D_MODEL), 0.05),
        "w_up": nrm(ks[13], (L, D_MODEL, 2 * D_FF), D_MODEL ** -0.5),
        "conv_w": nrm(ks[14], (L, CONV_W, D_FF), CONV_W ** -0.5),
        "conv_b": nrm(ks[15], (L, D_FF), 0.01),
        "w_down": nrm(ks[16], (L, D_FF, D_MODEL), D_FF ** -0.5),
        "final_norm_g": 1.0 + nrm(ks[17], (D_MODEL,), 0.05),
    }

def first_block(x, meta_tokens, lb_logits, norm1_g, w_in, b_f, head_norm_g, w_pool, pool_scale,
              w_branch_a, w_branch_b, w_out, norm2_g, w_up, conv_w, conv_b, w_down, final_norm_g):
    B_ = x.shape[0]
    meta = jnp.broadcast_to(meta_tokens.astype(x.dtype)[None], (B_, N_META, D_MODEL))
    h = jnp.concatenate([meta, x], axis=1)
    lb_all = jnp.cumsum(jax.nn.softmax(lb_logits.astype(jnp.float32), axis=0), axis=0)
    for l in range(DEPTH):
        z = rmsnorm(h, norm1_g[l])
        proj = z @ w_in[l]
        q, fl, iv, og, pin, ga, gb = jnp.split(proj, SPLITS, axis=-1)
        o_a = hgrn2_mixer(q, fl + b_f[l], iv, og, lb_all[l], head_norm_g[l])
        o_b = pool_mixer(pin, w_pool[l], pool_scale[l])
        mix = jax.nn.sigmoid(ga) * (o_a @ w_branch_a[l]) + jax.nn.sigmoid(gb) * (o_b @ w_branch_b[l])
        h = h + mix @ w_out[l]
        z = rmsnorm(h, norm2_g[l])
        u, v = jnp.split(z @ w_up[l], 2, axis=-1)
        u = causal_dwconv(u, conv_w[l], conv_b[l])
        h = h + (jax.nn.silu(u) * v) @ w_down[l]
    h = rmsnorm(h, final_norm_g)
    return h[:, N_META:]


DEPTH_2 = 2

HEAD_DIM = 64
N_Q_HEADS = 12
N_KV_HEADS_A = 4
N_MEM_HEADS = 4
N_MEM = 256
MIX_WIDTH = (N_Q_HEADS + N_MEM_HEADS) * HEAD_DIM
W_IN_A = (N_Q_HEADS + 2 * N_KV_HEADS_A + N_MEM_HEADS) * HEAD_DIM
W_IN_B = (3 * N_Q_HEADS + N_MEM_HEADS) * HEAD_DIM
WINDOW = 128
BLOCK = 128
GRID_W = 64
NA_ROWS_MAX = 8
NA_COLS = 16
D_FF_2 = -(-8 * D_MODEL // (3 * 256)) * 256
N_LAYERS_A = (DEPTH_2 + 1) // 2
N_LAYERS_B = DEPTH_2 // 2
NEG_INF = -1e30


def rmsnorm_2(x, g):
    x32 = x.astype(jnp.float32)
    y = x32 * lax.rsqrt(jnp.mean(x32 * x32, axis=-1, keepdims=True) + EPS)
    return (y * g.astype(jnp.float32)).astype(x.dtype)

def alibi_slopes(n_heads):
    return 2.0 ** (-8.0 * jnp.arange(1, n_heads + 1, dtype=jnp.float32) / n_heads)

def windowed_gqa(q, k, v, sink):
    B, S, H, D = q.shape
    Hk = k.shape[2]
    G = H // Hk
    nb = S // BLOCK
    qb = q.reshape(B, nb, BLOCK, Hk, G, D)
    pad = ((0, 0), (BLOCK, BLOCK), (0, 0), (0, 0))
    kp = jnp.pad(k, pad).reshape(B, nb + 2, BLOCK, Hk, D)
    vp = jnp.pad(v, pad).reshape(B, nb + 2, BLOCK, Hk, D)
    kband = jnp.concatenate([kp[:, :-2], kp[:, 1:-1], kp[:, 2:]], axis=2)
    vband = jnp.concatenate([vp[:, :-2], vp[:, 1:-1], vp[:, 2:]], axis=2)
    q_pos = jnp.arange(S).reshape(nb, BLOCK)
    k_pos = jnp.arange(nb)[:, None] * BLOCK - BLOCK + jnp.arange(3 * BLOCK)[None, :]
    dist = jnp.abs(q_pos[:, :, None] - k_pos[:, None, :])
    allowed = (dist <= WINDOW) & (k_pos[:, None, :] >= 0) & (k_pos[:, None, :] < S)
    slopes = alibi_slopes(H).reshape(1, Hk, G, 1, 1, 1)
    s = jnp.einsum('bnikgd,bnukd->bkgniu', qb, kband).astype(jnp.float32) * (D ** -0.5)
    s = s - slopes * dist.astype(jnp.float32)[None, None, None]
    s = jnp.where(allowed[None, None, None], s, NEG_INF)
    sink_col = jnp.broadcast_to(sink.astype(jnp.float32).reshape(1, Hk, G, 1, 1, 1), s.shape[:-1] + (1,))
    p = jax.nn.softmax(jnp.concatenate([s, sink_col], axis=-1), axis=-1)[..., :-1]
    o = jnp.einsum('bkgniu,bnukd->bnikgd', p.astype(v.dtype), vband)
    return o.reshape(B, S, H * D)

def neighbourhood_attn(q, k, v, rpb):
    B, S, H, D = q.shape
    rows = S // GRID_W
    kr = min(NA_ROWS_MAX, rows)
    qg = q.reshape(B, rows, GRID_W, H, D)
    kg = k.reshape(B, rows, GRID_W, H, D)
    vg = v.reshape(B, rows, GRID_W, H, D)
    r = jnp.arange(rows)
    row_start = jnp.clip(r - kr // 2, 0, rows - kr)
    row_idx = row_start[:, None] + jnp.arange(kr)[None, :]
    kband = kg[:, row_idx]
    vband = vg[:, row_idx]
    c = jnp.arange(GRID_W)
    col_start = jnp.clip(c - NA_COLS // 2, 0, GRID_W - NA_COLS)
    in_win = (c[None, :] >= col_start[:, None]) & (c[None, :] < col_start[:, None] + NA_COLS)
    dr_idx = row_idx - r[:, None] + NA_ROWS_MAX - 1
    dc_idx = jnp.clip(c[None, :] - c[:, None], -(NA_COLS - 1), NA_COLS - 1) + NA_COLS - 1
    bias = rpb.astype(jnp.float32)[:, dr_idx][:, :, :, dc_idx]
    bias = bias.transpose(0, 1, 3, 2, 4)
    s = jnp.einsum('brchd,brijhd->bhrcij', qg, kband).astype(jnp.float32) * (D ** -0.5)
    s = s + bias[None]
    s = jnp.where(in_win[None, None, None, :, None, :], s, NEG_INF)
    sh = s.shape
    p = jax.nn.softmax(s.reshape(sh[:-2] + (kr * GRID_W,)), axis=-1).reshape(sh)
    o = jnp.einsum('bhrcij,brijhd->brchd', p.astype(v.dtype), vband)
    return o.reshape(B, S, H * D)

def memory_attn(q, k, v):
    B, S, Hm, D = q.shape
    s = jnp.einsum('bshd,bmhd->bhsm', q, k).astype(jnp.float32) * (D ** -0.5)
    p = jax.nn.softmax(s, axis=-1)
    o = jnp.einsum('bhsm,bmhd->bshd', p.astype(v.dtype), v)
    return o.reshape(B, S, Hm * D)

def second_inputs(seed: int = 0) -> dict:
    key = jax.random.key(seed)
    ks = jax.random.split(key, 16)
    f32 = jnp.float32
    nrm = lambda k, shape, scale: jax.random.normal(k, shape, f32) * scale
    return {
        "x": nrm(ks[0], (BATCH, SEQ, D_MODEL), 1.0),
        "mem": nrm(ks[1], (BATCH, N_MEM, D_MODEL), 1.0),
        "norm_mix": 1.0 + nrm(ks[2], (DEPTH_2, D_MODEL), 0.02),
        "norm_ffn": 1.0 + nrm(ks[3], (DEPTH_2, D_MODEL), 0.02),
        "norm_mem": 1.0 + nrm(ks[4], (D_MODEL,), 0.02),
        "norm_final": 1.0 + nrm(ks[5], (D_MODEL,), 0.02),
        "w_in_a": nrm(ks[6], (N_LAYERS_A, D_MODEL, W_IN_A), D_MODEL ** -0.5),
        "sink_a": nrm(ks[7], (N_LAYERS_A, N_Q_HEADS), 0.5),
        "w_in_b": nrm(ks[8], (N_LAYERS_B, D_MODEL, W_IN_B), D_MODEL ** -0.5),
        "rpb_b": nrm(ks[9], (N_LAYERS_B, N_Q_HEADS, 2 * NA_ROWS_MAX - 1, 2 * NA_COLS - 1), 0.3),
        "w_mem_kv": nrm(ks[10], (DEPTH_2, D_MODEL, 2 * N_MEM_HEADS * HEAD_DIM), D_MODEL ** -0.5),
        "w_out": nrm(ks[11], (DEPTH_2, MIX_WIDTH, D_MODEL), MIX_WIDTH ** -0.5),
        "w_gate_up": nrm(ks[12], (DEPTH_2, D_MODEL, 2 * D_FF_2), D_MODEL ** -0.5),
        "w_down": nrm(ks[13], (DEPTH_2, D_FF_2, D_MODEL), D_FF_2 ** -0.5),
    }

def second_block(x, mem, norm_mix, norm_ffn, norm_mem, norm_final, w_in_a, sink_a, w_in_b, rpb_b,
              w_mem_kv, w_out, w_gate_up, w_down):
    B, S, _ = x.shape
    qw = N_Q_HEADS * HEAD_DIM
    kvw = N_KV_HEADS_A * HEAD_DIM
    mw = N_MEM_HEADS * HEAD_DIM
    mem_n = rmsnorm_2(mem, norm_mem)
    for i in range(DEPTH_2):
        li = i // 2
        h = rmsnorm_2(x, norm_mix[i])
        mkv = mem_n @ w_mem_kv[i]
        mk = mkv[..., :mw].reshape(B, N_MEM, N_MEM_HEADS, HEAD_DIM)
        mv = mkv[..., mw:].reshape(B, N_MEM, N_MEM_HEADS, HEAD_DIM)
        if i % 2 == 0:
            proj = h @ w_in_a[li]
            q, k, v, qm = jnp.split(proj, [qw, qw + kvw, qw + 2 * kvw], axis=-1)
            y_tok = windowed_gqa(q.reshape(B, S, N_Q_HEADS, HEAD_DIM),
                                 k.reshape(B, S, N_KV_HEADS_A, HEAD_DIM),
                                 v.reshape(B, S, N_KV_HEADS_A, HEAD_DIM), sink_a[li])
        else:
            proj = h @ w_in_b[li]
            q, k, v, qm = jnp.split(proj, [qw, 2 * qw, 3 * qw], axis=-1)
            y_tok = neighbourhood_attn(q.reshape(B, S, N_Q_HEADS, HEAD_DIM),
                                       k.reshape(B, S, N_Q_HEADS, HEAD_DIM),
                                       v.reshape(B, S, N_Q_HEADS, HEAD_DIM), rpb_b[li])
        y_mem = memory_attn(qm.reshape(B, S, N_MEM_HEADS, HEAD_DIM), mk, mv)
        x = x + jnp.concatenate([y_tok, y_mem], axis=-1) @ w_out[i]
        h = rmsnorm_2(x, norm_ffn[i])
        gu = h @ w_gate_up[i]
        x = x + (jax.nn.silu(gu[..., :D_FF_2]) * gu[..., D_FF_2:]) @ w_down[i]
    return rmsnorm_2(x, norm_final)


def setup_inputs(seed=0):
    out = dict(first_inputs(seed))
    for name, value in second_inputs(seed + 1).items():
        if name != "x":
            out[name + "_2"] = value
    return out


def reference(
    x, meta_tokens, lb_logits, norm1_g, w_in, b_f, head_norm_g, w_pool, pool_scale, w_branch_a,
    w_branch_b, w_out, norm2_g, w_up, conv_w, conv_b, w_down, final_norm_g, mem_2, norm_mix_2,
    norm_ffn_2, norm_mem_2, norm_final_2, w_in_a_2, sink_a_2, w_in_b_2, rpb_b_2, w_mem_kv_2,
    w_out_2, w_gate_up_2, w_down_2,
):
    x = first_block(
        x, meta_tokens, lb_logits, norm1_g, w_in, b_f, head_norm_g, w_pool, pool_scale,
        w_branch_a, w_branch_b, w_out, norm2_g, w_up, conv_w, conv_b, w_down, final_norm_g,
    )
    return second_block(
        x, mem_2, norm_mix_2, norm_ffn_2, norm_mem_2, norm_final_2, w_in_a_2, sink_a_2,
        w_in_b_2, rpb_b_2, w_mem_kv_2, w_out_2, w_gate_up_2, w_down_2,
    )


_drawn_inputs = setup_inputs


def setup_inputs(seed=0):
    import zlib

    import numpy as np

    out = dict(_drawn_inputs(seed))
    spreads = {}
    factors = {'b_f': 8.0,
     'head_norm_g': 2.733,
     'conv_b': 8.0,
     'norm_mix_2': 6.479,
     'norm_ffn_2': 2.726,
     'norm_mem_2': 8.0,
     'norm_final_2': 2.875,
     'sink_a_2': 4.831}
    for name, (base, spread) in spreads.items():
        noise = np.random.default_rng([zlib.crc32(name.encode()), seed]).standard_normal(out[name].shape)
        drawn = base * np.exp(spread * noise) if base else spread * noise
        out[name] = __import__('jax').numpy.asarray(drawn.astype(out[name].dtype))
    for name, factor in factors.items():
        out[name] = (out[name] * factor).astype(out[name].dtype)
    return out
```

```python
from contextlib import ExitStack

import concourse.bass as bass
from concourse import mybir
from concourse.alu_op_type import AluOpType as ALU

ACT = mybir.ActivationFunctionType
AX = mybir.AxisListType
F32 = mybir.dt.float32
F32R = mybir.dt.float32r
U8 = mybir.dt.uint8

P = 128
D = 1024
KD = D // P
SEQ = 512
META = 16
T1 = META + SEQ
HALF = T1 // 2
EPS = 1e-6

HEADS = D // P
VD = 64
WIDTH = D // 2
LEVELS = 7
CHUNKS = SEQ // P
PADC = 16
WINDOWS = (2, 4, 8, 16)
DFF = 2816
FT = DFF // P
FH = FT // 2

HD = 64
QH = 12
KVA = 4
MH = 4
NMEM = 256
GRID_R, GRID_C = 8, 64
BC = GRID_C // 4
NEG = -1e30

SLOT = FH * P
UNIT = KD * P


def columns():
    at, n = {}, 0
    for name, width in (("lb0", 8), ("lb1", 8), ("norm1", 8), ("b_f", 8), ("head_g", 4), ("pool_scale", 4),
                        ("norm2", 8), ("conv_w", 3 * FT), ("conv_b", FT), ("final_g", 8), ("mix_g", 16),
                        ("ffn_g", 16), ("mem_g", 8), ("out_g", 8), ("sink", QH)):
        at[name] = n
        n += width
    at["all"] = n
    return at


def constant_columns():
    at, n = {}, 0
    for name, width in (("ident", P), ("ones", P), ("pair_ones", P), ("restart", T1), ("first_counts", 64),
                        ("eps", 1), ("slopes", QH)):
        at[name] = n
        n += width
    at["all"] = n
    return at


AH = QH + MH


def build(nc, t):
    pc, cc = columns(), constant_columns()
    ctx = ExitStack()
    with ctx:
        def sem(name):
            return ctx.enter_context(nc.semaphore(name))

        fixed = [(nc.sbuf_usable_end - nc.sbuf_bytes_remaining + 31) // 32 * 32]

        def sb(at, name, shape, dt=F32):
            size = 1 if dt == U8 else 4
            for n in shape[1:]:
                size *= n
            x = nc.alloc_sbuf_tensor_at(name, shape, dt, offset=at[0])
            at[0] += (size + 31) // 32 * 32
            return x

        par = sb(fixed, "par", [P, pc["all"]])
        con = sb(fixed, "con", [P, cc["all"]])
        masks = sb(fixed, "masks", [P, LEVELS, P], U8)
        lbc = sb(fixed, "lbc", [P, 4, KD])
        stat = sb(fixed, "stat", [P, 6, 6])
        raw = [sb(fixed, f"raw{i}", [P, SLOT]) for i in range(2)]
        w_hi = [sb(fixed, f"w_hi{i}", [P, SLOT], F32R) for i in range(2)]
        w_lo = [sb(fixed, f"w_lo{i}", [P, SLOT], F32R) for i in range(2)]
        H = sb(fixed, "H", [P, KD, T1])
        z_hi = sb(fixed, "z_hi", [P, KD, T1], F32R)
        z_lo = sb(fixed, "z_lo", [P, KD, T1], F32R)
        region = fixed[0]

        at = [region]
        x_rows = sb(at, "x_rows", [P, CHUNKS, D])
        meta_rows = sb(at, "meta_rows", [META, D])
        mask_rows = sb(at, "mask_rows", [P, LEVELS * P])
        at = [region]
        qf = sb(at, "qf", [P, 2 * HEADS, T1])
        gates = sb(at, "gates", [P, 2 * KD, T1])
        og = sb(at, "og", [P, 4, T1])
        pin = sb(at, "pin", [P, 4, PADC + T1])
        V = sb(at, "V", [P, CHUNKS, WIDTH])
        V0 = sb(at, "V0", [META, WIDTH])
        scratch = at[0]
        at = [scratch]
        sq = [sb(at, f"sq{i}", [P, T1]) for i in range(2)]
        acc = sb(at, "acc", [P, T1])
        rstd = sb(at, "rstd", [P, T1])
        sig = sb(at, "sig", [P, T1])
        z_now = [sq[0], sq[1], rstd, sig]
        pool_a = sb(at, "pool_a", [P, PADC + T1])
        pool_b = sb(at, "pool_b", [P, PADC + T1])
        pool_w = sb(at, "pool_w", [P, 4, P])
        at = [scratch + 5 * 4 * T1]
        zt = [sb(at, f"zt{i}", [P, T1]) for i in range(2)]
        ta = sb(at, "ta", [P, T1])
        tb = sb(at, "tb", [P, T1])
        at = [region]
        mix_hi = sb(at, "mix_hi", [P, KD, T1], F32R)
        mix_lo = sb(at, "mix_lo", [P, KD, T1], F32R)
        at = [region]
        g_hi = sb(at, "g_hi", [P, FH, T1], F32R)
        g_lo = sb(at, "g_lo", [P, FH, T1], F32R)
        ub = sb(at, "ub", [P, 2 + T1])
        cv = [sb(at, f"cv{i}", [P, T1]) for i in range(3)]
        si = sb(at, "si", [P, T1])
        gv = [sb(at, f"gv{i}", [P, T1]) for i in range(2)]
        mem_rows = sb(at, "mem_rows", [P, 2, D])
        mem_square = sb(at, "mem_square", [P, D])
        mem_stat = sb(at, "mem_stat", [P, 3, 2])
        mz_hi = sb(at, "mz_hi", [P, KD, NMEM], F32R)
        mz_lo = sb(at, "mz_lo", [P, KD, NMEM], F32R)
        assert at[0] <= scratch
        at = [scratch + 5 * 4 * T1]
        mk = sb(at, "mk", [P, 2 * MH, NMEM])
        mv = sb(at, "mv", [P, 2 * 2, NMEM])
        att_con = sb(at, "att_con", [P, 3 * P + 3 * 48])
        row_max = [sb(at, f"row_max{i}", [P, 4]) for i in range(3)]
        neg_max = [sb(at, f"neg_max{i}", [P, 4]) for i in range(3)]
        row_sum = [sb(at, f"row_sum{i}", [P, 4]) for i in range(3)]
        sink_exp = [sb(at, f"sink_exp{i}", [P, 4]) for i in range(3)]
        rsum = [sb(at, f"rsum{i}", [P, 4]) for i in range(3)]
        rpb_last = sb(at, "rpb_raw2", [P, GRID_R, 48])
        at = [region]
        q_heads = sb(at, "q_heads", [P, QH + MH, SEQ])
        k_heads = sb(at, "k_heads", [P, QH, SEQ])
        v_tok = sb(at, "v_tok", [P, 4, QH * HD])
        y_tok = sb(at, "y_tok", [P, 4, D])
        q_now = [sb(at, "q_now0", [P, SEQ])]
        bias = [sb(at, "bias0", [P, GRID_R * (48 + 32 + 32)])]
        rpb_raw = [sb(at, f"rpb_raw{i}", [P, GRID_R, 48]) for i in range(2)] + [rpb_last]
        assert at[0] <= scratch
        at = [fixed[0] - 2 * 4 * KD * T1]
        ls = [sb(at, f"ls{i}", [P, 4, 3 * P]) for i in range(3)]
        bias += [sb(at, f"bias{i}", [P, GRID_R * (48 + 32 + 32)]) for i in range(1, 3)]
        q_now += [sb(at, f"q_now{i}", [P, SEQ]) for i in range(1, 3)]
        pts = [sb(at, f"pts{i}", [P, 3 * P]) for i in range(2)]
        assert at[0] <= fixed[0]
        at = [region]
        out_rows = sb(at, "out_rows", [P, CHUNKS, D])
        at = [scratch]
        lf = sb(at, "lf", [P, T1])
        kk = sb(at, "kk", [P, T1])
        A = sb(at, "A", [P, T1])
        qe = sb(at, "qe", [P, SEQ])
        kd = sb(at, "kd", [P, META + 3 * P])
        X = [sb(at, f"X{i}", [P, T1]) for i in range(3)]
        kdt = sb(at, "kdt", [P, 4, P])
        sc = sb(at, "sc", [P, SEQ])
        sc0 = sb(at, "sc0", [META, META])
        st = sb(at, "st", [P, 4, VD])
        dec = sb(at, "dec", [P, 4])
        vh = sb(at, "vh", [P, CHUNKS, VD])
        vh0 = sb(at, "vh0", [META, VD])
        spare = sb(at, "spare", [P, 1])

        ps = [ctx.enter_context(nc.psum_tensor(f"ps{i}", [P, 2, 512], F32)) for i in range(4)]

        def out528(i):
            return ps[i][:, :, 0:HALF]

        def two(x):
            return x.rearrange("p (b n) -> p b n", b=2)

        ident = con[:, cc["ident"]:cc["ident"] + P]
        ones = con[:, cc["ones"]:cc["ones"] + P]
        pair_ones = con[:, cc["pair_ones"]:cc["pair_ones"] + P]
        restart = con[:, cc["restart"]:cc["restart"] + T1]
        eps = con[:, cc["eps"]:cc["eps"] + 1]

        def vec(name, i=0):
            return par[:, bass.ds(pc[name] + i, 1)]

        def halves(x, l):
            h = 2 ** l
            lo = 0 if l <= 3 else META
            v = x[:, lo:T1].rearrange("p (n s h) -> p n s h", s=2, h=h)
            return v[:, :, 0, :], v[:, :, 1, :], v[:, :, 0, h - 1:h].to_broadcast([P, (T1 - lo) // (2 * h), h])

        def chunked(x, n):
            return x.rearrange("p (c t) -> p c t", c=n)

        x_loaded, const_loaded = sem("x_loaded"), sem("const_loaded")
        w_loaded = [sem("w_loaded0"), sem("w_loaded1")]
        hi_done = sem("hi_done")
        lo_done = sem("lo_done")
        used = sem("used")
        ps_free = [sem(f"ps_free{i}") for i in range(2)]
        x_turned, x_copied, meta_turned = sem("x_turned"), sem("x_copied"), sem("meta_turned")
        lb_step = sem("lb_step")

        def stage(prefix, *names):
            return {n: sem(f"{prefix}_{n}") for n in names}

        qs = stage("qf", "sig", "q")
        ops = stage("og", "sig", "pin")
        vs = stage("v", "act", "dve")
        pools = stage("pool", "step", "ready", "sum", "out")
        mx = stage("mx", "ln", "scan", "sub", "exp", "mul_r", "mul_l", "k", "kd_sub", "kd_exp", "kd", "qe_exp",
                   "qe", "turn", "score_read", "kdt", "meta", "states", "vh", "o", "sc", "o_read", "chain")
        oas = stage("oa", "sq", "inv", "scaled", "z", "hi", "lo", "pin_lo", "sum")
        brs = stage("br", "sig", "a", "mixed", "hi", "lo", "taken")
        pe_z = sem("z_again")


        class Round:

            def __init__(self, sems, base):
                self.sems, self.base = sems, base

            def __getitem__(self, name):
                return self.sems[name]

            def at(self, name, count):
                return self.sems[name], count + self.base[name]

        def rounds(prefix, *counts, start={}):
            sems = stage(prefix, *counts[0])
            base, out = {n: start.get(n, 0) for n in sems}, []
            for c in counts:
                out.append(Round(sems, dict(base)))
                for n in sems:
                    base[n] += c[n]
            return out

        norm_counts = {"sq": KD, "acc": KD + 1, "sum": 1, "root": 1, "inv": 6, "wide": 1, "z": KD, "hi": KD, "even": KD // 2,
                       "odd": KD // 2}
        plain = {**norm_counts, "hi": 0, "even": 0, "odd": 0}
        n1, n2, fin, norm_a0, norm_f0, norm_a1, norm_f1, norm_o = rounds(
            "norm", norm_counts, norm_counts, plain, *[norm_counts] * 4, plain)
        norm_a, norm_f = (norm_a0, norm_a1), (norm_f0, norm_f1)
        ffn_counts = {"conv": 6 * FH, "sig": 2 * FH, "si": 2 * FH, "hi": 2 * FH, "lo": 2 * FH}
        f1, *ffn2 = rounds("ffn", ffn_counts, {**ffn_counts, "conv": 0, "si": 0}, {**ffn_counts, "conv": 0, "si": 0})
        padded, masks_ready = sem("padded"), sem("masks_ready")
        mem_loaded, mem_step, mem_turned = sem("mem_loaded"), sem("mem_step"), sem("mem_turned")
        mem_hi, mem_lo = sem("mem_hi"), sem("mem_lo")
        att_counts = {"q": QH, "s": 4 * AH, "ls": 4 * AH, "max": 4 * AH, "neg": AH, "exp": 4 * AH, "t": 4 * AH,
                      "pa": 2 * AH, "pd": 2 * AH, "y": 4 * AH, "sum": QH, "inv": AH, "out": AH, "bias": 0,
                      "turned": KD, "hi": KD}
        ATT_START = {"s": 12, "ls": 12, "t": 12, "pa": 1, "pd": 1, "y": 2, "out": 3, "bias": 3}
        atts = rounds("att", att_counts, {**att_counts, "sum": 0, "bias": QH}, start=ATT_START)
        rpb_loaded = [sem(f"rpb_loaded{i}") for i in range(3)]
        att_loaded, out_turned, out_copied, out_sent = (sem("att_loaded"), sem("out_turned"), sem("out_copied"),
                                                        sem("out_sent"))

        STREAM = [("qf", 16, UNIT), ("v", 4, UNIT), ("ogpin", 8, UNIT), ("gates", 16, UNIT), ("branch", 8, UNIT),
                  ("out", 8, UNIT)]
        for half in "ab":
            STREAM += [(f"up_{half}", 2 * FH, UNIT), (f"down_{half}", 8, SLOT)]
        STREAM += [("mem", 8, UNIT)]
        for l in range(2):
            STREAM += [(f"qk{l}", (10, 14)[l], UNIT), (f"v{l}", (2, 8)[l], (UNIT, 2 * 384)[l]),
                       (f"out{l}", 8, UNIT)]
            for half in "ab":
                STREAM += [(f"up{l}_{half}", 2 * FH, UNIT), (f"down{l}_{half}", 8, SLOT)]
        UNITS, WIDTHS = {}, []
        for name, count, width in STREAM:
            UNITS[name] = len(WIDTHS)
            WIDTHS += [width] * count
        FREED, so_far = {}, (0, 0)
        for name, a, b in ([("qf", 8, 8), ("v", 1, 0), ("ogpin", 4, 0), ("pool", 2, 2), ("gates", 8, 8), ("oa", 2, 2),
                            ("out", 4, 4)] + [(f"{w}_{h}", c, c) for h in "ab" for w, c in (("up", FH), ("down", 4))]
                           + [("mem", 4, 2)]
                           + [x for l in range(2) for x in
                              [(f"qk{l}", (5, 7)[l], (5, 7)[l]), (f"v{l}", (1, 2)[l], (1, 2)[l]),
                               (f"turn{l}", 4, 4), (f"out{l}", 4, 4)]
                              + [(f"{w}{l}_{h}", c, c) for h in "ab" for w, c in (("up", FH), ("down", 4))]]):
            FREED[name] = so_far
            so_far = (so_far[0] + a, so_far[1] + b)

        POOLED = tuple(1 + x for x in FREED["gates"])

        def psv(tokens, i):
            return ps[i][:, :, 0:HALF] if tokens == T1 else ps[i][:, 0, 0:tokens]

        def shaped(tokens, x):
            return two(x[:, 0:T1]) if tokens == T1 else x[:, 0:tokens]

        def natural(x):
            return x.rearrange("p (r b c) -> p b r c", r=GRID_R, b=4)

        def blocked(x):
            return x.rearrange("p (b r c) -> p b r c", r=GRID_R, b=4)

        def banks(i):
            return (ps[1][:, 1, :], ps[2][:, 0, :], ps[2][:, 1, :])[i % 3]

        def turned_memory(k):
            return ps[2 + k % 4 // 2][:, k % 2, k // 4 * NMEM:(k // 4 + 1) * NMEM]

        def y_bank(r):
            return (ps[0][:, 0, :], ps[0][:, 1, :], ps[1][:, 0, :])[r][:, 0:4 * HD]

        def span(memory, b):
            return (0, NMEM) if memory else ((P, 2 * P), (0, 3 * P), (0, 3 * P), (0, 2 * P))[b]

        def key_block(memory, b, j):
            return j if memory else max(b - 1, 0) + j

        def head_steps(eng, step):
            for h in range(3):
                step(h, h, h, 0)
            with eng.Fori(0, QH // 3 - 1) as g:
                for r in range(3):
                    step(3 * g + (3 + r), r, 3, g + 1)
            for h in range(QH, AH + 3):
                step(h, h % 3, h, h // 3)

        def pieces(tokens):
            return (6, T1 // 6) if tokens == T1 else (4, P)

        def h_tile(tokens, k):
            return H[:, k, :] if tokens == T1 else H[:, k, META:]

        def peeled(eng, count, body, this, after):
            if this == after:
                with eng.Fori(0, count) as i:
                    body(i, this)
            else:
                with eng.Fori(0, count - 1) as i:
                    body(i, this)
                body(count - 1, after)

        def after(name, count):
            n = UNITS[name] + count
            return WIDTHS[n] if n < len(WIDTHS) else None

        block = ctx.enter_context(nc.Block())

        def cols(w, c0, kt=KD, k0=0, width=P):
            return w[k0 * P:(k0 + kt) * P, bass.ds(c0, width)].rearrange("(k p) c -> p k c", p=P)

        def turn_of(level):
            return level + 1 if level <= 3 else level + 3

        @block.sync
        def _(sp):
            for c in range(CHUNKS):
                sp.dma_start(x_rows[:, c, :], t["x"][0, c * P:(c + 1) * P, :]).then_inc(x_loaded, 16)
            sp.dma_start(meta_rows[:, :], t["meta_tokens"]).then_inc(x_loaded, 16)
            sp.dma_start(con[:, :], t["constants"]).then_inc(const_loaded, 16)
            sp.dma_start(par[:, :], t["parameters"]).then_inc(const_loaded, 16)
            sp.dma_start(mask_rows[:, :], t["level_masks"]).then_inc(const_loaded, 16)
            sp.dma_start(pool_w[:, :, :], t["w_pool"][0].rearrange("g c d -> c g d")).then_inc(const_loaded, 16)

            def load(n, s, src, kt=KD, width=P):
                sp.wait_ge(lo_done, n + 1)
                sp.dma_start(raw[s][:, 0:kt * width].rearrange("p (k c) -> p k c", k=kt), src)\
                  .then_inc(w_loaded[s], 16)

            w_in = t["w_in"][0]
            with sp.Fori(0, HEADS) as h:
                n = UNITS["qf"] + 2 * h
                load(n, 0, cols(w_in, h * P))
                load(n + 1, 1, cols(w_in, h * P + D))
            for i in range(4):
                load(UNITS["v"] + i, i % 2, cols(w_in, 2 * D, 2, 2 * i, 512), 2, 512)
            with sp.Fori(0, 4) as j:
                n = UNITS["ogpin"] + 2 * j
                load(n, 0, cols(w_in, j * P + 2 * D + WIDTH))
                load(n + 1, 1, cols(w_in, j * P + 2 * D + 2 * WIDTH))
            with sp.Fori(0, HEADS) as h:
                n = UNITS["gates"] + 2 * h
                load(n, 0, cols(w_in, h * P + 2 * D + 3 * WIDTH))
                load(n + 1, 1, cols(w_in, h * P + 3 * D + 3 * WIDTH))
            w_branch = t["w_branch"]
            for name, w in (("branch", w_branch), ("out", t["w_out"][0])):
                with sp.Fori(0, 4) as i:
                    n = UNITS[name] + 2 * i
                    load(n, 0, cols(w, i * (2 * P)))
                    load(n + 1, 1, cols(w, i * (2 * P) + P))

            def ffn(tag, w_up, w_down):
                for b, half in enumerate("ab"):
                    if tag == "" and b == 1:
                        sp.dma_start(mem_rows[:, :, :], t["mem_2"][0].rearrange("(c p) d -> p c d", p=P))\
                          .then_inc(mem_loaded, 16)
                        sp.dma_start(att_con[:, :], t["attention_constants"]).then_inc(att_loaded, 16)
                    with sp.Fori(0, FH) as j:
                        n = UNITS[f"up{tag}_{half}"] + 2 * j
                        load(n, 0, cols(w_up, j * P + b * FH * P))
                        load(n + 1, 1, cols(w_up, j * P + (DFF + b * FH * P)))
                    with sp.Fori(0, 4) as i:
                        n = UNITS[f"down{tag}_{half}"] + 2 * i
                        load(n, 0, cols(w_down, i * (2 * P), FH, b * FH), FH)
                        load(n + 1, 1, cols(w_down, i * (2 * P) + P, FH, b * FH), FH)
            ffn("", t["w_up"][0], t["w_down"][0])

            n = UNITS["mem"]
            for l in range(2):
                w = t["w_mem_kv_2"][l]
                for s in range(2):
                    load(n + 4 * l + s, s, cols(w, s * P))
                for s in range(2):
                    load(n + 4 * l + 2 + s, s, cols(w, MH * HD, 4, 4 * s, MH * HD), 4, MH * HD)

            def bias_load(h, r):
                sp.wait_ge(*atts[1].at("bias", h - 2))
                for rq in range(GRID_R):
                    rows = slice(GRID_R - 1 - rq, 2 * GRID_R - 1 - rq)
                    sp.dma_start(rpb_raw[r][rq * BC:(rq + 1) * BC, :, :],
                                 t["rpb"][bass.ds(h, 1), :, rows, :].rearrange("o c r x -> (o c) r x"))\
                      .then_inc(rpb_loaded[r], 16)

            for l in range(2):
                if l == 1:
                    for r in range(3):
                        bias_load(r, r)
                w = (t["w_in_a_2"], t["w_in_b_2"])[l][0]
                qkw = (QH + (KVA, QH)[l]) * HD
                vw = (KVA, QH)[l] * HD
                n = UNITS[f"qk{l}"]
                with sp.Fori(0, qkw // (2 * P)) as i:
                    load(n + 2 * i, 0, cols(w, i * (2 * P)))
                    load(n + 2 * i + 1, 1, cols(w, i * (2 * P) + P))
                for s in range(2):
                    load(n + qkw // P + s, s, cols(w, qkw + vw + s * P))
                n, kt, width = UNITS[f"v{l}"], (4, 2)[l], (KVA * HD, 384)[l]
                for i in range((2, 8)[l]):
                    load(n + i, i % 2, cols(w, qkw + width * (i * kt // KD), kt, i * kt % KD, width), kt, width)
                w_out, n = t["w_out_2"][l], UNITS[f"out{l}"]
                load(n, 0, cols(w_out, 0))
                load(n + 1, 1, cols(w_out, P))
                if l == 1:
                    with sp.Fori(0, QH // 3 - 1) as g:
                        for r in range(3):
                            bias_load(3 * g + (3 + r), r)
                with sp.Fori(0, 3) as i:
                    load(n + 2 * i + 2, 0, cols(w_out, i * (2 * P) + 2 * P))
                    load(n + 2 * i + 3, 1, cols(w_out, i * (2 * P) + 3 * P))
                ffn(str(l), t["w_gate_up_2"][l], t["w_down_2"][l])

            for c in range(CHUNKS):
                sp.wait_ge(out_copied, c + 1)
                sp.dma_start(t["out"][0, c * P:(c + 1) * P, :], out_rows[:, c, :]).then_inc(out_sent, 16)
            sp.wait_ge(out_sent, 16 * CHUNKS)

        @block.gpsimd
        def _(pool):
            for s, count in ((lo_done, 2), (used, 2), (ps_free[0], 1), (ps_free[1], 1), (mx["scan"], 1),
                             (mx["turn"], 1), (mx["score_read"], 2), (mx["o"], 1), (mx["o_read"], 1), (ops["pin"], 1),
                             (brs["mixed"], 2), (brs["lo"], 2), (f1["lo"], 1)):
                pool.nop().then_inc(s, count)
            for name, count in ATT_START.items():
                pool.nop().then_inc(atts[0][name], count)

            def norm_odd(s, tokens, order=None):
                for k in range(1, KD, 2):
                    pool.wait_ge(*s.at("hi", k + 1))
                    lo, z, hi = z_lo[:, k, 0:tokens], z_now[k % 4][:, 0:tokens], z_hi[:, k, 0:tokens].bitcast(F32)
                    if order:
                        lo, z, hi = blocked(lo), natural(z), blocked(hi)
                    pool.tensor_tensor(lo, z, hi, ALU.subtract).then_inc(s["odd"], 1)
            norm_odd(n1, T1)

            pool.memset(pin[:, :, 0:PADC], 0.0).then_inc(pools["step"], 1)
            pool.memset(pool_a[:, :], 0.0).then_inc(pools["step"], 1)
            pool.memset(pool_b[:, :], 0.0).then_inc(pools["step"], 1)
            steps = 3
            for g, w in enumerate(WINDOWS):
                pool.wait_ge(ops["pin"], g + 2)
                src, lag = pin[:, g, :], 1
                for r in range(g + 1):
                    dst = (pool_a, pool_b)[r % 2]
                    pool.wait_ge(pools["step"], steps)
                    pool.tensor_tensor(dst[:, lag:], src[:, lag:], src[:, 0:PADC + T1 - lag], ALU.add)\
                        .then_inc(pools["step"], 1)
                    steps += 1
                    src, lag = dst[:, :], 2 * lag
                pool.wait_ge(pools["step"], steps)
                c0 = cc["first_counts"] + 16 * g
                pool.tensor_tensor(src[:, PADC:PADC + 16], src[:, PADC:PADC + 16], con[:, c0:c0 + 16], ALU.mult)\
                    .then_inc(pools["step"], 1)
                pool.tensor_scalar(src[:, PADC + 16:], src[:, PADC + 16:], 1.0 / w, 1.0, ALU.mult, ALU.mult)\
                    .then_inc(pools["step"], 1)
                steps += 2
                pool.wait_ge(pools["step"], steps)
                pool.tensor_tensor(pin[:, g, PADC:], src[:, PADC:], pin[:, g, PADC:], ALU.subtract)\
                    .then_inc(pools["ready"], 1)
                pool.wait_ge(pools["ready"], g + 1)

            def head(h):
                pool.wait_ge(mx["o"], h + 1)
                pool.tensor_copy(vh[:, :, :], V[:, :, bass.ds(h * VD, VD)]).then_inc(mx["vh"], 1)
                pool.tensor_copy(vh0[:, :], V0[:, bass.ds(h * VD, VD)]).then_inc(mx["vh"], 1)
                pool.wait_ge(mx["k"], h + 1)
                for l in range(LEVELS):
                    left, _, _ = halves(X[l % 3][:, :], l)
                    kleft, _, _ = halves(kk[:, :], l)
                    pool.wait_ge(mx["exp"], h * LEVELS + l + 1)
                    pool.tensor_tensor(left, left, kleft, ALU.mult).then_inc(mx["mul_l"], 1)
                    if l == 1:
                        pool.wait_ge(mx["kd_exp"], h + 1)
                        pool.tensor_tensor(kd[:, :], kd[:, :], kk[:, 0:META + 3 * P], ALU.mult)\
                            .then_inc(mx["kd"], 1)

            pool.wait_ge(ps_free[0], POOLED[0])
            pool.wait_ge(ps_free[1], POOLED[1])
            pool.wait_ge(vs["act"], 1)
            pool.wait_ge(vs["dve"], 1)
            with pool.Fori(0, HEADS // 2) as p:
                for j in range(2):
                    head(2 * p + j)

            def low(n, src, hi, lo, done):
                pool.tensor_tensor(lo, src, hi.bitcast(F32), ALU.subtract).then_inc(done, 1)

            for p in range(4):
                pool.wait_ge(oas["hi"], p + 5)
                low(0, zt[p % 2][:, :], z_hi[:, p, :], z_lo[:, p, :], oas["lo"])
            with pool.Fori(0, 4) as i:
                for s in range(2):
                    m = 2 * i + s
                    pool.wait_ge(brs["hi"], m + 1)
                    low(0, zt[s][:, :], mix_hi[:, m, :], mix_lo[:, m, :], brs["lo"])
            pool.memset(ub[:, 0:2], 0.0).then_inc(padded, 1)
            norm_odd(n2, T1)

            def ffn_low(s, tokens):
                for b in range(2):
                    def body(j, par_):
                        pool.wait_ge(*s.at("hi", b * FH + j + 1))
                        low(0, gv[par_][:, 0:tokens], g_hi[:, j, 0:tokens], g_lo[:, j, 0:tokens], s["lo"])
                    with pool.Fori(0, FH) as j:
                        body(j, 0)
            ffn_low(f1, T1)

            for l in range(2):
                norm_odd(norm_a[l], SEQ, l)
                s = atts[l]
                pool.wait_ge(att_loaded, 16)

                def queries(h, r):
                    pool.wait_ge(*s.at("s", 4 * h - 8))
                    pool.tensor_copy(q_now[r][0:HD, :].rearrange("p (o n) -> p o n", o=1),
                                     q_heads[0:HD, bass.ds(h, 1), :]).then_inc(s["q"], 1)

                def biases(h, g, r):
                    if l == 1:
                        pool.wait_ge(rpb_loaded[r], 128 * g + 128)
                        pool.wait_ge(*s.at("ls", 4 * h - 8))
                        at_ = 0
                        for v, (first, n) in enumerate(((1, 2), (0, 3), (0, 2))):
                            x0 = first * BC
                            mask = att_con[:, 3 * P + 48 * v + x0:3 * P + 48 * v + x0 + n * BC]
                            x = pool.tensor_tensor(
                                bias[r][:, at_:at_ + n * P].rearrange("p (n r c) -> p n r c", n=n, r=GRID_R),
                                rpb_raw[r][:, :, x0:x0 + n * BC].rearrange("p r (n c) -> p n r c", n=n),
                                mask.rearrange("p (n o c) -> p n o c", n=n, o=1)
                                    .to_broadcast([P, n, GRID_R, BC]), ALU.add)
                            at_ += n * P
                        x.then_inc(s["bias"], 1)
                biases(0, 0, 0)
                pool.wait_ge(used, UNITS[f"v{l}"] + 2)
                pool.wait_ge(ps_free[0], FREED[f"v{l}"][0] + 1)
                pool.wait_ge(ps_free[1], FREED[f"v{l}"][1] + 1)
                queries(0, 0)
                pool.wait_ge(used, UNITS[f"out{l}"] + 2)
                for h in (1, 2):
                    queries(h, h)
                    biases(h, 0, h)
                with pool.Fori(0, QH // 3 - 1) as g:
                    for r in range(3):
                        queries(3 * g + (3 + r), r)
                        biases(3 * g + (3 + r), g + 1, r)
                norm_odd(norm_f[l], SEQ)
                ffn_low(ffn2[l], SEQ)

        @block.scalar
        def _(act):
            def split_hi(n, s, width=UNIT):
                act.wait_ge(w_loaded[s], (n - s) * 8 + 16)
                act.wait_ge(used, n + 1)
                act.activation(w_hi[s][:, 0:width], raw[s][:, 0:width], ACT.Copy).then_inc(hi_done, 1)

            act.wait_ge(const_loaded, 64)
            act.wait_ge(lb_step, 3)
            act.activation(lbc[:, 2:4, :], lbc[:, 0:2, :], ACT.Exp).then_inc(lb_step, 1)
            for k in range(KD):
                act.wait_ge(x_turned, k + 1)
                act.activation(H[:, k, META:], ps[k % 2][:, 0, :], ACT.Copy).then_inc(x_copied, 1)
            act.wait_ge(meta_turned, 1)
            act.activation(H[:, :, 0:META], ps[2][:, 0, 0:KD * META].rearrange("p (k t) -> p k t", k=KD), ACT.Copy)\
               .then_inc(x_copied, 1)
            split_hi(0, 0)
            split_hi(1, 1)

            def squares(s, tokens, x):
                for k in range(KD):
                    if k >= 2:
                        act.wait_ge(*s.at("acc", k))
                    act.activation(sq[k % 2][:, 0:tokens], x(k), ACT.Square).then_inc(s["sq"], 1)

            def norm_act(s, tokens):
                n, width = pieces(tokens)
                act.wait_ge(*s.at("inv", 1))
                act.activation(stat[0:width, 1, 0:n], stat[0:width, 0, 0:n], ACT.Sqrt).then_inc(s["root"], 1)

            def norm_hi(s, tokens, order=None):
                for k in range(KD):
                    hi, z = z_hi[:, k, 0:tokens], z_now[k % 4][:, 0:tokens]
                    if order:
                        hi, z = blocked(hi), natural(z)
                    act.wait_ge(*s.at("z", k + 1))
                    act.activation(hi, z, ACT.Copy).then_inc(s["hi"], 1)

            act.wait_ge(x_copied, KD + 1)
            squares(n1, T1, lambda k: H[:, k, :])
            norm_act(n1, T1)
            norm_hi(n1, T1)

            n = UNITS["qf"]

            def qf_step(h):
                split_hi(n + 2 * h + 2, 0)
                act.wait_ge(used, n + 2 * h + 3)
                act.activation(two(sig[:, :]), out528(0), ACT.Sigmoid).then_inc(qs["sig"], 1)
                split_hi(n + 2 * h + 3, 1)
                act.wait_ge(used, n + 2 * h + 4)
                act.activation(two(qf[:, 2 * h + 1, :]), out528(1), ACT.Sigmoid, bias=vec("b_f", h))\
                   .then_inc(ps_free[1], 1)
            with act.Fori(0, HEADS) as h:
                qf_step(h)

            n = UNITS["v"]
            split_hi(n + 2, 0)
            split_hi(n + 3, 1)
            split_hi(n + 4, 0)
            act.wait_ge(used, n + 6)
            act.activation(V[:, 0:2, :], ps[0][:, :, :], ACT.Copy).then_inc(ps_free[0], 1)
            act.activation(V0[:, :], ps[2][0:META, 0, :], ACT.Copy).then_inc(vs["act"], 1)
            split_hi(n + 5, 1)

            n = UNITS["ogpin"]

            def og_step(j):
                split_hi(n + 2 * j + 2, 0)
                act.wait_ge(used, n + 2 * j + 3)
                act.activation(two(sig[:, :]), out528(0), ACT.Sigmoid).then_inc(ops["sig"], 1)
                split_hi(n + 2 * j + 3, 1)
                act.wait_ge(used, n + 2 * j + 4)
                act.activation(two(pin[:, j, PADC:]), out528(1), ACT.Copy).then_inc(ops["pin"], 1)
            with act.Fori(0, 4) as j:
                og_step(j)
            for g in range(4):
                act.wait_ge(pools["sum"], g + 1)
                act.activation(two(pin[:, g, PADC:]), out528(g % 2), ACT.Identity, scale=vec("pool_scale", g))\
                   .then_inc(ps_free[g % 2], 1)
            act.wait_ge(lb_step, 9)

            n = UNITS["gates"]

            def head(h):
                act.wait_ge(mx["scan"], h + 1)
                act.activation(lf[:, :], qf[:, 2 * h + 1, :], ACT.Ln, scale=lbc[:, 1, bass.ds(h, 1)],
                               bias=lbc[:, 0, bass.ds(h, 1)]).then_inc(mx["ln"], 1)

                def expo(l):
                    lo = 0 if l <= 3 else META
                    act.wait_ge(mx["sub"], h * LEVELS + l + 1)
                    act.activation(X[l % 3][:, lo:], X[l % 3][:, lo:], ACT.Exp).then_inc(mx["exp"], 1)
                expo(0)
                expo(1)
                act.wait_ge(mx["o"], h + 1)
                act.activation(qe[:, :], A[:, META:], ACT.Exp).then_inc(mx["qe_exp"], 1)
                act.activation(dec[:, 0:3], A[:, META + P - 1:META + 3 * P:P], ACT.Exp).then_inc(mx["qe_exp"], 1)
                act.wait_ge(mx["kd_sub"], 2 * h + 2)
                act.activation(kd[:, :], kd[:, :], ACT.Exp).then_inc(mx["kd_exp"], 1)
                expo(2)
                expo(3)
                split_hi(n + 2 * h + 2, 0)
                act.wait_ge(used, n + 2 * h + 3)
                act.activation(two(gates[:, h, :]), out528(0), ACT.Copy).then_inc(ps_free[0], 1)
                expo(4)
                act.wait_ge(mx["turn"], 10 * h + 7)
                act.activation(kdt[0:META, 0, :], ps[2][0:META, 1, 0:P], ACT.Copy).then_inc(mx["kdt"], 1)
                act.activation(kdt[:, 1:, :], chunked(ps[2][:, 1, P:], 3), ACT.Copy).then_inc(mx["kdt"], 1)
                expo(5)
                expo(6)
                split_hi(n + 2 * h + 3, 1)
                act.wait_ge(used, n + 2 * h + 4)
                act.activation(two(gates[:, HEADS + h, :]), out528(1), ACT.Copy).then_inc(ps_free[1], 1)

            def pair(p):
                head(2 * p)
                head(2 * p + 1)
                act.wait_ge(mx["o"], 2 * p + 3)
                act.activation(qf[:, 4 * p, META:], ps[3][:, 0, :], ACT.Copy).then_inc(mx["o_read"], 1)
                act.activation(qf[:, 4 * p, 0:META], ps[3][:, 1, 96:96 + META], ACT.Copy).then_inc(mx["o_read"], 1)
            act.preload_act_table_set("natural_log_exp_and_others")
            with act.Fori(0, HEADS // 2) as p:
                pair(p)

            act.wait_ge(used, UNITS["gates"] + 18)
            for g in range(4):
                act.activation(z_hi[:, 4 + g, :], pin[:, g, PADC:], ACT.Copy).then_inc(oas["hi"], 1)
            act.wait_ge(mx["o_read"], 9)
            for p in range(4):
                if p >= 2:
                    act.wait_ge(oas["sum"], p - 1)
                act.activation(sq[p % 2][:, :], qf[:, 4 * p, :], ACT.Square).then_inc(oas["sq"], 1)
            for p in range(4):
                act.wait_ge(oas["sum"], p + 1)
                if p >= 2:
                    act.wait_ge(oas["scaled"], p - 1)
                inverse = (rstd, sig)[p % 2]
                act.activation(two(inverse[:, :]), out528(p % 2), ACT.Ln, scale=1.0 / VD, bias=eps)\
                   .then_inc(ps_free[p % 2], 1)
                act.wait_ge(ps_free[p % 2], FREED["oa"][p % 2] + 2 + p // 2)
                act.activation(inverse[:, :], inverse[:, :], ACT.Exp, scale=-0.5).then_inc(oas["inv"], 1)
            for p in range(4):
                act.wait_ge(oas["z"], p + 1)
                act.activation(z_hi[:, p, :], zt[p % 2][:, :], ACT.Copy).then_inc(oas["hi"], 1)

            n = UNITS["branch"]
            with act.Fori(0, 4) as i:
                for s in range(2):
                    m = 2 * i + s
                    act.activation(gates[:, m, :], gates[:, m, :], ACT.Sigmoid).then_inc(brs["sig"], 1)
                    act.activation(gates[:, HEADS + m, :], gates[:, HEADS + m, :], ACT.Sigmoid)\
                       .then_inc(brs["sig"], 1)
                    split_hi(n + m + 2, s)
                    act.wait_ge(brs["mixed"], m + 3)
                    act.activation(mix_hi[:, m, :], zt[s][:, :], ACT.Copy).then_inc(brs["hi"], 1)

            def residual_squares(name, tokens, sems):
                n, freed = UNITS[name], FREED[name]

                def body(i, width):
                    for s in range(2):
                        m = 2 * i + s
                        if width:
                            split_hi(n + m + 2, s, width)
                        if sems:
                            act.wait_ge(ps_free[s], freed[s] + 2 + i)
                            act.activation(sq[s][:, 0:tokens], h_tile(tokens, m), ACT.Square).then_inc(sems["sq"], 1)
                peeled(act, 4, body, WIDTHS[n], after(name, 8))

            residual_squares("out", T1, n2)
            norm_act(n2, T1)
            norm_hi(n2, T1)

            def memory_rows():
                act.wait_ge(mem_loaded, 16)
                for c in range(2):
                    act.activation(mem_square[:, :], mem_rows[:, c, :], ACT.Square, accum_out=mem_stat[:, 0, c:c + 1])\
                       .then_inc(mem_step, 1)
                    act.wait_ge(mem_step, c + 1)
                act.activation(mem_stat[:, 1, :], mem_stat[:, 0, :], ACT.Sqrt, scale=1.0 / D, bias=eps)\
                   .then_inc(mem_step, 1)
                act.wait_ge(mem_turned, 1)
                for k in range(KD):
                    if k >= 4:
                        act.wait_ge(mem_lo, k - 3)
                    act.activation(mz_hi[:, k, :], turned_memory(k), ACT.Identity, scale=vec("mem_g", k))\
                       .then_inc(mem_hi, 1)

            def ffn(tag, tokens, s, norm, between=None):
                for b, half in enumerate("ab"):
                    name = f"up{tag}_{half}"
                    n = UNITS[name]

                    def body(j, width):
                        jj = b * FH + j
                        split_hi(n + 2 * j + 2, 0, width)
                        act.wait_ge(used, n + 2 * j + 3)
                        if tokens == T1:
                            act.activation(two(ub[:, 2:]), out528(0), ACT.Copy).then_inc(ps_free[0], 1)
                            act.wait_ge(*s.at("conv", 3 * jj + 3))
                            act.activation(sig[:, :], cv[2][:, :], ACT.Sigmoid).then_inc(s["sig"], 1)
                        else:
                            act.activation(sig[:, 0:tokens], psv(tokens, 0), ACT.Sigmoid).then_inc(s["sig"], 1)
                        split_hi(n + 2 * j + 3, 1, width)
                        act.wait_ge(ps_free[1], FREED[name][1] + 2 + j)
                        act.activation(g_hi[:, j, 0:tokens], gv[0][:, 0:tokens], ACT.Copy).then_inc(s["hi"], 1)
                    peeled(act, FH, body, UNIT, SLOT)
                    if b and between:
                        between()
                    residual_squares(f"down{tag}_{half}", tokens, norm if b else None)
            ffn("", T1, f1, fin, memory_rows)

            n = UNITS["mem"]

            def memory_keys(l, t_):
                act.wait_ge(used, n + 4 * l + t_ + 3)
                head = MH * l + 2 * t_
                act.activation(mk[:, head, :], ps[t_][:, 0, 0:NMEM], ACT.Copy)
                for j in range(2):
                    x = act.activation(mk[j * HD:(j + 1) * HD, head + 1, :], ps[t_][HD:, 0, 0:NMEM], ACT.Copy)
                x.then_inc(ps_free[t_], 1)
            split_hi(n + 2, 0)
            memory_keys(0, 0)
            split_hi(n + 3, 1)
            memory_keys(0, 1)
            split_hi(n + 4, 0)
            split_hi(n + 5, 1)
            norm_act(fin, T1)
            for k in range(KD):
                act.wait_ge(*fin.at("z", k + 1))
                if k >= 2:
                    act.wait_ge(*norm_a0.at("acc", k))
                act.activation(sq[k % 2][:, 0:SEQ], h_tile(SEQ, k), ACT.Square).then_inc(norm_a0["sq"], 1)
                if k == 3:
                    memory_keys(1, 0)
                    split_hi(n + 6, 0)
                    memory_keys(1, 1)
                    split_hi(n + 7, 1)
            split_hi(n + 8, 0)
            split_hi(n + 9, 1)

            def layer(l):
                norm_act(norm_a[l], SEQ)
                norm_hi(norm_a[l], SEQ, l)

                n, freed = UNITS[f"qk{l}"], FREED[f"qk{l}"]

                def project(i, first, into, at_, scale, width):
                    for s in range(2):
                        m = 2 * (first + i) + s
                        split_hi(n + m + 2, s, width)
                        act.wait_ge(used, n + m + 3)
                        if into is k_heads:
                            act.activation(into[:, bass.ds(4 * i + (at_ + 2 * s), 1), :], ps[s][:, 0:1, :],
                                           ACT.Copy, scale=scale)
                            for j in range(2):
                                x = act.activation(
                                    into[j * HD:(j + 1) * HD, bass.ds(4 * i + (at_ + 2 * s + 1), 1), :],
                                    ps[s][HD:, 0:1, :], ACT.Copy, scale=scale)
                        else:
                            for j in range(2):
                                x = act.activation(into[0:HD, bass.ds(4 * i + (at_ + 2 * s + j), 1), :],
                                                   ps[s][j * HD:(j + 1) * HD, 0:1, :], ACT.Copy, scale=scale)
                        x.then_inc(ps_free[s], 1)
                with act.Fori(0, 3) as i:
                    project(i, 0, q_heads, 0, HD ** -0.5, UNIT)
                if l:
                    with act.Fori(0, 3) as i:
                        project(i, 3, k_heads, 0, 1.0, UNIT)
                else:
                    project(0, 3, k_heads, 0, 1.0, UNIT)
                project(0, (4, 6)[l], q_heads, QH, HD ** -0.5, WIDTHS[UNITS[f"v{l}"]])

                n = UNITS[f"v{l}"]
                for half in range((1, 2)[l]):
                    count, width = ((2, KVA * HD), (4, 384))[l]
                    for i in range(count - 1):
                        m = count * half + i
                        split_hi(n + m + 2, i % 2, WIDTHS[n + m + 2])
                    act.wait_ge(used, n + count * (half + 1) + 2)
                    act.activation(v_tok[:, 0:2, half * width:(half + 1) * width], ps[0][:, :, 0:width], ACT.Copy)\
                       .then_inc(ps_free[0], 1)
                    m = count * (half + 1) - 1
                    split_hi(n + m + 2, 1, WIDTHS[n + m + 2])

                s = atts[l]

                def exps(h, r, memory, blocks):
                    for b in blocks:
                        lo, width = span(memory, b)
                        act.activation(ls[r][:, b, lo:lo + width], ls[r][:, b, lo:lo + width], ACT.Exp,
                                       bias=neg_max[r][:, b:b + 1], accum_out=row_sum[r][:, b:b + 1])\
                           .then_inc(s["exp"], 1)

                def copy(h, memory, b):
                    _, width = span(memory, b)
                    act.wait_ge(*s.at("t", 4 * h + (b + 1)))
                    act.wait_ge(*s.at("y", 4 * h + (b - 1)))
                    act.activation(pts[0][:, 0:width], ps[3][:, 0, 0:width], ACT.Copy).then_inc(s["pa"], 1)

                def step(h, r, n_, g):
                    mid, back = 1 <= n_ <= AH, 2 <= n_ < AH + 2
                    if back:
                        copy(h - 2, n_ - 2 >= QH, 0)
                    if mid:
                        memory = n_ - 1 >= QH
                        act.wait_ge(*s.at("neg", h))
                        if l == 0 and not memory:
                            act.activation(sink_exp[(r + 2) % 3][:, :], neg_max[(r + 2) % 3][:, :], ACT.Exp,
                                           bias=vec("sink", h - 1))
                        exps(h - 1, (r + 2) % 3, memory, (0, 1))
                    if back:
                        copy(h - 2, n_ - 2 >= QH, 2)
                    if mid:
                        exps(h - 1, (r + 2) % 3, memory, (2, 3))
                head_steps(act, step)

                for k in range(KD):
                    act.wait_ge(*s.at("turned", k + 1))
                    act.activation(z_hi[:, k, 0:SEQ], ps[k % 2][:, 0, :], ACT.Copy).then_inc(s["hi"], 1)
                residual_squares(f"out{l}", SEQ, norm_f[l])
                norm_act(norm_f[l], SEQ)
                norm_hi(norm_f[l], SEQ)
                ffn(str(l), SEQ, ffn2[l], (norm_a1, norm_o)[l])
            layer(0)
            layer(1)
            norm_act(norm_o, SEQ)
            act.wait_ge(out_turned, 1)
            for c in range(CHUNKS - 1):
                act.activation(out_rows[:, c, 0:D // 2], ps[c][:, 0, :], ACT.Copy)
            act.wait_ge(out_turned, 2)
            for c in range(CHUNKS):
                if c == 3:
                    act.activation(out_rows[:, c, 0:D // 2], ps[c][:, 0, :], ACT.Copy)
                act.activation(out_rows[:, c, D // 2:], ps[c][:, 1, :], ACT.Copy).then_inc(out_copied, 1)

        @block.vector
        def _(dve):
            def split_lo(n, s, width=UNIT):
                dve.wait_ge(hi_done, n + 1)
                dve.tensor_tensor(w_lo[s][:, 0:width], raw[s][:, 0:width], w_hi[s][:, 0:width].bitcast(F32),
                                  ALU.subtract).then_inc(lo_done, 1)

            dve.wait_ge(const_loaded, 64)
            lb0 = par[:, pc["lb0"]:pc["lb0"] + 8]
            lb1 = par[:, pc["lb1"]:pc["lb1"] + 8]
            dve.tensor_tensor(lbc[:, 2, :], lb0, lb1, ALU.max).then_inc(lb_step, 1)
            dve.wait_ge(lb_step, 1)
            dve.tensor_tensor(lbc[:, 0, :], lb0, lbc[:, 2, :], ALU.subtract).then_inc(lb_step, 1)
            dve.tensor_tensor(lbc[:, 1, :], lb1, lbc[:, 2, :], ALU.subtract).then_inc(lb_step, 1)
            dve.wait_ge(lb_step, 4)
            dve.tensor_tensor(lbc[:, 0, :], lbc[:, 2, :], lbc[:, 3, :], ALU.add).then_inc(lb_step, 1)
            dve.wait_ge(lb_step, 5)
            dve.reciprocal(lbc[:, 1, :], lbc[:, 0, :]).then_inc(lb_step, 1)
            dve.wait_ge(lb_step, 6)
            dve.tensor_tensor(lbc[:, 0, :], lbc[:, 2, :], lbc[:, 1, :], ALU.mult).then_inc(lb_step, 1)
            dve.wait_ge(lb_step, 7)
            dve.tensor_scalar(lbc[:, 1, :], lbc[:, 0, :], -1.0, 1.0, ALU.mult, ALU.add).then_inc(lb_step, 1)
            dve.tensor_scalar(lbc[:, 2, :], lbc[:, 0, :], 1.0, -1.0, ALU.mult, ALU.add).then_inc(lb_step, 1)
            dve.tensor_copy(masks[:, :, :].rearrange("p a b -> p (a b)"), mask_rows[:, :]).then_inc(masks_ready, 1)
            split_lo(0, 0)
            split_lo(1, 1)

            def sum_squares(s, tokens):
                dve.memset(acc[:, 0:tokens], 0.0).then_inc(s["acc"], 1)
                for k in range(KD):
                    dve.wait_ge(*s.at("sq", k + 1))
                    dve.wait_ge(*s.at("acc", k + 1))
                    dve.tensor_tensor(acc[:, 0:tokens], acc[:, 0:tokens], sq[k % 2][:, 0:tokens], ALU.add)\
                       .then_inc(s["acc"], 1)

            def norm_inverse(s, tokens):
                n, width = pieces(tokens)
                v, root, y, yy, f, better = (stat[0:width, i, 0:n] for i in range(6))
                dve.wait_ge(*s.at("sum", 1))
                dve.tensor_scalar(v, ps[2][0:width, 0, 0:n], 1.0 / D, EPS, ALU.mult, ALU.add).then_inc(s["inv"], 1)
                dve.wait_ge(*s.at("root", 1))
                dve.reciprocal(y, root).then_inc(s["inv"], 1)
                dve.wait_ge(*s.at("inv", 2))
                dve.tensor_tensor(yy, y, y, ALU.mult).then_inc(s["inv"], 1)
                dve.wait_ge(*s.at("inv", 3))
                dve.tensor_tensor(f, yy, v, ALU.mult).then_inc(s["inv"], 1)
                dve.wait_ge(*s.at("inv", 4))
                dve.tensor_scalar(f, f, -0.5, 1.5, ALU.mult, ALU.add).then_inc(s["inv"], 1)
                dve.wait_ge(*s.at("inv", 5))
                dve.tensor_tensor(better, y, f, ALU.mult).then_inc(s["inv"], 1)
                dve.wait_ge(*s.at("wide", 1))

            def norm_scale(s, tokens, x, g, order=None):
                norm_inverse(s, tokens)
                for k in range(KD):
                    if k >= 4:
                        dve.wait_ge(*s.at(("even", "odd")[k % 2], k // 2 - 1))
                    dve.scalar_tensor_tensor(shaped(tokens, z_now[k % 4]), two(x(k)) if tokens == T1 else x(k), g(k),
                                             psv(tokens, 3), ALU.mult, ALU.mult).then_inc(s["z"], 1)
                    if k % 2:
                        lo, z = z_lo[:, k - 1, 0:tokens], z_now[(k - 1) % 4][:, 0:tokens]
                        hi = z_hi[:, k - 1, 0:tokens].bitcast(F32)
                        if order:
                            lo, z, hi = blocked(lo), natural(z), blocked(hi)
                        dve.wait_ge(*s.at("hi", k))
                        dve.tensor_tensor(lo, z, hi, ALU.subtract).then_inc(s["even"], 1)

            sum_squares(n1, T1)
            norm_scale(n1, T1, lambda k: H[:, k, :], lambda k: vec("norm1", k))

            n = UNITS["qf"]
            with dve.Fori(0, HEADS) as h:
                split_lo(n + 2 * h + 2, 0)
                dve.wait_ge(qs["sig"], h + 1)
                dve.tensor_tensor(two(qf[:, 2 * h, :]), out528(0), two(sig[:, :]), ALU.mult).then_inc(ps_free[0], 1)
                split_lo(n + 2 * h + 3, 1)
            n = UNITS["v"]
            split_lo(n + 2, 0)
            split_lo(n + 3, 1)
            split_lo(n + 4, 0)
            dve.wait_ge(used, n + 6)
            dve.tensor_copy(V[:, 2:4, :], ps[1][:, :, :]).then_inc(vs["dve"], 1)
            split_lo(n + 5, 1)
            n = UNITS["ogpin"]
            with dve.Fori(0, 4) as j:
                split_lo(n + 2 * j + 2, 0)
                dve.wait_ge(ops["sig"], j + 1)
                dve.tensor_tensor(two(og[:, j, :]), out528(0), two(sig[:, :]), ALU.mult).then_inc(ps_free[0], 1)
                split_lo(n + 2 * j + 3, 1)

            n = UNITS["gates"]
            dve.wait_ge(ps_free[0], POOLED[0])
            dve.wait_ge(ps_free[1], POOLED[1])
            dve.wait_ge(masks_ready, 1)

            def head(h):
                dve.wait_ge(mx["turn"], 10 * h + 1)
                dve.tensor_scalar(kk[:, :], qf[:, 2 * h + 1, :], lbc[:, 2, bass.ds(h, 1)], lbc[:, 1, bass.ds(h, 1)],
                                  ALU.mult, ALU.add).then_inc(mx["k"], 1)
                dve.wait_ge(mx["ln"], h + 1)
                dve.tensor_tensor_scan(A[:, :], restart, lf[:, :], 0.0, ALU.mult, ALU.add).then_inc(mx["scan"], 1)
                dve.wait_ge(mx["scan"], h + 2)

                def sub(l):
                    left, right, _ = halves(X[l % 3][:, :], l)
                    aleft, aright, ref = halves(A[:, :], l)
                    if l >= 3:
                        dve.wait_ge(mx["turn"], 10 * h + turn_of(l - 3) + 2)
                    dve.tensor_tensor(right, aright, ref, ALU.subtract)
                    dve.tensor_tensor(left, ref, aleft, ALU.subtract).then_inc(mx["sub"], 1)

                def mul_right(l):
                    _, right, _ = halves(X[l % 3][:, :], l)
                    _, qright, _ = halves(qf[:, 2 * h, :], l)
                    dve.wait_ge(mx["exp"], h * LEVELS + l + 1)
                    dve.tensor_tensor(right, right, qright, ALU.mult).then_inc(mx["mul_r"], 1)

                def scored(l):
                    dve.wait_ge(mx["turn"], 10 * h + turn_of(l) + 2)
                    dve.wait_ge(mx["score_read"], 9 * h + (l + 3 if l <= 3 else l + 4))

                def take(l):
                    tt = turn_of(l)
                    dve.copy_predicated(chunked(sc[:, :], 4),
                                        masks[:, l:l + 1, :].to_broadcast([P, 4, P]),
                                        chunked(ps[2][:, tt % 2, :], 4))\
                       .then_inc(mx["score_read"], 1)

                sub(0)
                sub(1)
                dve.tensor_tensor(kd[:, 0:META], A[:, META - 1:META].to_broadcast([P, META]), A[:, 0:META],
                                  ALU.subtract).then_inc(mx["kd_sub"], 1)
                mid = chunked(A[:, META:META + 3 * P], 3)
                dve.tensor_tensor(chunked(kd[:, META:], 3), mid[:, :, P - 1:P].to_broadcast([P, 3, P]), mid,
                                  ALU.subtract).then_inc(mx["kd_sub"], 1)
                mul_right(0)
                dve.wait_ge(mx["o"], h + 1)
                dve.wait_ge(mx["turn"], 10 * h + 2)
                dve.tensor_tensor(chunked(sc[:, :], 4), chunked(ps[2][:, 0, :], 4),
                                  ident.rearrange("p (c t) -> p c t", c=1).to_broadcast([P, 4, P]), ALU.mult)\
                   .then_inc(mx["score_read"], 1)
                sub(2)
                scored(0)
                mul_right(1)
                take(0)
                dve.wait_ge(mx["qe_exp"], 2 * h + 1)
                dve.tensor_tensor(qe[:, :], qe[:, :], qf[:, 2 * h, META:], ALU.mult).then_inc(mx["qe"], 1)
                sub(3)
                scored(1)
                mul_right(2)
                take(1)
                sub(4)
                scored(2)
                mul_right(3)
                take(2)
                sub(5)
                split_lo(n + 2 * h + 2, 0)
                scored(3)
                mul_right(4)
                take(3)
                s0 = ps[3][0:META, 1, :]
                dve.tensor_tensor(sc0[:, :], s0[:, 0:META], ident[0:META, 0:META], ALU.mult).then_inc(mx["meta"], 1)

                def take_meta(l):
                    dve.copy_predicated(sc0[:, :], masks[0:META, l, 0:META],
                                        s0[:, (l + 1) * META:(l + 2) * META]).then_inc(mx["meta"], 1)

                dve.wait_ge(mx["meta"], 5 * h + 1)
                sub(6)
                take_meta(0)
                dve.wait_ge(mx["meta"], 5 * h + 2)
                mul_right(5)
                take_meta(1)
                dve.wait_ge(mx["turn"], 10 * h + 8)
                dve.wait_ge(mx["qe_exp"], 2 * h + 2)
                dve.wait_ge(mx["meta"], 5 * h + 3)
                dve.tensor_copy(st[:, 0, :], ps[2][:, 0, 0:VD]).then_inc(mx["states"], 1)
                take_meta(2)
                for c in range(1, 4):
                    dve.wait_ge(mx["states"], 3 * h + c)
                    if c == 2:
                        dve.wait_ge(mx["meta"], 5 * h + 4)
                    x = dve.scalar_tensor_tensor(st[:, c, :], st[:, c - 1, :], dec[:, c - 1:c],
                                                 ps[2][:, 0, c * VD:(c + 1) * VD], ALU.mult, ALU.add)
                    x.then_inc(mx["states"] if c < 3 else mx["score_read"], 1)
                    if c == 2:
                        take_meta(3)
                scored(4)
                mul_right(6)
                take(4)
                scored(5)
                split_lo(n + 2 * h + 3, 1)
                take(5)
                scored(6)
                dve.memset(spare[:, :], 0.0)
                take(6)

            with dve.Fori(0, HEADS // 2) as p:
                head(2 * p)
                head(2 * p + 1)

            for g in range(4):
                dve.wait_ge(oas["hi"], g + 1)
                dve.tensor_tensor(z_lo[:, 4 + g, :], pin[:, g, PADC:], z_hi[:, 4 + g, :].bitcast(F32), ALU.subtract)\
                   .then_inc(oas["pin_lo"], 1)
            for p in range(4):
                dve.wait_ge(oas["inv"], p + 1)
                scaled = (ta, tb)[p % 2]
                if p >= 2:
                    dve.wait_ge(oas["z"], p - 1)
                dve.scalar_tensor_tensor(scaled[:, :], qf[:, 4 * p, :], vec("head_g", p), (rstd, sig)[p % 2][:, :],
                                         ALU.mult, ALU.mult).then_inc(oas["scaled"], 1)
                dve.wait_ge(oas["scaled"], p + 1)
                if p >= 2:
                    dve.wait_ge(oas["lo"], p - 1)
                dve.tensor_tensor(zt[p % 2][:, :], scaled[:, :], og[:, p, :], ALU.mult).then_inc(oas["z"], 1)

            n = UNITS["branch"]
            with dve.Fori(0, 4) as i:
                for s in range(2):
                    m = 2 * i + s
                    split_lo(n + m + 2, s)
                    dve.wait_ge(used, n + m + 3)
                    dve.wait_ge(brs["sig"], 2 * m + 2)
                    dve.tensor_tensor(two(ta[:, :]), out528(2 * s), two(gates[:, m, :]), ALU.mult)\
                       .then_inc(brs["a"], 1)
                    dve.tensor_tensor(two(tb[:, :]), out528(2 * s + 1), two(gates[:, HEADS + m, :]), ALU.mult)\
                       .then_inc(brs["a"], 1)
                    dve.wait_ge(brs["a"], 2 * m + 2)
                    dve.wait_ge(brs["lo"], m + 1)
                    dve.tensor_tensor(zt[s][:, :], ta[:, :], tb[:, :], ALU.add).then_inc(brs["mixed"], 1)

            def residual(name, tokens, sems, order=None):
                n, freed = UNITS[name], FREED[name]
                if sems:
                    dve.memset(acc[:, 0:tokens], 0.0).then_inc(sems["acc"], 1)

                def body(i, width):
                    for s in range(2):
                        m = 2 * i + s
                        if width:
                            split_lo(n + m + 2, s, width)
                        dve.wait_ge(used, n + m + 3)
                        tile, add = h_tile(tokens, m), psv(tokens, s)
                        if tokens == T1:
                            tile = two(tile)
                        elif order:
                            tile, add = natural(tile), blocked(add)
                        dve.tensor_tensor(tile, tile, add, ALU.add).then_inc(ps_free[s], 1)
                        if sems:
                            dve.wait_ge(*sems.at("sq", m + 1))
                            dve.wait_ge(*sems.at("acc", m + 1))
                            dve.tensor_tensor(acc[:, 0:tokens], acc[:, 0:tokens], sq[s][:, 0:tokens], ALU.add)\
                               .then_inc(sems["acc"], 1)
                peeled(dve, 4, body, WIDTHS[n], after(name, 8))

            residual("out", T1, n2)
            dve.wait_ge(padded, 1)
            norm_scale(n2, T1, lambda k: H[:, k, :], lambda k: vec("norm2", k))

            def memory_rows():
                dve.wait_ge(mem_step, 3)
                dve.reciprocal(mem_stat[:, 2, :], mem_stat[:, 1, :]).then_inc(mem_step, 1)
                dve.wait_ge(mem_step, 4)
                for c in range(2):
                    dve.tensor_scalar(mem_rows[:, c, :], mem_rows[:, c, :], mem_stat[:, 2, c:c + 1], 1.0,
                                      ALU.mult, ALU.mult).then_inc(mem_step, 1)
                for k in range(KD):
                    dve.wait_ge(mem_hi, k + 1)
                    dve.scalar_tensor_tensor(mz_lo[:, k, :], turned_memory(k), vec("mem_g", k),
                                             mz_hi[:, k, :].bitcast(F32), ALU.mult, ALU.subtract).then_inc(mem_lo, 1)

            def ffn(tag, tokens, s, norm, between=None):
                for b, half in enumerate("ab"):
                    name = f"up{tag}_{half}"
                    n = UNITS[name]

                    def body(j, width):
                        jj = b * FH + j
                        split_lo(n + 2 * j + 2, 0, width)
                        if tokens == T1:
                            w = [vec("conv_w", i * FT + jj) for i in range(3)]
                            dve.wait_ge(ps_free[0], FREED[name][0] + 2 + j)
                            dve.tensor_scalar(cv[0][:, :], ub[:, 2:], w[2], vec("conv_b", jj), ALU.mult, ALU.add)\
                               .then_inc(s["conv"], 1)
                            dve.wait_ge(*s.at("conv", 3 * jj + 1))
                            dve.scalar_tensor_tensor(cv[1][:, :], ub[:, 1:1 + T1], w[1], cv[0][:, :],
                                                     ALU.mult, ALU.add).then_inc(s["conv"], 1)
                            dve.wait_ge(*s.at("conv", 3 * jj + 2))
                            dve.scalar_tensor_tensor(cv[2][:, :], ub[:, 0:T1], w[0], cv[1][:, :],
                                                     ALU.mult, ALU.add).then_inc(s["conv"], 1)
                            dve.wait_ge(*s.at("conv", 3 * jj + 3))
                            dve.wait_ge(*s.at("sig", jj + 1))
                            dve.tensor_tensor(si[:, :], cv[2][:, :], sig[:, :], ALU.mult).then_inc(s["si"], 1)
                        else:
                            dve.wait_ge(*s.at("sig", jj + 1))
                            dve.tensor_tensor(si[:, 0:tokens], psv(tokens, 0), sig[:, 0:tokens], ALU.mult)\
                               .then_inc(ps_free[0], 1)
                        split_lo(n + 2 * j + 3, 1, width)
                        dve.wait_ge(used, n + 2 * j + 4)
                        if tokens == T1:
                            dve.wait_ge(*s.at("si", jj + 1))
                        else:
                            dve.wait_ge(ps_free[0], FREED[name][0] + 2 + j)
                        dve.wait_ge(*s.at("lo", jj + 1))
                        dve.tensor_tensor(shaped(tokens, gv[0]), shaped(tokens, si), psv(tokens, 1), ALU.mult)\
                           .then_inc(ps_free[1], 1)
                    peeled(dve, FH, body, UNIT, SLOT)
                    if b and between:
                        between()
                    residual(f"down{tag}_{half}", tokens, norm if b else None)
            ffn("", T1, f1, fin, memory_rows)

            n = UNITS["mem"]

            def memory_values(l):
                dve.wait_ge(used, n + 4 * l + 6)
                dve.tensor_copy(mv[:, 2 * l:2 * l + 2, :], ps[0][:, :, 0:NMEM]).then_inc(ps_free[0], 1)
            split_lo(n + 2, 0)
            split_lo(n + 3, 1)
            split_lo(n + 4, 0)
            split_lo(n + 5, 1)
            norm_inverse(fin, T1)
            dve.memset(acc[:, 0:SEQ], 0.0).then_inc(norm_a0["acc"], 1)

            def add_square(k):
                dve.wait_ge(*norm_a0.at("sq", k + 1))
                dve.wait_ge(*norm_a0.at("acc", k + 1))
                dve.tensor_tensor(acc[:, 0:SEQ], acc[:, 0:SEQ], sq[k % 2][:, 0:SEQ], ALU.add)\
                   .then_inc(norm_a0["acc"], 1)
            for k in range(KD):
                dve.scalar_tensor_tensor(two(H[:, k, :]), two(H[:, k, :]), vec("final_g", k), out528(3),
                                         ALU.mult, ALU.mult).then_inc(fin["z"], 1)
                if k >= 1:
                    add_square(k - 1)
                if k == 0:
                    memory_values(0)
                if k == 4:
                    split_lo(n + 6, 0)
                    split_lo(n + 7, 1)
            add_square(KD - 1)
            split_lo(n + 8, 0)
            memory_values(1)
            split_lo(n + 9, 1)

            def layer(l):
                norm_scale(norm_a[l], SEQ, lambda k: h_tile(SEQ, k), lambda k: vec("mix_g", KD * l + k), l)
                n = UNITS[f"qk{l}"]

                def body(i, width):
                    split_lo(n + 2 * i + 2, 0, width)
                    split_lo(n + 2 * i + 3, 1, width)
                peeled(dve, (5, 7)[l], body, UNIT, WIDTHS[UNITS[f"v{l}"]])
                dve.memset(q_heads[HD:, QH:, :], 0.0)
                dve.memset(q_now[0][HD:, :], 0.0)
                n = UNITS[f"v{l}"]
                for half in range((1, 2)[l]):
                    count, width = ((2, KVA * HD), (4, 384))[l]
                    for i in range(count - 1):
                        m = count * half + i
                        split_lo(n + m + 2, i % 2, WIDTHS[n + m + 2])
                    dve.wait_ge(used, n + count * (half + 1) + 2)
                    if half == l:
                        dve.memset(q_now[1][HD:, :], 0.0)
                        dve.memset(q_now[2][HD:, :], 0.0)
                    dve.tensor_copy(v_tok[:, 2:4, half * width:(half + 1) * width], ps[1][:, :, 0:width])\
                       .then_inc(ps_free[1], 1)
                    m = count * (half + 1) - 1
                    split_lo(n + m + 2, 1, WIDTHS[n + m + 2])

                s = atts[l]
                if l == 0:
                    dve.wait_ge(att_loaded, 16)

                def biased(h, r, memory, b):
                    lo, width = span(memory, b)
                    out, x = ls[r][:, b, lo:lo + width], banks(r + b)[:, 0:width]
                    dve.wait_ge(*s.at("s", 4 * h + (b + 1)))
                    if memory:
                        dve.tensor_copy(out, x).then_inc(s["ls"], 1)
                    elif l == 0:
                        dve.scalar_tensor_tensor(out, att_con[:, lo:lo + width],
                                                 con[:, bass.ds(cc["slopes"] + h, 1)], x, ALU.mult, ALU.add)\
                           .then_inc(s["ls"], 1)
                    else:
                        at_ = (0, 2 * P, 2 * P, 5 * P)[b]
                        dve.tensor_tensor(out, x, bias[r][:, at_:at_ + width], ALU.add).then_inc(s["ls"], 1)

                def largest(h, r, memory, b):
                    lo, width = span(memory, b)
                    dve.wait_ge(*s.at("ls", 4 * h + (b + 1)))
                    dve.tensor_reduce(row_max[r][:, b:b + 1], ls[r][:, b, lo:lo + width], AX.X, ALU.max)\
                       .then_inc(s["max"], 1)

                def copy(h, memory, b):
                    _, width = span(memory, b)
                    dve.wait_ge(*s.at("t", 4 * h + (b + 1)))
                    dve.wait_ge(*s.at("y", 4 * h + (b - 1)))
                    dve.tensor_copy(pts[1][:, 0:width], ps[3][:, 1, 0:width]).then_inc(s["pd"], 1)

                def step(h, r, n_, g):
                    front, back = n_ < AH, 2 <= n_ < AH + 2
                    memory, back_memory = n_ >= QH, n_ - 2 >= QH
                    rb = (r + 1) % 3
                    if front:
                        dve.wait_ge(*s.at("t", 4 * h - 8))
                        if l == 1 and not memory:
                            dve.wait_ge(*s.at("bias", h + 1))
                        biased(h, r, memory, 0)
                        biased(h, r, memory, 1)
                    if back:
                        dve.wait_ge(*s.at("exp", 4 * h - 4))
                        if l == 0 and not back_memory:
                            dve.tensor_tensor(row_sum[rb][:, :], row_sum[rb][:, :], sink_exp[rb][:, :], ALU.add)\
                               .then_inc(s["sum"], 1)
                            dve.wait_ge(*s.at("sum", h - 1))
                        dve.reciprocal(rsum[rb][:, :], row_sum[rb][:, :]).then_inc(s["inv"], 1)
                        copy(h - 2, back_memory, 1)
                    if n_ >= 3:
                        dve.wait_ge(*s.at("inv", h - 2))
                        dve.wait_ge(*s.at("y", 4 * h - 8))
                        dve.tensor_tensor(y_tok[:, :, bass.ds(h * HD - 3 * HD, HD)], chunked(y_bank(r), 4),
                                          rsum[r][:, :].rearrange("p (c o) -> p c o", o=1)
                                                       .to_broadcast([P, 4, HD]), ALU.mult).then_inc(s["out"], 1)
                    if front:
                        largest(h, r, memory, 0)
                        biased(h, r, memory, 2)
                        largest(h, r, memory, 1)
                        biased(h, r, memory, 3)
                        largest(h, r, memory, 2)
                    if back:
                        copy(h - 2, back_memory, 3)
                    if front:
                        largest(h, r, memory, 3)
                        dve.wait_ge(*s.at("max", 4 * h + 4))
                        if l == 0 and not memory:
                            dve.tensor_scalar(neg_max[r][:, :], row_max[r][:, :], vec("sink", h), -1.0,
                                              ALU.max, ALU.mult).then_inc(s["neg"], 1)
                        else:
                            dve.tensor_scalar(neg_max[r][:, :], row_max[r][:, :], -1.0, 1.0, ALU.mult, ALU.mult)\
                               .then_inc(s["neg"], 1)
                head_steps(dve, step)

                for k in range(KD):
                    dve.wait_ge(*s.at("hi", k + 1))
                    dve.tensor_tensor(z_lo[:, k, 0:SEQ], ps[k % 2][:, 0, :], z_hi[:, k, 0:SEQ].bitcast(F32),
                                      ALU.subtract).then_inc(ps_free[k % 2], 1)
                residual(f"out{l}", SEQ, norm_f[l], l)
                norm_scale(norm_f[l], SEQ, lambda k: h_tile(SEQ, k), lambda k: vec("ffn_g", KD * l + k))
                ffn(str(l), SEQ, ffn2[l], (norm_a1, norm_o)[l])
            layer(0)
            layer(1)

            norm_inverse(norm_o, SEQ)
            for k in range(KD):
                dve.scalar_tensor_tensor(h_tile(SEQ, k), h_tile(SEQ, k), vec("out_g", k), psv(SEQ, 3),
                                         ALU.mult, ALU.mult).then_inc(norm_o["z"], 1)

        @block.tensor
        def _(pe):
            uses = [0, 0]

            def products(s, k, w0, rhs_hi, rhs_lo, outs, first, last):
                for w, rhs, a, b in ((w_hi, rhs_hi, first, False), (w_hi, rhs_lo, False, False),
                                     (w_lo, rhs_hi, False, last)):
                    for out, lo, width in outs:
                        x = pe.matmul(out, w[s][:, w0 + k * P:w0 + (k + 1) * P], rhs[:, lo:lo + width],
                                      start=a, stop=b)
                return x

            def outs528(i):
                return [(ps[i][:, b, 0:HALF], b * HALF, HALF) for b in range(2)]

            def unit(n, s, i, kt=KD):
                pe.wait_ge(lo_done, n + 3)
                for k in range(kt):
                    x = products(s, k, 0, z_hi[:, k, :], z_lo[:, k, :], outs528(i), k == 0, k == kt - 1)
                x.then_inc(used, 1)

            def gemm(name, tokens, count, hi, lo, kt=KD, tile_ready=None):
                n, freed = UNITS[name], FREED[name]

                def pair(i, tile_ready):
                    for s in range(2):
                        pe.wait_ge(ps_free[s], freed[s] + 1 + i)
                        pe.wait_ge(lo_done, n + 2 * i + s + 3)
                        outs = outs528(s) if tokens == T1 else [(ps[s][:, 0, 0:tokens], 0, tokens)]
                        for k in range(kt):
                            if tile_ready and s == 0:
                                tile_ready(k)
                            x = products(s, k, 0, hi[:, k, :], lo[:, k, :], outs, k == 0, k == kt - 1)
                        x.then_inc(used, 1)
                if tile_ready:
                    pair(0, tile_ready)
                    with pe.Fori(0, count - 1) as i:
                        pair(i + 1, None)
                else:
                    with pe.Fori(0, count) as i:
                        pair(i, None)

            def z_tile(s):
                return lambda k: pe.wait_ge(*s.at(("even", "odd")[k % 2], k // 2 + 1))

            pe.wait_ge(const_loaded, 64)
            pe.wait_ge(x_loaded, 80)
            for k in range(KD):
                if k >= 2:
                    pe.wait_ge(x_copied, k - 1)
                for c in range(CHUNKS):
                    x = pe.transpose(ps[k % 2][:, 0, c * P:(c + 1) * P], x_rows[:, c, k * P:(k + 1) * P], ident)
                x.then_inc(x_turned, 1)
            for k in range(KD):
                x = pe.transpose(ps[2][:, 0, k * META:(k + 1) * META], meta_rows[:, k * P:(k + 1) * P],
                                 ident[0:META, 0:META])
            x.then_inc(meta_turned, 1)

            def norm_sum(s, tokens):
                n, width = pieces(tokens)
                pe.wait_ge(*s.at("acc", KD + 1))
                for c in range(n):
                    x = pe.matmul(ps[2][0:width, 0, c:c + 1], acc[:, c * width:(c + 1) * width], ones[:, 0:1],
                                  start=True, stop=True)
                x.then_inc(s["sum"], 1)

            def norm_spread(s, tokens):
                n, width = pieces(tokens)
                pe.wait_ge(*s.at("inv", 6))
                for c in range(n):
                    b, lo = divmod(c * width, HALF) if tokens == T1 else (0, c * width)
                    x = pe.matmul(ps[3][:, b, lo:lo + width], stat[0:width, 5, c:c + 1].to_broadcast([width, P]),
                                  ident[0:width, 0:width], start=True, stop=True)
                x.then_inc(s["wide"], 1)

            pe.wait_ge(x_copied, KD + 1)
            norm_sum(n1, T1)
            norm_spread(n1, T1)

            gemm("qf", T1, HEADS, z_hi, z_lo, KD, z_tile(n1))
            uses = [HEADS, HEADS]

            n = UNITS["v"]
            pe.wait_ge(ps_free[0], uses[0] + 1)
            pe.wait_ge(ps_free[1], uses[1] + 1)
            into = [(ps[0], 0, META), (ps[0], 1, META + P), (ps[1], 0, META + 2 * P), (ps[1], 1, META + 3 * P),
                    (ps[2], 0, 0)]
            for i in range(4):
                pe.wait_ge(lo_done, n + i + 3)
                s = i % 2
                for kk_ in range(2):
                    k = 2 * i + kk_
                    for zz, ww, a, b in ((z_hi, w_hi, k == 0, False), (z_lo, w_hi, False, False),
                                         (z_hi, w_lo, False, k == KD - 1)):
                        for buf, bank, lo in into:
                            x = pe.matmul(buf[:, bank, :], zz[:, k, lo:lo + P], ww[s][:, kk_ * 512:(kk_ + 1) * 512],
                                          start=a, stop=b)
                x.then_inc(used, 1)
            uses = [uses[0] + 1, uses[1]]

            n = UNITS["ogpin"]
            pe.wait_ge(vs["dve"], 1)
            with pe.Fori(0, 4) as j:
                pe.wait_ge(ps_free[0], uses[0] + 1 + j)
                unit(n + 2 * j, 0, 0)
                pe.wait_ge(ops["pin"], j + 1)
                unit(n + 2 * j + 1, 1, 1)
            uses = [uses[0] + 4, uses[1]]
            pe.wait_ge(ops["pin"], 5)

            for g in range(4):
                pe.wait_ge(pools["ready"], g + 1)
                pe.wait_ge(ps_free[g % 2], uses[g % 2] + 1)
                uses[g % 2] += 1
                for b in range(2):
                    x = pe.matmul(ps[g % 2][:, b, 0:HALF], pool_w[:, g, :],
                                  pin[:, g, PADC + b * HALF:PADC + (b + 1) * HALF], start=True, stop=True)
                x.then_inc(pools["sum"], 1)

            n = UNITS["gates"]
            base = list(uses)
            pe.wait_ge(vs["act"], 1)

            def head(h, j):
                def gate(i, k):
                    if k == 0:
                        pe.wait_ge(ps_free[i], base[i] + 1 + h)
                        pe.wait_ge(lo_done, n + 2 * h + i + 3)
                    for kq in (k, k + 1):
                        x = products(i, kq, 0, z_hi[:, kq, :], z_lo[:, kq, :], outs528(i), kq == 0, kq == KD - 1)
                    if k + 2 == KD:
                        x.then_inc(used, 1)

                def scores(tt, x):
                    if x is None:
                        lhs, rhs = kk, qf[:, 2 * h, :]
                    else:
                        lhs, rhs = x, x[:, :]
                    bank = ps[2][:, tt % 2, :]
                    if tt <= 4:
                        pe.matmul(ps[3][0:META, 1, tt * META:(tt + 1) * META], lhs[:, 0:META], rhs[:, 0:META],
                                  start=True, stop=True)
                    for c in range(CHUNKS):
                        lo = META + c * P
                        x_ = pe.matmul(bank[:, c * P:(c + 1) * P], lhs[:, lo:lo + P], rhs[:, lo:lo + P],
                                       start=True, stop=True)
                    x_.then_inc(mx["turn"], 1)

                def level(l):
                    pe.wait_ge(mx["mul_r"], h * LEVELS + l + 1)
                    pe.wait_ge(mx["mul_l"], h * LEVELS + l + 1)
                    scores(turn_of(l), X[l % 3])

                gate(0, 0)
                if j == 0:
                    pe.wait_ge(mx["o_read"], h + 1)
                pe.wait_ge(mx["k"], h + 1)
                pe.wait_ge(mx["score_read"], 9 * h + 1)
                scores(0, None)
                gate(0, 2)
                pe.wait_ge(mx["score_read"], 9 * h + 2)
                level(0)
                gate(0, 4)
                pe.wait_ge(mx["score_read"], 9 * h + 3)
                level(1)
                gate(0, 6)
                pe.wait_ge(mx["score_read"], 9 * h + 4)
                level(2)
                gate(1, 0)
                pe.wait_ge(mx["score_read"], 9 * h + 5)
                level(3)
                gate(1, 2)
                pe.wait_ge(mx["kd"], h + 1)
                pe.wait_ge(mx["score_read"], 9 * h + 6)
                pe.transpose(ps[2][0:META, 1, 0:P], kd[:, 0:META], ident)
                for c in range(1, 4):
                    x = pe.transpose(ps[2][:, 1, c * P:(c + 1) * P], kd[:, META + (c - 1) * P:META + c * P], ident)
                x.then_inc(mx["turn"], 1)
                gate(1, 4)
                pe.wait_ge(mx["kdt"], 2 * h + 2)
                pe.wait_ge(mx["vh"], 2 * h + 2)
                pe.wait_ge(mx["score_read"], 9 * h + 7)
                for c in range(4):
                    lhs = kdt[0:META, 0, :] if c == 0 else kdt[:, c, :]
                    rhs = vh0[:, :] if c == 0 else vh[:, c - 1, :]
                    x = pe.matmul(ps[2][:, 0, c * VD:(c + 1) * VD], lhs, rhs, start=True, stop=True)
                x.then_inc(mx["turn"], 1)
                gate(1, 6)
                level(4)
                pe.wait_ge(mx["score_read"], 9 * h + 8)
                level(5)
                pe.wait_ge(mx["score_read"], 9 * h + 9)
                level(6)
                pe.wait_ge(mx["meta"], 5 * h + 5)
                pe.wait_ge(mx["score_read"], 9 * h + 11)
                pe.wait_ge(mx["qe"], h + 1)
                rows = slice(j * VD, (j + 1) * VD)
                pe.matmul(ps[3][rows, 1, 96:96 + META], vh0[:, :], sc0[:, :], start=True, stop=True)
                for c in range(CHUNKS):
                    cs = slice(c * P, (c + 1) * P)
                    pe.matmul(ps[3][rows, 0, cs], vh[:, c, :], sc[:, cs], start=True, stop=False)
                    x = pe.matmul(ps[3][rows, 0, cs], st[:, c, :], qe[:, cs], start=False, stop=True)
                x.then_inc(mx["o"], 1)

            with pe.Fori(0, HEADS // 2) as p:
                head(2 * p, 0)
                head(2 * p + 1, 1)

            for p in range(4):
                pe.wait_ge(oas["sq"], p + 1)
                pe.wait_ge(ps_free[p % 2], FREED["oa"][p % 2] + 1 + p // 2)
                for b in range(2):
                    x = pe.matmul(ps[p % 2][:, b, 0:HALF], pair_ones, sq[p % 2][:, b * HALF:(b + 1) * HALF],
                                  start=True, stop=True)
                x.then_inc(oas["sum"], 1)

            n = UNITS["branch"]
            pe.wait_ge(ps_free[0], FREED["out"][0] + 1)
            pe.wait_ge(ps_free[1], FREED["out"][1] + 1)

            def branch_pair(i, first):
                for s in range(2):
                    m = 2 * i + s
                    pe.wait_ge(lo_done, n + m + 3)
                    pe.wait_ge(brs["mixed"], m + 1)
                    for k in (4, 5, 6, 7, 0, 1, 2, 3):
                        if first and s == 0:
                            if k >= 4:
                                pe.wait_ge(oas["pin_lo"], k - 3)
                            else:
                                pe.wait_ge(oas["lo"], k + 1)
                        x = products(s, k, 0, z_hi[:, k, :], z_lo[:, k, :], outs528(2 * s + k // 4),
                                     k % 4 == 0, k % 4 == 3)
                    x.then_inc(used, 1)
            branch_pair(0, True)
            with pe.Fori(0, 3) as i:
                branch_pair(i + 1, False)

            pe.wait_ge(brs["mixed"], 9)
            gemm("out", T1, 4, mix_hi, mix_lo, KD, lambda k: pe.wait_ge(brs["lo"], k + 3))

            def ffn(tag, tokens, s, norm, between=None):
                for b, half in enumerate("ab"):
                    gemm(f"up{tag}_{half}", tokens, FH, z_hi, z_lo, KD, None if b else z_tile(norm))
                    if b and between:
                        between()
                    gemm(f"down{tag}_{half}", tokens, 4, g_hi, g_lo, FH,
                         lambda k: pe.wait_ge(*s.at("lo", 2 + b * FH + k)))
            def memory_turned():
                pe.wait_ge(mem_step, 6)
                for k in range(KD):
                    for c in range(2):
                        x = pe.transpose(turned_memory(k)[:, c * P:(c + 1) * P], mem_rows[:, c, k * P:(k + 1) * P],
                                         ident)
                x.then_inc(mem_turned, 1)

            norm_sum(n2, T1)
            norm_spread(n2, T1)
            ffn("", T1, f1, n2, memory_turned)

            n, freed = UNITS["mem"], FREED["mem"]
            pe.wait_ge(mem_lo, KD)
            for l in range(2):
                for s in range(2):
                    pe.wait_ge(ps_free[s], freed[s] + 1 + (2 * l, l)[s])
                    pe.wait_ge(lo_done, n + 4 * l + s + 3)
                    for k in range(KD):
                        x = products(s, k, 0, mz_hi[:, k, :], mz_lo[:, k, :], [(ps[s][:, 0, 0:NMEM], 0, NMEM)],
                                     k == 0, k == KD - 1)
                    x.then_inc(used, 1)
                pe.wait_ge(ps_free[0], freed[0] + 2 + 2 * l)
                for s in range(2):
                    pe.wait_ge(lo_done, n + 4 * l + s + 5)
                    for kk_ in range(4):
                        k = 4 * s + kk_
                        for zz, ww, a, b in ((mz_hi, w_hi, k == 0, False), (mz_lo, w_hi, False, False),
                                             (mz_hi, w_lo, False, k == KD - 1)):
                            for c in range(2):
                                x = pe.matmul(ps[0][:, c, 0:NMEM], zz[:, k, c * P:(c + 1) * P],
                                              ww[s][:, kk_ * NMEM:(kk_ + 1) * NMEM], start=a, stop=b)
                    x.then_inc(used, 1)
                if l == 0:
                    norm_sum(fin, T1)
                    norm_spread(fin, T1)

            def layer(l):
                norm_sum(norm_a[l], SEQ)
                norm_spread(norm_a[l], SEQ)
                gemm(f"qk{l}", SEQ, (5, 7)[l], z_hi, z_lo, KD, z_tile(norm_a[l]))

                n, freed = UNITS[f"v{l}"], FREED[f"v{l}"]
                count, kt, width = ((2, 4, KVA * HD), (4, 2, 384))[l]
                for half in range((1, 2)[l]):
                    for i in range(count):
                        s, m = i % 2, n + count * half + i
                        if i == 0:
                            pe.wait_ge(ps_free[0], freed[0] + 1 + half)
                            pe.wait_ge(ps_free[1], freed[1] + 1 + half)
                        pe.wait_ge(lo_done, m + 3)
                        for kk_ in range(kt):
                            k = kt * i + kk_
                            for zz, ww, a, b in ((z_hi, w_hi, k == 0, False), (z_lo, w_hi, False, False),
                                                 (z_hi, w_lo, False, k == KD - 1)):
                                for c in range(4):
                                    x = pe.matmul(ps[c // 2][:, c % 2, 0:width], zz[:, k, c * P:(c + 1) * P],
                                                  ww[s][:, kk_ * width:(kk_ + 1) * width], start=a, stop=b)
                        x.then_inc(used, 1)

                s = atts[l]
                pe.wait_ge(ps_free[0], FREED[f"turn{l}"][0] + 1)
                pe.wait_ge(ps_free[1], FREED[f"turn{l}"][1] + 1)

                def scores(h, r, n_, b, kv):
                    memory = n_ >= QH
                    _, width = span(memory, b)
                    if memory:
                        q, keys = q_heads[:, n_, b * P:(b + 1) * P], mk[:, MH * l + n_ - QH, :]
                    else:
                        lo = key_block(False, b, 0) * P
                        q, keys = q_now[r][:, b * P:(b + 1) * P], k_heads[:, bass.ds(kv, 1), lo:lo + width]
                    pe.matmul(banks(r + b)[:, 0:width], q, keys, start=True, stop=True).then_inc(s["s"], 1)

                def turn(h, r, memory, b):
                    _, width = span(memory, b)
                    lo = span(memory, b)[0]
                    pe.wait_ge(*s.at("exp", 4 * h + (b + 1)))
                    pe.wait_ge(*s.at(("pa", "pd")[b % 2], 2 * h + b // 2))
                    for j in range(width // P):
                        x = pe.transpose(ps[3][:, b % 2, j * P:(j + 1) * P],
                                         ls[r][:, b, lo + j * P:lo + (j + 1) * P], ident)
                    x.then_inc(s["t"], 1)

                def values(h, r, memory, b, kv, n_):
                    _, width = span(memory, b)
                    if b == 0:
                        pe.wait_ge(*s.at("out", h - 2))
                    pe.wait_ge(*s.at(("pa", "pd")[b % 2], 2 * h + (b // 2 + 1)))
                    for j in range(width // P):
                        block = key_block(memory, b, j)
                        if memory:
                            v = mv[:, 2 * l + block, (n_ - QH) * HD:(n_ - QH + 1) * HD]
                        else:
                            v = v_tok[:, block, bass.ds(kv * HD, HD)]
                        x = pe.matmul(y_bank(r)[:, b * HD:(b + 1) * HD], pts[b % 2][:, j * P:(j + 1) * P], v,
                                      start=j == 0, stop=j == width // P - 1)
                    x.then_inc(s["y"], 1)

                def step(h, r, n_, g):
                    front, back = n_ < AH, 2 <= n_ < AH + 2
                    kv, back_kv, last_kv = (h, h - 2, h - 3) if l else (g, g - 1 if r < 2 else g, g - 1)
                    rb, memory = (r + 1) % 3, n_ - 2 >= QH
                    for b in range(4):
                        if front:
                            pe.wait_ge(*s.at("ls", 4 * h + (b - 2)))
                            if n_ < QH:
                                pe.wait_ge(*s.at("q", h + 1))
                        if back:
                            turn(h - 2, rb, memory, b)
                        if front:
                            scores(h, r, n_, b, kv)
                        if b == 0 and n_ >= 3:
                            values(h - 3, r, n_ - 3 >= QH, 3, last_kv, n_ - 3)
                        elif b and back:
                            values(h - 2, rb, memory, b - 1, back_kv, n_ - 2)

                head_steps(pe, step)

                pe.wait_ge(*s.at("out", AH))
                for k in range(KD):
                    pe.wait_ge(ps_free[k % 2], FREED[f"turn{l}"][k % 2] + 1 + k // 2)
                    for c in range(4):
                        x = pe.transpose(ps[k % 2][:, 0, c * P:(c + 1) * P], y_tok[:, c, k * P:(k + 1) * P], ident)
                    x.then_inc(s["turned"], 1)
                pe.wait_ge(ps_free[1], FREED[f"out{l}"][1] + 1)
                gemm(f"out{l}", SEQ, 4, z_hi, z_lo)
                norm_sum(norm_f[l], SEQ)
                norm_spread(norm_f[l], SEQ)
                ffn(str(l), SEQ, ffn2[l], norm_f[l])
            layer(0)
            layer(1)

            pe.wait_ge(ps_free[0], so_far[0] + 1)
            pe.wait_ge(ps_free[1], so_far[1] + 1)
            norm_sum(norm_o, SEQ)
            norm_spread(norm_o, SEQ)
            def out_turn(c, k):
                return pe.transpose(ps[c][:, k // 4, k % 4 * P:(k % 4 + 1) * P],
                                    H[:, k, META + c * P:META + (c + 1) * P], ident)
            for k in range(KD):
                pe.wait_ge(*norm_o.at("z", k + 1))
                for c in range(CHUNKS):
                    if c < 3 or k >= 4:
                        x = out_turn(c, k)
                if k == 3:
                    x.then_inc(out_turned, 1)
            for k in range(4):
                x = out_turn(3, k)
            x.then_inc(out_turned, 1)


def constants():
    import numpy as np

    cc = constant_columns()
    c = np.zeros((P, cc["all"]), np.float32)
    c[:, cc["ident"]:cc["ident"] + P] = np.eye(P)
    c[:, cc["ones"]:cc["ones"] + P] = 1
    c[:, cc["pair_ones"]:cc["pair_ones"] + P] = np.kron(np.eye(2), np.ones((VD, VD)))
    restart = np.ones(T1)
    restart[[0] + [META + P * i for i in range(CHUNKS)]] = 0
    c[:, cc["restart"]:cc["restart"] + T1] = restart
    counts = np.array([[1 / min(i + 1, w) for i in range(16)] for w in WINDOWS])
    c[:, cc["first_counts"]:cc["first_counts"] + 64] = counts.reshape(-1)
    c[:, cc["eps"]] = EPS
    c[:, cc["slopes"]:cc["slopes"] + QH] = -2.0 ** (-8.0 * np.arange(1, QH + 1) / QH)
    s, q = np.arange(P)[:, None], np.arange(P)[None, :]
    masks = np.zeros((P, LEVELS, P), np.float32)
    for l in range(LEVELS):
        h = 2 ** l
        masks[:, l] = (s // (2 * h) == q // (2 * h)) & (s % (2 * h) < h) & (q % (2 * h) >= h)
    return c, masks.reshape(P, -1)


def attention_constants():
    import numpy as np

    a = np.zeros((P, 3 * P + 3 * 48), np.float32)
    distance = np.abs(np.arange(P)[:, None] + P - np.arange(3 * P)[None, :])
    a[:, 0:3 * P] = np.where(distance <= P, distance, -1e3 * NEG)
    x = np.arange(48)[None, :]
    for v, b in enumerate((0, 1, 3)):
        column = BC * b + np.arange(P)[:, None] % BC
        start = np.clip(column - BC // 2, 0, GRID_C - BC)
        key = BC * (b - 1) + x
        a[:, 3 * P + 48 * v:3 * P + 48 * (v + 1)] = np.where((key >= start) & (key < start + BC), 0, NEG)
    return a


def laid_out(inputs):
    import numpy as np

    a = {k: np.asarray(v) for k, v in inputs.items()}
    pc = columns()
    par = np.zeros((P, pc["all"]), np.float32)

    def put(name, v):
        v = v.reshape(-1, P).T
        par[:, pc[name]:pc[name] + v.shape[1]] = v
    put("lb0", a["lb_logits"][0])
    put("lb1", a["lb_logits"][1])
    put("norm1", a["norm1_g"])
    put("b_f", a["b_f"])
    put("head_g", a["head_norm_g"])
    put("pool_scale", a["pool_scale"])
    put("norm2", a["norm2_g"])
    put("conv_w", a["conv_w"])
    put("conv_b", a["conv_b"])
    put("final_g", a["final_norm_g"])
    put("mix_g", a["norm_mix_2"])
    put("ffn_g", a["norm_ffn_2"])
    put("mem_g", a["norm_mem_2"])
    put("out_g", a["norm_final_2"])
    par[:, pc["sink"]:pc["sink"] + QH] = a["sink_a_2"][0][None]
    out = {k: a[k] for k in ("x", "meta_tokens", "w_in", "w_pool", "w_out", "w_up", "w_down")}
    out["w_branch"] = np.concatenate([a["w_branch_a"][0], a["w_branch_b"][0]])
    out["parameters"] = par
    out["constants"], out["level_masks"] = constants()
    for k in ("mem_2", "w_in_a_2", "w_in_b_2", "w_mem_kv_2", "w_out_2", "w_gate_up_2", "w_down_2"):
        out[k] = a[k]
    padded = np.pad(a["rpb_b_2"][0], ((0, 0), (0, 0), (BC, BC + 1)))
    out["rpb"] = np.stack([padded[:, :, BC - 1 - c:4 * BC - 1 - c] for c in range(BC)], axis=1)
    out["attention_constants"] = attention_constants()
    return {k: np.ascontiguousarray(v) for k, v in out.items()}


def kernel(**inputs):
    import concourse.bacc as bacc
    import numpy as np
    from concourse.bass_utils import run_bass_kernel_spmd

    arrays = laid_out(inputs)
    nc = bacc.Bacc("TRN2", target_bir_lowering=False, num_devices=1)
    t = {k: nc.dram_tensor(k, v.shape, mybir.dt.from_np(v.dtype), kind="ExternalInput").ap()
         for k, v in arrays.items()}
    t["out"] = nc.dram_tensor("out", (1, SEQ, D), F32, kind="ExternalOutput").ap()
    build(nc, t)
    return run_bass_kernel_spmd(nc, [arrays], core_ids=[0]).results[0]["out"]
```

```python
from contextlib import ExitStack

import concourse.bass as bass
from concourse import mybir
from concourse.alu_op_type import AluOpType as ALU

ACT = mybir.ActivationFunctionType
AX = mybir.AxisListType
F32 = mybir.dt.float32
F32R = mybir.dt.float32r
U8 = mybir.dt.uint8

P = 128
D = 1024
KD = D // P
SEQ = 512
META = 16
T1 = META + SEQ
HALF = T1 // 2
EPS = 1e-6

HEADS = D // P
VD = 64
WIDTH = D // 2
LEVELS = 7
CHUNKS = SEQ // P
PADC = 16
WINDOWS = (2, 4, 8, 16)
DFF = 2816
FT = DFF // P
FH = FT // 2

HD = 64
QH = 12
KVA = 4
MH = 4
AH = QH + MH
NMEM = 256
GRID_R, GRID_C = 8, 64
BC = GRID_C // 4
NEG = -1e30

SLOT = FH * P
UNIT = KD * P


def columns():
    at, n = {}, 0
    for name, width in (("lb0", 8), ("lb1", 8), ("norm1", 8), ("b_f", 8), ("head_g", 4), ("pool_scale", 4),
                        ("norm2", 8), ("conv_w", 3 * FT), ("conv_b", FT), ("final_g", 8), ("mix_g", 16),
                        ("ffn_g", 16), ("mem_g", 8), ("out_g", 8), ("sink", QH)):
        at[name] = n
        n += width
    at["all"] = n
    return at


def constant_columns():
    at, n = {}, 0
    for name, width in (("ident", P), ("ones", P), ("pair_ones", P), ("restart", T1), ("first_counts", 64),
                        ("eps", 1), ("slopes", QH)):
        at[name] = n
        n += width
    at["all"] = n
    return at


def build(nc, t):
    pc, cc = columns(), constant_columns()
    ctx = ExitStack()
    with ctx:
        def sem(name):
            return ctx.enter_context(nc.semaphore(name))

        fixed = [(nc.sbuf_usable_end - nc.sbuf_bytes_remaining + 31) // 32 * 32]

        def sb(at, name, shape, dt=F32):
            size = 1 if dt == U8 else 4
            for n in shape[1:]:
                size *= n
            x = nc.alloc_sbuf_tensor_at(name, shape, dt, offset=at[0])
            at[0] += (size + 31) // 32 * 32
            return x

        par = sb(fixed, "par", [P, pc["all"]])
        con = sb(fixed, "con", [P, cc["all"]])
        masks = sb(fixed, "masks", [P, LEVELS, P], U8)
        lbc = sb(fixed, "lbc", [P, 4, KD])
        stat = sb(fixed, "stat", [P, 6, 6])
        carrier = sb(fixed, "carrier", [P, 1])
        raw = [sb(fixed, f"raw{i}", [P, SLOT]) for i in range(2)]
        w_hi = [sb(fixed, f"w_hi{i}", [P, SLOT], F32R) for i in range(2)]
        w_lo = [sb(fixed, f"w_lo{i}", [P, SLOT], F32R) for i in range(2)]
        H = sb(fixed, "H", [P, KD, T1])
        z_hi = sb(fixed, "z_hi", [P, KD, T1], F32R)
        z_lo = sb(fixed, "z_lo", [P, KD, T1], F32R)
        region = fixed[0]

        at = [region]
        x_rows = sb(at, "x_rows", [P, CHUNKS, D])
        meta_rows = sb(at, "meta_rows", [META, D])
        at = [region]
        qf = sb(at, "qf", [P, 2 * HEADS, T1])
        gates = sb(at, "gates", [P, 2 * KD, T1])
        og = sb(at, "og", [P, 4, T1])
        pin = sb(at, "pin", [P, 4, PADC + T1])
        V = sb(at, "V", [P, CHUNKS, WIDTH])
        V0 = sb(at, "V0", [META, WIDTH])
        scratch = at[0]
        at = [scratch]
        sq = [sb(at, f"sq{i}", [P, T1]) for i in range(2)]
        acc = sb(at, "acc", [P, T1])
        rstd = sb(at, "rstd", [P, T1])
        sig = sb(at, "sig", [P, T1])
        z_now = [sq[0], sq[1], rstd, sig]
        mask_rows = nc.alloc_sbuf_tensor_at("mask_rows", [P, LEVELS * P], F32, offset=at[0])
        pool_a = sb(at, "pool_a", [P, PADC + T1])
        pool_b = sb(at, "pool_b", [P, PADC + T1])
        pool_w = sb(at, "pool_w", [P, 4, P])
        at = [scratch + 5 * 4 * T1]
        zt = [sb(at, f"zt{i}", [P, T1]) for i in range(2)]
        ta = sb(at, "ta", [P, T1])
        tb = sb(at, "tb", [P, T1])
        at = [region]
        mix_hi = sb(at, "mix_hi", [P, KD, T1], F32R)
        mix_lo = sb(at, "mix_lo", [P, KD, T1], F32R)
        at = [region]
        g_hi = sb(at, "g_hi", [P, FH, T1], F32R)
        g_lo = sb(at, "g_lo", [P, FH, T1], F32R)
        ub = sb(at, "ub", [P, 4 + SEQ])
        cv = [sb(at, f"cv{i}", [P, T1]) for i in range(3)]
        si = sb(at, "si", [P, T1])
        gv = sb(at, "gv", [P, T1])
        mem_rows = sb(at, "mem_rows", [P, 2, D])
        mem_square = sb(at, "mem_square", [P, D])
        mem_stat = sb(at, "mem_stat", [P, 3, 2])
        mz_hi = sb(at, "mz_hi", [P, KD, NMEM], F32R)
        mz_lo = sb(at, "mz_lo", [P, KD, NMEM], F32R)
        assert at[0] <= scratch
        at = [scratch + 5 * 4 * T1]
        mk = sb(at, "mk", [P, 2 * MH, NMEM])
        mv = sb(at, "mv", [P, 2 * 2, NMEM])
        att_con = sb(at, "att_con", [P, 3 * P + 3 * 48])
        row_max = [sb(at, f"row_max{i}", [P, 4]) for i in range(3)]
        neg_max = [sb(at, f"neg_max{i}", [P, 4]) for i in range(3)]
        row_sum = [sb(at, f"row_sum{i}", [P, 4]) for i in range(3)]
        sink_exp = [sb(at, f"sink_exp{i}", [P, 4]) for i in range(3)]
        rsum = [sb(at, f"rsum{i}", [P, 4]) for i in range(3)]
        rpb_last = sb(at, "rpb_raw2", [P, GRID_R, 48])
        at = [region]
        q_heads = sb(at, "q_heads", [P, QH + MH, SEQ])
        k_heads = sb(at, "k_heads", [P, QH, SEQ])
        v_tok = sb(at, "v_tok", [P, 4, QH * HD])
        y_tok = sb(at, "y_tok", [P, 4, D])
        q_now = [sb(at, "q_now0", [P, SEQ])]
        bias = [sb(at, "bias0", [P, GRID_R * (48 + 32 + 32)])]
        rpb_raw = [sb(at, f"rpb_raw{i}", [P, GRID_R, 48]) for i in range(2)] + [rpb_last]
        assert at[0] <= scratch
        at = [fixed[0] - 2 * 4 * KD * T1]
        ls = [sb(at, f"ls{i}", [P, 4, 3 * P]) for i in range(3)]
        bias += [sb(at, f"bias{i}", [P, GRID_R * (48 + 32 + 32)]) for i in range(1, 3)]
        q_now += [sb(at, f"q_now{i}", [P, SEQ]) for i in range(1, 3)]
        pts = [sb(at, f"pts{i}", [P, 3 * P]) for i in range(2)]
        assert at[0] <= fixed[0]
        at = [region]
        out_rows = sb(at, "out_rows", [P, CHUNKS, D])
        at = [scratch]
        lf = sb(at, "lf", [P, T1])
        kk = sb(at, "kk", [P, T1])
        A = sb(at, "A", [P, T1])
        qe = sb(at, "qe", [P, SEQ])
        kd = sb(at, "kd", [P, META + 3 * P])
        X = [sb(at, f"X{i}", [P, T1]) for i in range(3)]
        kdt = sb(at, "kdt", [P, 4, P])
        sc = sb(at, "sc", [P, SEQ])
        sc0 = sb(at, "sc0", [META, META])
        st = sb(at, "st", [P, 4, VD])
        dec = sb(at, "dec", [P, 4])
        vh = sb(at, "vh", [P, CHUNKS, VD])
        vh0 = sb(at, "vh0", [META, VD])
        spare = sb(at, "spare", [P, 1])

        ps = [ctx.enter_context(nc.psum_tensor(f"ps{i}", [P, 2, 512], F32)) for i in range(4)]

        def out528(i):
            return ps[i][:, :, 0:HALF]

        def two(x):
            return x.rearrange("p (b n) -> p b n", b=2)

        ident = con[:, cc["ident"]:cc["ident"] + P]
        ones = con[:, cc["ones"]:cc["ones"] + P]
        pair_ones = con[:, cc["pair_ones"]:cc["pair_ones"] + P]
        restart = con[:, cc["restart"]:cc["restart"] + T1]
        eps = con[:, cc["eps"]:cc["eps"] + 1]

        def vec(name, i=0):
            return par[:, bass.ds(pc[name] + i, 1)]

        def halves(x, l):
            h = 2 ** l
            lo = 0 if l <= 3 else META
            v = x[:, lo:T1].rearrange("p (n s h) -> p n s h", s=2, h=h)
            return v[:, :, 0, :], v[:, :, 1, :], v[:, :, 0, h - 1:h].to_broadcast([P, (T1 - lo) // (2 * h), h])

        def right_halves(x, l):
            return x.rearrange("p (n s h) -> p n s h", s=2, h=2 ** l)[:, :, 1, :]

        def chunked(x, n):
            return x.rearrange("p (c t) -> p c t", c=n)

        x_loaded, const_loaded, late_loaded = [sem("x_loaded0"), sem("x_loaded1")], sem("const_loaded"), sem("late")
        w_loaded = [sem("w_loaded0"), sem("w_loaded1")]
        hi_done = sem("hi_done")
        lo_done = sem("lo_done")
        used = sem("used")
        ps_free = [sem(f"ps_free{i}") for i in range(2)]
        x_turned, meta_turned = sem("x_turned"), sem("meta_turned")
        x_copied, x_copied_odd = sem("x_copied"), sem("x_copied_odd")
        lb_step = sem("lb_step")

        def stage(prefix, *names):
            return {n: sem(f"{prefix}_{n}") for n in names}

        qs = stage("qf", "sig")
        og_sig = sem("og_sig")
        vs = stage("v", "act", "dve")
        pools = stage("pool", "step", "ready", "sum")
        mx = stage("mx", "ln", "scan", "sub", "exp", "mul_r", "mul_l", "k", "kd_sub", "kd_exp", "kd", "qe_exp",
                   "qe", "turn", "score_read", "kdt", "meta", "states", "vh", "o", "o_read")
        oas = stage("oa", "sq", "inv", "scaled", "z", "hi", "lo", "pin_lo", "sum")
        brs = stage("br", "sig", "a", "mixed", "hi", "lo")

        class Round:

            def __init__(self, sems, base):
                self.sems, self.base = sems, base

            def __getitem__(self, name):
                return self.sems[name]

            def at(self, name, count):
                return self.sems[name], count + self.base[name]

        def rounds(prefix, *counts, start={}):
            sems = stage(prefix, *counts[0])
            base, out = {n: start.get(n, 0) for n in sems}, []
            for c in counts:
                out.append(Round(sems, dict(base)))
                for n in sems:
                    base[n] += c[n]
            return out

        norm_counts = {"sq": KD, "acc": KD + 1, "sum": 1, "root": 1, "inv": 6, "wide": 1, "z": KD, "hi": KD,
                       "even": KD // 2, "odd": KD // 2}
        plain = {**norm_counts, "hi": 0, "even": 0, "odd": 0}
        n1, n2, fin, norm_a0, norm_f0, norm_a1, norm_f1, norm_o = rounds(
            "norm", norm_counts, norm_counts, plain, *[norm_counts] * 4, plain)
        norm_a, norm_f = (norm_a0, norm_a1), (norm_f0, norm_f1)
        ffn_counts = {"conv": 6 * FH, "sig": 2 * FH, "si": 2 * FH, "hi": 2 * FH, "lo": 2 * FH}
        f1, *ffn2 = rounds("ffn", ffn_counts, {**ffn_counts, "conv": 0, "si": 0}, {**ffn_counts, "conv": 0, "si": 0})
        masks_ready = sem("masks_ready")
        mem_loaded, mem_step, mem_turned = sem("mem_loaded"), sem("mem_step"), sem("mem_turned")
        mem_hi, mem_lo = sem("mem_hi"), sem("mem_lo")
        att_counts = {"q": QH, "s": 4 * AH, "ls": 4 * AH, "max": 4 * MH, "neg": AH, "exp": 4 * AH, "t": 4 * AH,
                      "pa": 3 * AH, "pd": AH, "y": 4 * AH, "sum": QH, "inv": AH, "out": AH, "bias": QH,
                      "turned": KD, "hi": KD}
        ATT_START = {"s": 12, "ls": 12, "t": 12, "pa": 1, "pd": 1, "y": 2, "out": 3, "bias": 3}
        atts = rounds("att", att_counts, {**att_counts, "sum": 0}, start=ATT_START)
        rpb_loaded = [sem(f"rpb_loaded{i}") for i in range(3)]
        att_loaded, out_turned, out_copied, out_sent = (sem("att_loaded"), sem("out_turned"), sem("out_copied"),
                                                        sem("out_sent"))

        STREAM = [("qf", 16, UNIT), ("v", 4, UNIT), ("pinog", 8, UNIT), ("gates", 16, UNIT), ("branch", 8, UNIT),
                  ("out", 8, UNIT)]
        for half in "ab":
            STREAM += [(f"up_{half}", 2 * FH, UNIT), (f"down_{half}", 8, SLOT)]
        STREAM += [("mem", 8, UNIT)]
        for l in range(2):
            STREAM += [(f"qk{l}", (10, 14)[l], UNIT), (f"v{l}", (2, 8)[l], (UNIT, 2 * 384)[l]),
                       (f"out{l}", 8, UNIT)]
            for half in "ab":
                STREAM += [(f"up{l}_{half}", 2 * FH, UNIT), (f"down{l}_{half}", 8, SLOT)]
        UNITS, WIDTHS = {}, []
        for name, count, width in STREAM:
            UNITS[name] = len(WIDTHS)
            WIDTHS += [width] * count
        FREED, so_far = {}, (0, 0)
        for name, a, b in ([("qf", 8, 8), ("v", 1, 0), ("pinog", 4, 4), ("pool", 2, 2), ("gates", 8, 8), ("oa", 2, 2),
                            ("out", 4, 4)] + [(f"{w}_{h}", c, c) for h in "ab" for w, c in (("up", FH), ("down", 4))]
                           + [("mem", 4, 2)]
                           + [x for l in range(2) for x in
                              [(f"qk{l}", (5, 7)[l], (5, 7)[l]), (f"v{l}", (1, 2)[l], (1, 2)[l]),
                               (f"turn{l}", 4, 4), (f"out{l}", 4, 4)]
                              + [(f"{w}{l}_{h}", c, c) for h in "ab" for w, c in (("up", FH), ("down", 4))]]):
            FREED[name] = so_far
            so_far = (so_far[0] + a, so_far[1] + b)

        POOLED = tuple(1 + x for x in FREED["gates"])

        def psv(tokens, i):
            return ps[i][:, :, 0:HALF] if tokens == T1 else ps[i][:, 0, 0:tokens]

        def shaped(tokens, x):
            return two(x[:, 0:T1]) if tokens == T1 else x[:, 0:tokens]

        def natural(x):
            return x.rearrange("p (r b c) -> p b r c", r=GRID_R, b=4)

        def blocked(x):
            return x.rearrange("p (b r c) -> p b r c", r=GRID_R, b=4)

        def banks(i):
            return (ps[1][:, 1, :], ps[2][:, 0, :], ps[2][:, 1, :])[i % 3]

        def turned_memory(k):
            return ps[2 + k % 4 // 2][:, k % 2, k // 4 * NMEM:(k // 4 + 1) * NMEM]

        def y_bank(r):
            return (ps[0][:, 0, :], ps[0][:, 1, :], ps[1][:, 0, :])[r][:, 0:4 * HD]

        def span(memory, b):
            return (0, NMEM) if memory else ((P, 2 * P), (0, 3 * P), (0, 3 * P), (0, 2 * P))[b]

        def key_block(memory, b, j):
            return j if memory else max(b - 1, 0) + j

        def head_steps(eng, step):
            for h in range(3):
                step(h, h, h, 0)
            with eng.Fori(0, QH // 3 - 1) as g:
                for r in range(3):
                    step(3 * g + (3 + r), r, 3, g + 1)
            for h in range(QH, AH + 3):
                step(h, h % 3, h, h // 3)

        def pieces(tokens):
            return (6, T1 // 6) if tokens == T1 else (4, P)

        CONV = SEQ + 4

        def conv_outs(s):
            if s == 0:
                return [(ps[0][:, b, 0:CONV // 2], T1 - CONV + b * CONV // 2, CONV // 2) for b in range(2)]
            return [(ps[1][:, 0, 0:SEQ], META, SEQ)]

        def h_tile(tokens, k):
            return H[:, k, :] if tokens == T1 else H[:, k, META:]

        def peeled(eng, count, body, this, after):
            if this == after:
                with eng.Fori(0, count) as i:
                    body(i, this)
            else:
                with eng.Fori(0, count - 1) as i:
                    body(i, this)
                body(count - 1, after)

        def after(name, count):
            n = UNITS[name] + count
            return WIDTHS[n] if n < len(WIDTHS) else None

        block = ctx.enter_context(nc.Block())

        def cols(w, c0, kt=KD, k0=0, width=P):
            return w[k0 * P:(k0 + kt) * P, bass.ds(c0, width)].rearrange("(k p) c -> p k c", p=P)

        def turn_of(level):
            return level + 1 if level <= 3 else level + 3

        @block.sync
        def _(sp):
            for c in range(CHUNKS):
                if c == 0:
                    sp.dma_start(con[:, :], t["constants"]).then_inc(const_loaded, 16)
                    sp.dma_start(par[:, :], t["parameters"]).then_inc(const_loaded, 16)
                    sp.dma_start(meta_rows[:, :], t["meta_tokens"]).then_inc(x_loaded[0], 16)
                sp.dma_start(x_rows[:, c, :], t["x"][0, c * P:(c + 1) * P, :]).then_inc(x_loaded[c // 2], 16)

            def load(n, s, src, kt=KD, width=P):
                sp.wait_ge(lo_done, n + 1)
                sp.dma_start(raw[s][:, 0:kt * width].rearrange("p (k c) -> p k c", k=kt), src)\
                  .then_inc(w_loaded[s], 16)

            w_in = t["w_in"][0]
            with sp.Fori(0, HEADS) as h:
                n = UNITS["qf"] + 2 * h
                load(n, 0, cols(w_in, h * P))
                load(n + 1, 1, cols(w_in, h * P + D))
            sp.dma_start(mask_rows[:, :], t["level_masks"]).then_inc(late_loaded, 16)
            sp.dma_start(pool_w[:, :, :], t["w_pool"][0].rearrange("g c d -> c g d")).then_inc(late_loaded, 16)
            for i in range(4):
                load(UNITS["v"] + i, i % 2, cols(w_in, 2 * D, 2, 2 * i, 512), 2, 512)
            for first, c0 in ((0, 2 * D + 2 * WIDTH), (4, 2 * D + WIDTH)):
                with sp.Fori(0, 2) as i:
                    n = UNITS["pinog"] + first + 2 * i
                    load(n, 0, cols(w_in, i * (2 * P) + c0))
                    load(n + 1, 1, cols(w_in, i * (2 * P) + (c0 + P)))
            with sp.Fori(0, HEADS) as h:
                n = UNITS["gates"] + 2 * h
                load(n, 0, cols(w_in, h * P + 2 * D + 3 * WIDTH))
                load(n + 1, 1, cols(w_in, h * P + 3 * D + 3 * WIDTH))
            w_branch = t["w_branch"]
            for name, w in (("branch", w_branch), ("out", t["w_out"][0])):
                with sp.Fori(0, 4) as i:
                    n = UNITS[name] + 2 * i
                    load(n, 0, cols(w, i * (2 * P)))
                    load(n + 1, 1, cols(w, i * (2 * P) + P))

            def ffn(tag, w_up, w_down):
                for b, half in enumerate("ab"):
                    if tag == "" and b == 0:
                        sp.dma_start(mem_rows[:, :, :], t["mem_2"][0].rearrange("(c p) d -> p c d", p=P))\
                          .then_inc(mem_loaded, 16)
                        sp.dma_start(att_con[:, :], t["attention_constants"]).then_inc(att_loaded, 16)
                    with sp.Fori(0, FH) as j:
                        n = UNITS[f"up{tag}_{half}"] + 2 * j
                        load(n, 0, cols(w_up, j * P + b * FH * P))
                        load(n + 1, 1, cols(w_up, j * P + (DFF + b * FH * P)))
                    with sp.Fori(0, 4) as i:
                        n = UNITS[f"down{tag}_{half}"] + 2 * i
                        load(n, 0, cols(w_down, i * (2 * P), FH, b * FH), FH)
                        load(n + 1, 1, cols(w_down, i * (2 * P) + P, FH, b * FH), FH)
            ffn("", t["w_up"][0], t["w_down"][0])

            n = UNITS["mem"]
            for l in range(2):
                w = t["w_mem_kv_2"][l]
                for s in range(2):
                    load(n + 4 * l + s, s, cols(w, s * P))
                for s in range(2):
                    load(n + 4 * l + 2 + s, s, cols(w, MH * HD, 4, 4 * s, MH * HD), 4, MH * HD)

            def bias_load(h, r):
                sp.wait_ge(*atts[1].at("bias", h - 2))
                for rq in range(GRID_R):
                    rows = slice(GRID_R - 1 - rq, 2 * GRID_R - 1 - rq)
                    sp.dma_start(rpb_raw[r][rq * BC:(rq + 1) * BC, :, :],
                                 t["rpb"][bass.ds(h, 1), :, rows, :].rearrange("o c r x -> (o c) r x"))\
                      .then_inc(rpb_loaded[r], 16)

            for l in range(2):
                if l == 1:
                    for r in range(3):
                        bias_load(r, r)
                w = (t["w_in_a_2"], t["w_in_b_2"])[l][0]
                qkw = (QH + (KVA, QH)[l]) * HD
                vw = (KVA, QH)[l] * HD
                n = UNITS[f"qk{l}"]
                with sp.Fori(0, qkw // (2 * P)) as i:
                    load(n + 2 * i, 0, cols(w, i * (2 * P)))
                    load(n + 2 * i + 1, 1, cols(w, i * (2 * P) + P))
                for s in range(2):
                    load(n + qkw // P + s, s, cols(w, qkw + vw + s * P))
                n, kt, width = UNITS[f"v{l}"], (4, 2)[l], (KVA * HD, 384)[l]
                for i in range((2, 8)[l]):
                    load(n + i, i % 2, cols(w, qkw + width * (i * kt // KD), kt, i * kt % KD, width), kt, width)
                w_out, n = t["w_out_2"][l], UNITS[f"out{l}"]
                load(n, 0, cols(w_out, 0))
                load(n + 1, 1, cols(w_out, P))
                if l == 1:
                    with sp.Fori(0, QH // 3 - 1) as g:
                        for r in range(3):
                            bias_load(3 * g + (3 + r), r)
                with sp.Fori(0, 3) as i:
                    load(n + 2 * i + 2, 0, cols(w_out, i * (2 * P) + 2 * P))
                    load(n + 2 * i + 3, 1, cols(w_out, i * (2 * P) + 3 * P))
                ffn(str(l), t["w_gate_up_2"][l], t["w_down_2"][l])

            for c in range(CHUNKS):
                sp.wait_ge(out_copied, c + 1)
                sp.dma_start(t["out"][0, c * P:(c + 1) * P, :], out_rows[:, c, :]).then_inc(out_sent, 16)
            sp.wait_ge(out_sent, 16 * CHUNKS)

        @block.gpsimd
        def _(pool):
            for s, count in ((lo_done, 2), (used, 2), (ps_free[0], 1), (ps_free[1], 1), (mx["scan"], 1),
                             (mx["turn"], 1), (mx["score_read"], 2), (mx["o"], 1), (mx["o_read"], 1),
                             (brs["mixed"], 2), (brs["lo"], 2), (f1["lo"], 1)):
                pool.nop().then_inc(s, count)
            for name, count in ATT_START.items():
                pool.nop().then_inc(atts[0][name], count)

            def norm_odd(s, tokens, order=None):
                for k in range(1, KD, 2):
                    pool.wait_ge(*s.at("hi", k + 1))
                    lo, z, hi = z_lo[:, k, 0:tokens], z_now[k % 4][:, 0:tokens], z_hi[:, k, 0:tokens].bitcast(F32)
                    if order:
                        lo, z, hi = blocked(lo), natural(z), blocked(hi)
                    pool.tensor_tensor(lo, z, hi, ALU.subtract).then_inc(s["odd"], 1)
            norm_odd(n1, T1)

            pool.memset(pin[:, :, 0:PADC], 0.0).then_inc(pools["step"], 1)
            pool.wait_ge(masks_ready, 1)
            pool.memset(pool_a[:, :], 0.0).then_inc(pools["step"], 1)
            pool.memset(pool_b[:, :], 0.0).then_inc(pools["step"], 1)
            steps = 3
            for g, w in enumerate(WINDOWS):
                pool.wait_ge(ps_free[g % 2], FREED["pinog"][g % 2] + 2 + g // 2)
                src, lag = pin[:, g, :], 1
                for r in range(g + 1):
                    dst = (pool_a, pool_b)[r % 2]
                    pool.wait_ge(pools["step"], steps)
                    pool.tensor_tensor(dst[:, lag:], src[:, lag:], src[:, 0:PADC + T1 - lag], ALU.add)\
                        .then_inc(pools["step"], 1)
                    steps += 1
                    src, lag = dst[:, :], 2 * lag
                pool.wait_ge(pools["step"], steps)
                c0 = cc["first_counts"] + 16 * g
                pool.tensor_tensor(src[:, PADC:PADC + 16], src[:, PADC:PADC + 16], con[:, c0:c0 + 16], ALU.mult)\
                    .then_inc(pools["step"], 1)
                pool.tensor_scalar(src[:, PADC + 16:], src[:, PADC + 16:], 1.0 / w, 1.0, ALU.mult, ALU.mult)\
                    .then_inc(pools["step"], 1)
                steps += 2
                pool.wait_ge(pools["step"], steps)
                pool.tensor_tensor(pin[:, g, PADC:], src[:, PADC:], pin[:, g, PADC:], ALU.subtract)\
                    .then_inc(pools["ready"], 1)
                pool.wait_ge(pools["ready"], g + 1)

            def head(h):
                pool.wait_ge(mx["o"], h + 1)
                pool.tensor_copy(vh[:, :, :], V[:, :, bass.ds(h * VD, VD)]).then_inc(mx["vh"], 1)
                pool.tensor_copy(vh0[:, :], V0[:, bass.ds(h * VD, VD)]).then_inc(mx["vh"], 1)
                pool.wait_ge(mx["k"], h + 1)
                for l in range(LEVELS):
                    left, _, _ = halves(X[l % 3][:, :], l)
                    kleft, _, _ = halves(kk[:, :], l)
                    pool.wait_ge(mx["exp"], h * LEVELS + l + 1)
                    pool.tensor_tensor(left, left, kleft, ALU.mult).then_inc(mx["mul_l"], 1)
                    if l == 1:
                        pool.wait_ge(mx["kd_exp"], h + 1)
                        pool.tensor_tensor(kd[:, :], kd[:, :], kk[:, 0:META + 3 * P], ALU.mult)\
                            .then_inc(mx["kd"], 1)

            pool.wait_ge(ps_free[0], POOLED[0])
            pool.wait_ge(ps_free[1], POOLED[1])
            pool.wait_ge(vs["act"], 1)
            pool.wait_ge(vs["dve"], 1)
            with pool.Fori(0, HEADS // 2) as p:
                for j in range(2):
                    head(2 * p + j)

            def low(src, hi, lo, done):
                pool.tensor_tensor(lo, src, hi.bitcast(F32), ALU.subtract).then_inc(done, 1)

            for p in range(4):
                pool.wait_ge(oas["hi"], p + 5)
                low(zt[p % 2][:, :], z_hi[:, p, :], z_lo[:, p, :], oas["lo"])
            with pool.Fori(0, 4) as i:
                for s in range(2):
                    m = 2 * i + s
                    pool.wait_ge(brs["hi"], m + 1)
                    low(zt[s][:, :], mix_hi[:, m, :], mix_lo[:, m, :], brs["lo"])
            norm_odd(n2, T1)

            def ffn_low(s, tokens):
                for b in range(2):
                    def body(j):
                        pool.wait_ge(*s.at("hi", b * FH + j + 1))
                        low(gv[:, 0:tokens], g_hi[:, j, 0:tokens], g_lo[:, j, 0:tokens], s["lo"])
                    with pool.Fori(0, FH) as j:
                        body(j)
            ffn_low(f1, SEQ)

            for l in range(2):
                norm_odd(norm_a[l], SEQ, l)
                s = atts[l]
                pool.wait_ge(att_loaded, 16)

                def queries(h, r):
                    pool.wait_ge(*s.at("s", 4 * h - 8))
                    pool.tensor_copy(q_now[r][0:HD, :].rearrange("p (o n) -> p o n", o=1),
                                     q_heads[0:HD, bass.ds(h, 1), :]).then_inc(s["q"], 1)

                def biases(h, g, r):
                    if l == 0:
                        pool.wait_ge(*s.at("ls", 4 * h - 8))
                        pool.tensor_tensor(bias[r][:, 0:3 * P], att_con[:, 0:3 * P],
                                           con[:, bass.ds(cc["slopes"] + h, 1)].to_broadcast([P, 3 * P]),
                                           ALU.mult).then_inc(s["bias"], 1)
                    else:
                        pool.wait_ge(rpb_loaded[r], 128 * g + 128)
                        pool.wait_ge(*s.at("ls", 4 * h - 8))
                        at_ = 0
                        for v, (first, n) in enumerate(((1, 2), (0, 3), (0, 2))):
                            x0 = first * BC
                            mask = att_con[:, 3 * P + 48 * v + x0:3 * P + 48 * v + x0 + n * BC]
                            x = pool.tensor_tensor(
                                bias[r][:, at_:at_ + n * P].rearrange("p (n r c) -> p n r c", n=n, r=GRID_R),
                                rpb_raw[r][:, :, x0:x0 + n * BC].rearrange("p r (n c) -> p n r c", n=n),
                                mask.rearrange("p (n o c) -> p n o c", n=n, o=1)
                                    .to_broadcast([P, n, GRID_R, BC]), ALU.add)
                            at_ += n * P
                        x.then_inc(s["bias"], 1)
                biases(0, 0, 0)
                pool.wait_ge(used, UNITS[f"v{l}"] + 2)
                pool.wait_ge(ps_free[0], FREED[f"v{l}"][0] + 1)
                pool.wait_ge(ps_free[1], FREED[f"v{l}"][1] + 1)
                queries(0, 0)
                pool.wait_ge(used, UNITS[f"out{l}"] + 2)
                for h in (1, 2):
                    queries(h, h)
                    biases(h, 0, h)
                with pool.Fori(0, QH // 3 - 1) as g:
                    for r in range(3):
                        queries(3 * g + (3 + r), r)
                        biases(3 * g + (3 + r), g + 1, r)
                norm_odd(norm_f[l], SEQ)
                ffn_low(ffn2[l], SEQ)

        @block.scalar
        def _(act):
            def split_hi(n, s, width=UNIT):
                act.wait_ge(w_loaded[s], (n - s) * 8 + 16)
                act.wait_ge(used, n + 1)
                act.activation(w_hi[s][:, 0:width], raw[s][:, 0:width], ACT.Copy).then_inc(hi_done, 1)

            act.wait_ge(const_loaded, 32)
            act.wait_ge(lb_step, 3)
            act.activation(lbc[:, 2:4, :], lbc[:, 0:2, :], ACT.Exp).then_inc(lb_step, 1)
            for k in range(0, KD, 2):
                act.wait_ge(x_turned, k + 1)
                act.activation(H[:, k, META:], ps[k // 2][:, k % 2, :], ACT.Copy).then_inc(x_copied, 1)
            act.wait_ge(meta_turned, 1)
            act.activation(H[:, :, 0:META], ps[2][:, 0, 0:KD * META].rearrange("p (k t) -> p k t", k=KD), ACT.Copy)\
               .then_inc(x_copied, 1)

            def squares(s, tokens, x):
                for k in range(KD):
                    if k >= 2:
                        act.wait_ge(*s.at("acc", k))
                    act.activation(sq[k % 2][:, 0:tokens], x(k), ACT.Square).then_inc(s["sq"], 1)

            def norm_act(s, tokens):
                n, width = pieces(tokens)
                act.wait_ge(*s.at("inv", 1))
                act.activation(stat[0:width, 1, 0:n], stat[0:width, 0, 0:n], ACT.Sqrt).then_inc(s["root"], 1)

            def norm_hi(s, tokens, order=None):
                for k in range(KD):
                    hi, z = z_hi[:, k, 0:tokens], z_now[k % 4][:, 0:tokens]
                    if order:
                        hi, z = blocked(hi), natural(z)
                    act.wait_ge(*s.at("z", k + 1))
                    act.activation(hi, z, ACT.Copy).then_inc(s["hi"], 1)

            act.wait_ge(x_copied, 5)
            act.wait_ge(x_copied_odd, 4)
            squares(n1, T1, lambda k: H[:, k, :])
            split_hi(0, 0)
            norm_act(n1, T1)
            split_hi(1, 1)
            norm_hi(n1, T1)

            n = UNITS["qf"]

            def qf_step(h):
                split_hi(n + 2 * h + 2, 0)
                act.wait_ge(used, n + 2 * h + 3)
                act.activation(two(sig[:, :]), out528(0), ACT.Sigmoid).then_inc(qs["sig"], 1)
                split_hi(n + 2 * h + 3, 1)
                act.wait_ge(used, n + 2 * h + 4)
                act.activation(two(qf[:, 2 * h + 1, :]), out528(1), ACT.Sigmoid, bias=vec("b_f", h))\
                   .then_inc(ps_free[1], 1)
            with act.Fori(0, HEADS) as h:
                qf_step(h)

            n = UNITS["v"]
            split_hi(n + 2, 0)
            split_hi(n + 3, 1)
            split_hi(n + 4, 0)
            act.wait_ge(used, n + 6)
            act.activation(V[:, 0:2, :], ps[0][:, :, :], ACT.Copy).then_inc(ps_free[0], 1)
            act.activation(V0[:, :], ps[2][0:META, 0, :], ACT.Copy).then_inc(vs["act"], 1)
            split_hi(n + 5, 1)

            n = UNITS["pinog"]
            with act.Fori(0, 2) as i:
                for s in range(2):
                    split_hi(n + 2 * i + s + 2, s)
                    act.wait_ge(used, n + 2 * i + s + 3)
                    act.activation(two(pin[:, 2 * i + s, PADC:]), out528(s), ACT.Copy).then_inc(ps_free[s], 1)
            with act.Fori(0, 2) as i:
                for s in range(2):
                    split_hi(n + 2 * i + s + 6, s)
                    act.wait_ge(used, n + 2 * i + s + 7)
                    act.activation(two((sig, rstd)[s][:, :]), out528(s), ACT.Sigmoid).then_inc(og_sig, 1)
            for g in range(4):
                act.wait_ge(pools["sum"], g + 1)
                act.activation(two(pin[:, g, PADC:]), out528(g % 2), ACT.Identity, scale=vec("pool_scale", g))\
                   .then_inc(ps_free[g % 2], 1)
            act.wait_ge(lb_step, 9)

            n = UNITS["gates"]

            def logarithms(h):
                act.wait_ge(mx["scan"], h + 1)
                act.activation(lf[:, :], qf[:, 2 * h + 1, :], ACT.Ln, scale=lbc[:, 1, bass.ds(h, 1)],
                               bias=lbc[:, 0, bass.ds(h, 1)]).then_inc(mx["ln"], 1)

            def head(h, last):
                def expo(l):
                    lo = 0 if l <= 3 else META
                    act.wait_ge(mx["sub"], h * LEVELS + l + 1)
                    act.activation(X[l % 3][:, lo:], X[l % 3][:, lo:], ACT.Exp).then_inc(mx["exp"], 1)
                expo(0)
                expo(1)
                act.wait_ge(mx["o"], h + 1)
                act.activation(qe[:, :], A[:, META:], ACT.Exp).then_inc(mx["qe_exp"], 1)
                act.activation(dec[:, 0:3], A[:, META + P - 1:META + 3 * P:P], ACT.Exp).then_inc(mx["qe_exp"], 1)
                act.wait_ge(mx["kd_sub"], 2 * h + 2)
                act.activation(kd[:, :], kd[:, :], ACT.Exp).then_inc(mx["kd_exp"], 1)
                expo(2)
                expo(3)
                split_hi(n + 2 * h + 2, 0)
                act.wait_ge(used, n + 2 * h + 3)
                act.activation(two(gates[:, h, :]), out528(0), ACT.Copy).then_inc(ps_free[0], 1)
                expo(4)
                act.wait_ge(mx["turn"], 10 * h + 7)
                act.activation(kdt[0:META, 0, :], ps[2][0:META, 1, 0:P], ACT.Copy).then_inc(mx["kdt"], 1)
                act.activation(kdt[:, 1:, :], chunked(ps[2][:, 1, P:], 3), ACT.Copy).then_inc(mx["kdt"], 1)
                expo(5)
                if not last:
                    logarithms(h + 1)
                expo(6)
                split_hi(n + 2 * h + 3, 1)
                act.wait_ge(used, n + 2 * h + 4)
                act.activation(two(gates[:, HEADS + h, :]), out528(1), ACT.Copy).then_inc(ps_free[1], 1)

            def pair(p, last):
                head(2 * p, False)
                head(2 * p + 1, last)
                act.wait_ge(mx["o"], 2 * p + 3)
                act.activation(qf[:, 4 * p, META:], ps[3][:, 0, :], ACT.Copy).then_inc(mx["o_read"], 1)
                act.activation(qf[:, 4 * p, 0:META], ps[3][:, 1, 96:96 + META], ACT.Copy).then_inc(mx["o_read"], 1)
            act.preload_act_table_set("natural_log_exp_and_others")
            logarithms(0)
            with act.Fori(0, HEADS // 2 - 1) as p:
                pair(p, False)
            pair(HEADS // 2 - 1, True)

            act.wait_ge(used, UNITS["gates"] + 18)
            for g in range(4):
                act.activation(z_hi[:, 4 + g, :], pin[:, g, PADC:], ACT.Copy).then_inc(oas["hi"], 1)
            act.wait_ge(mx["o_read"], 9)
            for p in range(4):
                if p >= 2:
                    act.wait_ge(oas["sum"], p - 1)
                act.activation(sq[p % 2][:, :], qf[:, 4 * p, :], ACT.Square).then_inc(oas["sq"], 1)
            for p in range(4):
                act.wait_ge(oas["sum"], p + 1)
                if p >= 2:
                    act.wait_ge(oas["scaled"], p - 1)
                inverse = (rstd, sig)[p % 2]
                act.activation(two(inverse[:, :]), out528(p % 2), ACT.Ln, scale=1.0 / VD, bias=eps)\
                   .then_inc(ps_free[p % 2], 1)
                act.wait_ge(ps_free[p % 2], FREED["oa"][p % 2] + 2 + p // 2)
                act.activation(inverse[:, :], inverse[:, :], ACT.Exp, scale=-0.5).then_inc(oas["inv"], 1)
            for p in range(4):
                act.wait_ge(oas["z"], p + 1)
                act.activation(z_hi[:, p, :], zt[p % 2][:, :], ACT.Copy).then_inc(oas["hi"], 1)

            n = UNITS["branch"]
            with act.Fori(0, 4) as i:
                for s in range(2):
                    m = 2 * i + s
                    act.activation(gates[:, m, :], gates[:, m, :], ACT.Sigmoid).then_inc(brs["sig"], 1)
                    act.activation(gates[:, HEADS + m, :], gates[:, HEADS + m, :], ACT.Sigmoid)\
                       .then_inc(brs["sig"], 1)
                    split_hi(n + m + 2, s)
                    act.wait_ge(brs["mixed"], m + 3)
                    act.activation(mix_hi[:, m, :], zt[s][:, :], ACT.Copy).then_inc(brs["hi"], 1)

            def residual_squares(name, tokens, sems):
                n, freed = UNITS[name], FREED[name]

                def body(i, width):
                    for s in range(2):
                        m = 2 * i + s
                        if sems:
                            act.wait_ge(ps_free[s], freed[s] + 2 + i)
                            act.activation(sq[s][:, 0:tokens], h_tile(tokens, m), ACT.Square).then_inc(sems["sq"], 1)
                        if width:
                            split_hi(n + m + 2, s, width)
                peeled(act, 4, body, WIDTHS[n], after(name, 8))

            residual_squares("out", T1, n2)
            norm_act(n2, T1)
            norm_hi(n2, T1)

            def memory_rows():
                act.wait_ge(mem_loaded, 16)
                for c in range(2):
                    act.activation(mem_square[:, :], mem_rows[:, c, :], ACT.Square, accum_out=mem_stat[:, 0, c:c + 1])\
                       .then_inc(mem_step, 1)
                    act.wait_ge(mem_step, c + 1)
                act.activation(mem_stat[:, 1, :], mem_stat[:, 0, :], ACT.Sqrt, scale=1.0 / D, bias=eps)\
                   .then_inc(mem_step, 1)

            def memory_split():
                act.wait_ge(mem_turned, 1)
                for k in range(KD):
                    if k >= 4:
                        act.wait_ge(mem_lo, k - 3)
                    act.activation(mz_hi[:, k, :], turned_memory(k), ACT.Identity, scale=vec("mem_g", k))\
                       .then_inc(mem_hi, 1)

            def ffn(tag, tokens, s, norm, before=None, between=None):
                for b, half in enumerate("ab"):
                    name = f"up{tag}_{half}"
                    n = UNITS[name]
                    if b and before:
                        before()

                    def body(j, width):
                        jj = b * FH + j
                        split_hi(n + 2 * j + 2, 0, width)
                        act.wait_ge(used, n + 2 * j + 3)
                        if tag == "":
                            act.activation(two(ub[:, :]), ps[0][:, :, 0:CONV // 2], ACT.Copy).then_inc(ps_free[0], 1)
                            act.wait_ge(*s.at("conv", 3 * jj + 3))
                            act.activation(sig[:, 0:SEQ], cv[2][:, 0:SEQ], ACT.Sigmoid).then_inc(s["sig"], 1)
                        else:
                            act.activation(sig[:, 0:tokens], psv(tokens, 0), ACT.Sigmoid).then_inc(s["sig"], 1)
                        split_hi(n + 2 * j + 3, 1, width)
                        act.wait_ge(ps_free[1], FREED[name][1] + 2 + j)
                        act.activation(g_hi[:, j, 0:tokens], gv[:, 0:tokens], ACT.Copy).then_inc(s["hi"], 1)
                    peeled(act, FH, body, UNIT, SLOT)
                    if b and between:
                        between()
                    residual_squares(f"down{tag}_{half}", tokens, norm if b else None)
            ffn("", SEQ, f1, fin, memory_rows, memory_split)

            n = UNITS["mem"]

            def memory_keys(l, t_):
                act.wait_ge(used, n + 4 * l + t_ + 3)
                head = MH * l + 2 * t_
                act.activation(mk[:, head, :], ps[t_][:, 0, 0:NMEM], ACT.Copy)
                for j in range(2):
                    x = act.activation(mk[j * HD:(j + 1) * HD, head + 1, :], ps[t_][HD:, 0, 0:NMEM], ACT.Copy)
                x.then_inc(ps_free[t_], 1)
            split_hi(n + 2, 0)
            memory_keys(0, 0)
            split_hi(n + 3, 1)
            memory_keys(0, 1)
            split_hi(n + 4, 0)
            split_hi(n + 5, 1)
            norm_act(fin, SEQ)
            for k in range(KD):
                act.wait_ge(*fin.at("z", k + 1))
                if k >= 2:
                    act.wait_ge(*norm_a0.at("acc", k))
                act.activation(sq[k % 2][:, 0:SEQ], h_tile(SEQ, k), ACT.Square).then_inc(norm_a0["sq"], 1)
                if k == 3:
                    memory_keys(1, 0)
                    split_hi(n + 6, 0)
                    memory_keys(1, 1)
                    split_hi(n + 7, 1)
            split_hi(n + 8, 0)
            split_hi(n + 9, 1)

            def layer(l):
                norm_act(norm_a[l], SEQ)
                norm_hi(norm_a[l], SEQ, l)

                n, freed = UNITS[f"qk{l}"], FREED[f"qk{l}"]

                def project(i, first, into, at_, scale, width):
                    for s in range(2):
                        m = 2 * (first + i) + s
                        split_hi(n + m + 2, s, width)
                        act.wait_ge(used, n + m + 3)
                        if into is k_heads:
                            act.activation(into[:, bass.ds(4 * i + (at_ + 2 * s), 1), :], ps[s][:, 0:1, :],
                                           ACT.Copy, scale=scale)
                            for j in range(2):
                                x = act.activation(
                                    into[j * HD:(j + 1) * HD, bass.ds(4 * i + (at_ + 2 * s + 1), 1), :],
                                    ps[s][HD:, 0:1, :], ACT.Copy, scale=scale)
                        else:
                            for j in range(2):
                                x = act.activation(into[0:HD, bass.ds(4 * i + (at_ + 2 * s + j), 1), :],
                                                   ps[s][j * HD:(j + 1) * HD, 0:1, :], ACT.Copy, scale=scale)
                        x.then_inc(ps_free[s], 1)
                with act.Fori(0, 3) as i:
                    project(i, 0, q_heads, 0, HD ** -0.5, UNIT)
                if l:
                    with act.Fori(0, 3) as i:
                        project(i, 3, k_heads, 0, 1.0, UNIT)
                else:
                    project(0, 3, k_heads, 0, 1.0, UNIT)
                project(0, (4, 6)[l], q_heads, QH, HD ** -0.5, WIDTHS[UNITS[f"v{l}"]])

                n = UNITS[f"v{l}"]
                for half in range((1, 2)[l]):
                    count, width = ((2, KVA * HD), (4, 384))[l]
                    for i in range(count - 1):
                        m = count * half + i
                        split_hi(n + m + 2, i % 2, WIDTHS[n + m + 2])
                    act.wait_ge(used, n + count * (half + 1) + 2)
                    act.activation(v_tok[:, 0:2, half * width:(half + 1) * width], ps[0][:, :, 0:width], ACT.Copy)\
                       .then_inc(ps_free[0], 1)
                    m = count * (half + 1) - 1
                    split_hi(n + m + 2, 1, WIDTHS[n + m + 2])

                s = atts[l]

                def exps(h, r, memory, blocks):
                    for b in blocks:
                        lo, width = span(memory, b)
                        act.activation(ls[r][:, b, lo:lo + width], ls[r][:, b, lo:lo + width], ACT.Exp,
                                       bias=neg_max[r][:, b:b + 1], accum_out=row_sum[r][:, b:b + 1])\
                           .then_inc(s["exp"], 1)

                def copy(h, memory, b):
                    _, width = span(memory, b)
                    act.wait_ge(*s.at("t", 4 * h + (b + 1)))
                    act.wait_ge(*s.at("y", 4 * h + (b - 1)))
                    act.activation(pts[b % 2][:, 0:width], ps[3][:, b % 2, 0:width], ACT.Copy).then_inc(s["pa"], 1)

                def step(h, r, n_, g):
                    mid, back = 1 <= n_ <= AH, 2 <= n_ < AH + 2
                    memory = n_ - 1 >= QH
                    if back:
                        copy(h - 2, n_ - 2 >= QH, 0)
                    if mid:
                        act.wait_ge(*s.at("neg", h))
                        if l == 0 and not memory:
                            act.activation(sink_exp[(r + 2) % 3][:, :], neg_max[(r + 2) % 3][:, :], ACT.Exp,
                                           bias=vec("sink", h - 1))
                        exps(h - 1, (r + 2) % 3, memory, (0,))
                    for b in (1, 2):
                        if back:
                            copy(h - 2, n_ - 2 >= QH, b)
                        if mid:
                            exps(h - 1, (r + 2) % 3, memory, ((1,), (2, 3))[b - 1])
                head_steps(act, step)

                for k in range(KD):
                    act.wait_ge(*s.at("turned", k + 1))
                    act.activation(z_hi[:, k, 0:SEQ], ps[k % 2][:, 0, :], ACT.Copy).then_inc(s["hi"], 1)
                residual_squares(f"out{l}", SEQ, norm_f[l])
                norm_act(norm_f[l], SEQ)
                norm_hi(norm_f[l], SEQ)
                ffn(str(l), SEQ, ffn2[l], (norm_a1, norm_o)[l])
            layer(0)
            layer(1)
            norm_act(norm_o, SEQ)
            act.wait_ge(out_turned, 1)
            for c in range(CHUNKS - 1):
                act.activation(out_rows[:, c, 0:D // 2], ps[c][:, 0, :], ACT.Copy)
            act.wait_ge(out_turned, 2)
            for c in range(CHUNKS):
                if c == 3:
                    act.activation(out_rows[:, c, 0:D // 2], ps[c][:, 0, :], ACT.Copy)
                act.activation(out_rows[:, c, D // 2:], ps[c][:, 1, :], ACT.Copy).then_inc(out_copied, 1)

        @block.vector
        def _(dve):
            def split_lo(n, s, width=UNIT):
                dve.wait_ge(hi_done, n + 1)
                dve.tensor_tensor(w_lo[s][:, 0:width], raw[s][:, 0:width], w_hi[s][:, 0:width].bitcast(F32),
                                  ALU.subtract).then_inc(lo_done, 1)

            dve.wait_ge(const_loaded, 32)
            lb0 = par[:, pc["lb0"]:pc["lb0"] + 8]
            lb1 = par[:, pc["lb1"]:pc["lb1"] + 8]
            dve.tensor_tensor(lbc[:, 2, :], lb0, lb1, ALU.max).then_inc(lb_step, 1)
            dve.wait_ge(lb_step, 1)
            dve.tensor_tensor(lbc[:, 0, :], lb0, lbc[:, 2, :], ALU.subtract).then_inc(lb_step, 1)
            dve.tensor_tensor(lbc[:, 1, :], lb1, lbc[:, 2, :], ALU.subtract).then_inc(lb_step, 1)
            dve.wait_ge(lb_step, 4)
            dve.tensor_tensor(lbc[:, 0, :], lbc[:, 2, :], lbc[:, 3, :], ALU.add).then_inc(lb_step, 1)
            dve.wait_ge(lb_step, 5)
            dve.reciprocal(lbc[:, 1, :], lbc[:, 0, :]).then_inc(lb_step, 1)
            dve.wait_ge(lb_step, 6)
            dve.tensor_tensor(lbc[:, 0, :], lbc[:, 2, :], lbc[:, 1, :], ALU.mult).then_inc(lb_step, 1)
            dve.wait_ge(lb_step, 7)
            dve.tensor_scalar(lbc[:, 1, :], lbc[:, 0, :], -1.0, 1.0, ALU.mult, ALU.add).then_inc(lb_step, 1)
            dve.tensor_scalar(lbc[:, 2, :], lbc[:, 0, :], 1.0, -1.0, ALU.mult, ALU.add).then_inc(lb_step, 1)
            for k in range(1, KD, 2):
                dve.wait_ge(x_turned, k + 1)
                dve.tensor_copy(H[:, k, META:], ps[k // 2][:, k % 2, :]).then_inc(x_copied_odd, 1)

            def sum_squares(s, tokens):
                dve.memset(acc[:, 0:tokens], 0.0).then_inc(s["acc"], 1)
                for k in range(KD):
                    dve.wait_ge(*s.at("sq", k + 1))
                    dve.wait_ge(*s.at("acc", k + 1))
                    dve.tensor_tensor(acc[:, 0:tokens], acc[:, 0:tokens], sq[k % 2][:, 0:tokens], ALU.add)\
                       .then_inc(s["acc"], 1)

            def norm_inverse(s, tokens, meanwhile=None):
                n, width = pieces(tokens)
                v, root, y, yy, f, better = (stat[0:width, i, 0:n] for i in range(6))
                dve.wait_ge(*s.at("sum", 1))
                dve.tensor_scalar(v, ps[2][0:width, 0, 0:n], 1.0 / D, EPS, ALU.mult, ALU.add).then_inc(s["inv"], 1)
                dve.wait_ge(*s.at("root", 1))
                dve.reciprocal(y, root).then_inc(s["inv"], 1)
                dve.wait_ge(*s.at("inv", 2))
                dve.tensor_tensor(yy, y, y, ALU.mult).then_inc(s["inv"], 1)
                dve.wait_ge(*s.at("inv", 3))
                dve.tensor_tensor(f, yy, v, ALU.mult).then_inc(s["inv"], 1)
                dve.wait_ge(*s.at("inv", 4))
                dve.tensor_scalar(f, f, -0.5, 1.5, ALU.mult, ALU.add).then_inc(s["inv"], 1)
                dve.wait_ge(*s.at("inv", 5))
                dve.tensor_tensor(better, y, f, ALU.mult).then_inc(s["inv"], 1)
                if meanwhile:
                    meanwhile()
                dve.wait_ge(*s.at("wide", 1))

            def norm_scale(s, tokens, x, g, order=None, meanwhile=None):
                norm_inverse(s, tokens, meanwhile)
                for k in range(KD):
                    if k >= 4:
                        dve.wait_ge(*s.at(("even", "odd")[k % 2], k // 2 - 1))
                    dve.scalar_tensor_tensor(shaped(tokens, z_now[k % 4]), two(x(k)) if tokens == T1 else x(k), g(k),
                                             psv(tokens, 3), ALU.mult, ALU.mult).then_inc(s["z"], 1)
                    if k % 2:
                        lo, z = z_lo[:, k - 1, 0:tokens], z_now[(k - 1) % 4][:, 0:tokens]
                        hi = z_hi[:, k - 1, 0:tokens].bitcast(F32)
                        if order:
                            lo, z, hi = blocked(lo), natural(z), blocked(hi)
                        dve.wait_ge(*s.at("hi", k))
                        dve.tensor_tensor(lo, z, hi, ALU.subtract).then_inc(s["even"], 1)

            def first_units():
                split_lo(0, 0)
                split_lo(1, 1)
            sum_squares(n1, T1)
            norm_scale(n1, T1, lambda k: H[:, k, :], lambda k: vec("norm1", k), None, first_units)

            n = UNITS["qf"]
            with dve.Fori(0, HEADS) as h:
                split_lo(n + 2 * h + 2, 0)
                dve.wait_ge(qs["sig"], h + 1)
                dve.tensor_tensor(two(qf[:, 2 * h, :]), out528(0), two(sig[:, :]), ALU.mult).then_inc(ps_free[0], 1)
                split_lo(n + 2 * h + 3, 1)
            dve.wait_ge(late_loaded, 32)
            dve.tensor_copy(masks[:, :, :].rearrange("p a b -> p (a b)"), mask_rows[:, :]).then_inc(masks_ready, 1)
            n = UNITS["v"]
            split_lo(n + 2, 0)
            split_lo(n + 3, 1)
            split_lo(n + 4, 0)
            dve.wait_ge(used, n + 6)
            dve.tensor_copy(V[:, 2:4, :], ps[1][:, :, :]).then_inc(vs["dve"], 1)
            split_lo(n + 5, 1)
            n = UNITS["pinog"]
            with dve.Fori(0, 2) as i:
                split_lo(n + 2 * i + 2, 0)
                split_lo(n + 2 * i + 3, 1)
            with dve.Fori(0, 2) as i:
                for s in range(2):
                    split_lo(n + 2 * i + s + 6, s)
                    dve.wait_ge(og_sig, 2 * i + s + 1)
                    dve.tensor_tensor(two(og[:, 2 * i + s, :]), out528(s), two((sig, rstd)[s][:, :]), ALU.mult)\
                       .then_inc(ps_free[s], 1)

            n = UNITS["gates"]
            dve.wait_ge(ps_free[0], POOLED[0])
            dve.wait_ge(ps_free[1], POOLED[1])
            dve.wait_ge(masks_ready, 1)

            def scan(h):
                dve.wait_ge(mx["ln"], h + 1)
                dve.tensor_tensor_scan(A[:, :], restart, lf[:, :], 0.0, ALU.mult, ALU.add).then_inc(mx["scan"], 1)

            def head(h, last):
                dve.wait_ge(mx["turn"], 10 * h + 1)
                dve.tensor_scalar(kk[:, :], qf[:, 2 * h + 1, :], lbc[:, 2, bass.ds(h, 1)], lbc[:, 1, bass.ds(h, 1)],
                                  ALU.mult, ALU.add).then_inc(mx["k"], 1)
                dve.wait_ge(mx["scan"], h + 2)

                def sub(l):
                    left, right, _ = halves(X[l % 3][:, :], l)
                    aleft, aright, ref = halves(A[:, :], l)
                    if l >= 3:
                        dve.wait_ge(mx["turn"], 10 * h + turn_of(l - 3) + 2)
                    dve.tensor_tensor(right, aright, ref, ALU.subtract)
                    dve.tensor_tensor(left, ref, aleft, ALU.subtract).then_inc(mx["sub"], 1)

                def mul_right(l):
                    _, right, _ = halves(X[l % 3][:, :], l)
                    _, qright, _ = halves(qf[:, 2 * h, :], l)
                    dve.wait_ge(mx["exp"], h * LEVELS + l + 1)
                    dve.tensor_tensor(right, right, qright, ALU.mult).then_inc(mx["mul_r"], 1)

                def scored(l):
                    dve.wait_ge(mx["turn"], 10 * h + turn_of(l) + 2)
                    dve.wait_ge(mx["score_read"], 9 * h + (l + 3 if l <= 3 else l + 4))

                def take(l):
                    tt = turn_of(l)
                    h = 2 ** l
                    taken = sc[:, :].rearrange("p (c n s h) -> p c n s h", c=4, s=2, h=h)[:, :, :, 1, :]
                    mask = masks[:, l, :].rearrange("p (c n s h) -> p c n s h", c=1, s=2, h=h)[:, :, :, 1, :]
                    dve.copy_predicated(taken, mask.to_broadcast([P, 4, P // (2 * h), h]),
                                        ps[2][:, tt % 2, 0:SEQ // 2].rearrange("p (c n h) -> p c n h", c=4, h=h))\
                       .then_inc(mx["score_read"], 1)

                sub(0)
                sub(1)
                dve.tensor_tensor(kd[:, 0:META], A[:, META - 1:META].to_broadcast([P, META]), A[:, 0:META],
                                  ALU.subtract).then_inc(mx["kd_sub"], 1)
                mid = chunked(A[:, META:META + 3 * P], 3)
                dve.tensor_tensor(chunked(kd[:, META:], 3), mid[:, :, P - 1:P].to_broadcast([P, 3, P]), mid,
                                  ALU.subtract).then_inc(mx["kd_sub"], 1)
                mul_right(0)
                dve.wait_ge(mx["o"], h + 1)
                dve.wait_ge(mx["turn"], 10 * h + 2)
                dve.tensor_tensor(chunked(sc[:, :], 4), chunked(ps[2][:, 0, :], 4),
                                  ident.rearrange("p (c t) -> p c t", c=1).to_broadcast([P, 4, P]), ALU.mult)\
                   .then_inc(mx["score_read"], 1)
                sub(2)
                scored(0)
                mul_right(1)
                take(0)
                dve.wait_ge(mx["qe_exp"], 2 * h + 1)
                dve.tensor_tensor(qe[:, :], qe[:, :], qf[:, 2 * h, META:], ALU.mult).then_inc(mx["qe"], 1)
                sub(3)
                scored(1)
                mul_right(2)
                take(1)
                sub(4)
                scored(2)
                mul_right(3)
                take(2)
                sub(5)
                split_lo(n + 2 * h + 2, 0)
                scored(3)
                mul_right(4)
                take(3)
                s0 = ps[3][0:META, 1, :]
                dve.tensor_tensor(sc0[:, :], s0[:, 0:META], ident[0:META, 0:META], ALU.mult).then_inc(mx["meta"], 1)

                def take_meta(l):
                    dve.copy_predicated(sc0[:, :], masks[0:META, l, 0:META],
                                        s0[:, (l + 1) * META:(l + 2) * META]).then_inc(mx["meta"], 1)

                dve.wait_ge(mx["meta"], 5 * h + 1)
                sub(6)
                take_meta(0)
                dve.wait_ge(mx["meta"], 5 * h + 2)
                mul_right(5)
                take_meta(1)
                dve.wait_ge(mx["turn"], 10 * h + 8)
                dve.wait_ge(mx["qe_exp"], 2 * h + 2)
                dve.wait_ge(mx["meta"], 5 * h + 3)
                dve.tensor_copy(st[:, 0, :], ps[2][:, 0, 0:VD]).then_inc(mx["states"], 1)
                take_meta(2)
                for c in range(1, 4):
                    dve.wait_ge(mx["states"], 3 * h + c)
                    if c == 2:
                        dve.wait_ge(mx["meta"], 5 * h + 4)
                    x = dve.scalar_tensor_tensor(st[:, c, :], st[:, c - 1, :], dec[:, c - 1:c],
                                                 ps[2][:, 0, c * VD:(c + 1) * VD], ALU.mult, ALU.add)
                    x.then_inc(mx["states"] if c < 3 else mx["score_read"], 1)
                    if c == 2:
                        take_meta(3)
                scored(4)
                mul_right(6)
                take(4)
                if not last:
                    dve.wait_ge(mx["sub"], (h + 1) * LEVELS)
                    scan(h + 1)
                scored(5)
                split_lo(n + 2 * h + 3, 1)
                take(5)
                scored(6)
                dve.memset(spare[:, :], 0.0)
                take(6)

            scan(0)
            with dve.Fori(0, HEADS // 2 - 1) as p:
                head(2 * p, False)
                head(2 * p + 1, False)
            head(HEADS - 2, False)
            head(HEADS - 1, True)

            for g in range(4):
                dve.wait_ge(oas["hi"], g + 1)
                dve.tensor_tensor(z_lo[:, 4 + g, :], pin[:, g, PADC:], z_hi[:, 4 + g, :].bitcast(F32), ALU.subtract)\
                   .then_inc(oas["pin_lo"], 1)
            for p in range(4):
                dve.wait_ge(oas["inv"], p + 1)
                scaled = (ta, tb)[p % 2]
                if p >= 2:
                    dve.wait_ge(oas["z"], p - 1)
                dve.scalar_tensor_tensor(scaled[:, :], qf[:, 4 * p, :], vec("head_g", p), (rstd, sig)[p % 2][:, :],
                                         ALU.mult, ALU.mult).then_inc(oas["scaled"], 1)
                dve.wait_ge(oas["scaled"], p + 1)
                if p >= 2:
                    dve.wait_ge(oas["lo"], p - 1)
                dve.tensor_tensor(zt[p % 2][:, :], scaled[:, :], og[:, p, :], ALU.mult).then_inc(oas["z"], 1)

            n = UNITS["branch"]
            with dve.Fori(0, 4) as i:
                for s in range(2):
                    m = 2 * i + s
                    split_lo(n + m + 2, s)
                    dve.wait_ge(used, n + m + 3)
                    dve.wait_ge(brs["sig"], 2 * m + 2)
                    dve.tensor_tensor(two(ta[:, :]), out528(2 * s), two(gates[:, m, :]), ALU.mult)\
                       .then_inc(brs["a"], 1)
                    dve.tensor_tensor(two(tb[:, :]), out528(2 * s + 1), two(gates[:, HEADS + m, :]), ALU.mult)\
                       .then_inc(brs["a"], 1)
                    dve.wait_ge(brs["a"], 2 * m + 2)
                    dve.wait_ge(brs["lo"], m + 1)
                    dve.tensor_tensor(zt[s][:, :], ta[:, :], tb[:, :], ALU.add).then_inc(brs["mixed"], 1)

            def residual(name, tokens, sems, order=None):
                n, freed = UNITS[name], FREED[name]
                if sems:
                    dve.memset(acc[:, 0:tokens], 0.0).then_inc(sems["acc"], 1)

                def body(i, width):
                    for s in range(2):
                        m = 2 * i + s
                        dve.wait_ge(used, n + m + 3)
                        tile, add = h_tile(tokens, m), psv(tokens, s)
                        if tokens == T1:
                            tile = two(tile)
                        elif order:
                            tile, add = natural(tile), blocked(add)
                        dve.tensor_tensor(tile, tile, add, ALU.add).then_inc(ps_free[s], 1)
                        if sems:
                            dve.wait_ge(*sems.at("sq", m + 1))
                            dve.wait_ge(*sems.at("acc", m + 1))
                            dve.tensor_tensor(acc[:, 0:tokens], acc[:, 0:tokens], sq[s][:, 0:tokens], ALU.add)\
                               .then_inc(sems["acc"], 1)
                        if width:
                            split_lo(n + m + 2, s, width)
                peeled(dve, 4, body, WIDTHS[n], after(name, 8))

            residual("out", T1, n2)
            norm_scale(n2, T1, lambda k: H[:, k, :], lambda k: vec("norm2", k))

            def memory_rows():
                dve.wait_ge(mem_step, 3)
                dve.reciprocal(mem_stat[:, 2, :], mem_stat[:, 1, :]).then_inc(mem_step, 1)
                dve.wait_ge(mem_step, 4)
                for c in range(2):
                    dve.tensor_scalar(mem_rows[:, c, :], mem_rows[:, c, :], mem_stat[:, 2, c:c + 1], 1.0,
                                      ALU.mult, ALU.mult).then_inc(mem_step, 1)

            def memory_split():
                for k in range(KD):
                    dve.wait_ge(mem_hi, k + 1)
                    dve.scalar_tensor_tensor(mz_lo[:, k, :], turned_memory(k), vec("mem_g", k),
                                             mz_hi[:, k, :].bitcast(F32), ALU.mult, ALU.subtract).then_inc(mem_lo, 1)

            def ffn(tag, tokens, s, norm, before=None, between=None):
                for b, half in enumerate("ab"):
                    name = f"up{tag}_{half}"
                    n = UNITS[name]
                    if b and before:
                        before()

                    def body(j, width):
                        jj = b * FH + j
                        split_lo(n + 2 * j + 2, 0, width)
                        if tag == "":
                            w = [vec("conv_w", i * FT + jj) for i in range(3)]
                            dve.wait_ge(ps_free[0], FREED[name][0] + 2 + j)
                            dve.tensor_scalar(cv[0][:, 0:SEQ], ub[:, 4:], w[2], vec("conv_b", jj), ALU.mult, ALU.add)\
                               .then_inc(s["conv"], 1)
                            dve.wait_ge(*s.at("conv", 3 * jj + 1))
                            dve.scalar_tensor_tensor(cv[1][:, 0:SEQ], ub[:, 3:3 + SEQ], w[1], cv[0][:, 0:SEQ],
                                                     ALU.mult, ALU.add).then_inc(s["conv"], 1)
                            dve.wait_ge(*s.at("conv", 3 * jj + 2))
                            dve.scalar_tensor_tensor(cv[2][:, 0:SEQ], ub[:, 2:2 + SEQ], w[0], cv[1][:, 0:SEQ],
                                                     ALU.mult, ALU.add).then_inc(s["conv"], 1)
                            dve.wait_ge(*s.at("conv", 3 * jj + 3))
                            dve.wait_ge(*s.at("sig", jj + 1))
                            dve.tensor_tensor(si[:, 0:SEQ], cv[2][:, 0:SEQ], sig[:, 0:SEQ], ALU.mult)\
                               .then_inc(s["si"], 1)
                        else:
                            dve.wait_ge(*s.at("sig", jj + 1))
                            dve.tensor_tensor(si[:, 0:tokens], psv(tokens, 0), sig[:, 0:tokens], ALU.mult)\
                               .then_inc(ps_free[0], 1)
                        split_lo(n + 2 * j + 3, 1, width)
                        dve.wait_ge(used, n + 2 * j + 4)
                        if tag == "":
                            dve.wait_ge(*s.at("si", jj + 1))
                        else:
                            dve.wait_ge(ps_free[0], FREED[name][0] + 2 + j)
                        dve.wait_ge(*s.at("lo", jj + 1))
                        dve.tensor_tensor(shaped(tokens, gv), shaped(tokens, si), psv(tokens, 1), ALU.mult)\
                           .then_inc(ps_free[1], 1)
                    peeled(dve, FH, body, UNIT, SLOT)
                    if b and between:
                        between()
                    residual(f"down{tag}_{half}", tokens, norm if b else None)
            ffn("", SEQ, f1, fin, memory_rows, memory_split)

            n = UNITS["mem"]

            def memory_values(l):
                dve.wait_ge(used, n + 4 * l + 6)
                dve.tensor_copy(mv[:, 2 * l:2 * l + 2, :], ps[0][:, :, 0:NMEM]).then_inc(ps_free[0], 1)
            split_lo(n + 2, 0)
            split_lo(n + 3, 1)
            split_lo(n + 4, 0)
            split_lo(n + 5, 1)
            norm_inverse(fin, SEQ)
            dve.memset(acc[:, 0:SEQ], 0.0).then_inc(norm_a0["acc"], 1)

            def add_square(k):
                dve.wait_ge(*norm_a0.at("sq", k + 1))
                dve.wait_ge(*norm_a0.at("acc", k + 1))
                dve.tensor_tensor(acc[:, 0:SEQ], acc[:, 0:SEQ], sq[k % 2][:, 0:SEQ], ALU.add)\
                   .then_inc(norm_a0["acc"], 1)
            for k in range(KD):
                dve.scalar_tensor_tensor(h_tile(SEQ, k), h_tile(SEQ, k), vec("final_g", k), psv(SEQ, 3),
                                         ALU.mult, ALU.mult).then_inc(fin["z"], 1)
                if k >= 1:
                    add_square(k - 1)
                if k == 0:
                    memory_values(0)
                if k == 4:
                    split_lo(n + 6, 0)
                    split_lo(n + 7, 1)
            add_square(KD - 1)
            split_lo(n + 8, 0)
            memory_values(1)
            split_lo(n + 9, 1)

            def layer(l):
                norm_scale(norm_a[l], SEQ, lambda k: h_tile(SEQ, k), lambda k: vec("mix_g", KD * l + k), l)
                n = UNITS[f"qk{l}"]

                def body(i, width):
                    split_lo(n + 2 * i + 2, 0, width)
                    split_lo(n + 2 * i + 3, 1, width)
                peeled(dve, (5, 7)[l], body, UNIT, WIDTHS[UNITS[f"v{l}"]])
                dve.memset(q_heads[HD:, QH:, :], 0.0)
                dve.memset(q_now[0][HD:, :], 0.0)
                n = UNITS[f"v{l}"]
                for half in range((1, 2)[l]):
                    count, width = ((2, KVA * HD), (4, 384))[l]
                    for i in range(count - 1):
                        m = count * half + i
                        split_lo(n + m + 2, i % 2, WIDTHS[n + m + 2])
                    dve.wait_ge(used, n + count * (half + 1) + 2)
                    if half == l:
                        dve.memset(q_now[1][HD:, :], 0.0)
                        dve.memset(q_now[2][HD:, :], 0.0)
                    dve.tensor_copy(v_tok[:, 2:4, half * width:(half + 1) * width], ps[1][:, :, 0:width])\
                       .then_inc(ps_free[1], 1)
                    m = count * (half + 1) - 1
                    split_lo(n + m + 2, 1, WIDTHS[n + m + 2])

                s = atts[l]
                if l == 0:
                    dve.wait_ge(att_loaded, 16)

                def scored(h, b):
                    dve.wait_ge(*s.at("s", 4 * h + (b + 1)))

                def biased(h, r, b):
                    lo, width = span(False, b)
                    at_ = (0, 2 * P, 2 * P, 5 * P)[b] if l else lo
                    dve.tensor_tensor_reduce(ls[r][:, b, lo:lo + width], banks(r + b)[:, 0:width],
                                             bias[r][:, at_:at_ + width], 1.0, 3 * NEG, ALU.add, ALU.max,
                                             row_max[r][:, b:b + 1]).then_inc(s["ls"], 1)

                def taken(h, r, b):
                    dve.wait_ge(*s.at("s", 4 * h + (b + 1)))
                    dve.tensor_copy(ls[r][:, b, 0:NMEM], banks(r + b)[:, 0:NMEM]).then_inc(s["ls"], 1)

                def largest(h, r, b):
                    dve.wait_ge(*s.at("ls", 4 * h + (b + 1)))
                    dve.tensor_reduce(row_max[r][:, b:b + 1], ls[r][:, b, 0:NMEM], AX.X, ALU.max)\
                       .then_inc(s["max"], 1)

                def copy(h, memory, b):
                    _, width = span(memory, b)
                    dve.wait_ge(*s.at("t", 4 * h + (b + 1)))
                    dve.wait_ge(*s.at("y", 4 * h + (b - 1)))
                    dve.tensor_copy(pts[1][:, 0:width], ps[3][:, 1, 0:width]).then_inc(s["pd"], 1)

                def step(h, r, n_, g):
                    banded, front, back, done = n_ < QH, n_ < AH, 2 <= n_ < AH + 2, n_ >= 3
                    back_memory = n_ - 2 >= QH
                    rb = (r + 1) % 3
                    if front:
                        dve.wait_ge(*s.at("t", 4 * h - 8))
                        if banded:
                            dve.wait_ge(*s.at("bias", h + 1))
                            scored(h, 0)
                    if back:
                        dve.wait_ge(*s.at("exp", 4 * h - 4))
                        if l == 0 and not back_memory:
                            dve.tensor_tensor(row_sum[rb][:, :], row_sum[rb][:, :], sink_exp[rb][:, :], ALU.add)\
                               .then_inc(s["sum"], 1)
                            dve.wait_ge(*s.at("sum", h - 1))
                        dve.reciprocal(rsum[rb][:, :], row_sum[rb][:, :]).then_inc(s["inv"], 1)
                    if banded:
                        biased(h, r, 0)
                        scored(h, 1)
                    elif front:
                        taken(h, r, 0)
                        taken(h, r, 1)
                    if done:
                        dve.wait_ge(*s.at("inv", h - 2))
                        dve.wait_ge(*s.at("y", 4 * h - 8))
                        dve.tensor_tensor(y_tok[:, :, bass.ds(h * HD - 3 * HD, HD)], chunked(y_bank(r), 4),
                                          rsum[r][:, :].rearrange("p (c o) -> p c o", o=1)
                                                       .to_broadcast([P, 4, HD]), ALU.mult).then_inc(s["out"], 1)
                    if banded:
                        biased(h, r, 1)
                        scored(h, 2)
                        dve.memset(carrier[:, :], 0.0)
                        biased(h, r, 2)
                        scored(h, 3)
                    elif front:
                        largest(h, r, 0)
                        taken(h, r, 2)
                        largest(h, r, 1)
                        taken(h, r, 3)
                        largest(h, r, 2)
                    if back:
                        copy(h - 2, back_memory, 3)
                    if banded:
                        biased(h, r, 3)
                        dve.wait_ge(*s.at("ls", 4 * h + 4))
                    elif front:
                        largest(h, r, 3)
                        dve.wait_ge(*s.at("max", 4 * (n_ - QH) + 4))
                    if banded and l == 0:
                        dve.tensor_scalar(neg_max[r][:, :], row_max[r][:, :], vec("sink", h), -1.0,
                                          ALU.max, ALU.mult).then_inc(s["neg"], 1)
                    elif front:
                        dve.tensor_scalar(neg_max[r][:, :], row_max[r][:, :], -1.0, 1.0, ALU.mult, ALU.mult)\
                           .then_inc(s["neg"], 1)
                head_steps(dve, step)

                for k in range(KD):
                    dve.wait_ge(*s.at("hi", k + 1))
                    dve.tensor_tensor(z_lo[:, k, 0:SEQ], ps[k % 2][:, 0, :], z_hi[:, k, 0:SEQ].bitcast(F32),
                                      ALU.subtract).then_inc(ps_free[k % 2], 1)
                residual(f"out{l}", SEQ, norm_f[l], l)
                norm_scale(norm_f[l], SEQ, lambda k: h_tile(SEQ, k), lambda k: vec("ffn_g", KD * l + k))
                ffn(str(l), SEQ, ffn2[l], (norm_a1, norm_o)[l])
            layer(0)
            layer(1)

            norm_inverse(norm_o, SEQ)
            for k in range(KD):
                dve.scalar_tensor_tensor(h_tile(SEQ, k), h_tile(SEQ, k), vec("out_g", k), psv(SEQ, 3),
                                         ALU.mult, ALU.mult).then_inc(norm_o["z"], 1)

        @block.tensor
        def _(pe):
            uses = [0, 0]

            def products(s, k, w0, rhs_hi, rhs_lo, outs, first, last):
                for w, rhs, a, b in ((w_hi, rhs_hi, first, False), (w_hi, rhs_lo, False, False),
                                     (w_lo, rhs_hi, False, last)):
                    for out, lo, width in outs:
                        x = pe.matmul(out, w[s][:, w0 + k * P:w0 + (k + 1) * P], rhs[:, lo:lo + width],
                                      start=a, stop=b)
                return x

            def outs528(i):
                return [(ps[i][:, b, 0:HALF], b * HALF, HALF) for b in range(2)]

            def gemm(name, tokens, count, hi, lo, kt=KD, tile_ready=None, outs_of=None):
                n, freed = UNITS[name], FREED[name]

                def pair(i, tile_ready):
                    for s in range(2):
                        pe.wait_ge(ps_free[s], freed[s] + 1 + i)
                        pe.wait_ge(lo_done, n + 2 * i + s + 3)
                        if outs_of:
                            outs = outs_of(s)
                        else:
                            outs = outs528(s) if tokens == T1 else [(ps[s][:, 0, 0:tokens], 0, tokens)]
                        for k in range(kt):
                            if tile_ready and s == 0:
                                tile_ready(k)
                            x = products(s, k, 0, hi[:, k, :], lo[:, k, :], outs, k == 0, k == kt - 1)
                        x.then_inc(used, 1)
                if tile_ready:
                    pair(0, tile_ready)
                    with pe.Fori(0, count - 1) as i:
                        pair(i + 1, None)
                else:
                    with pe.Fori(0, count) as i:
                        pair(i, None)

            def z_tile(s):
                return lambda k: pe.wait_ge(*s.at(("even", "odd")[k % 2], k // 2 + 1))

            pe.wait_ge(const_loaded, 32)
            for c in range(CHUNKS):
                if c % 2 == 0:
                    pe.wait_ge(x_loaded[c // 2], (48, 32)[c // 2])
                for k in range(KD):
                    x = pe.transpose(ps[k // 2][:, k % 2, c * P:(c + 1) * P], x_rows[:, c, k * P:(k + 1) * P], ident)
                    if c == CHUNKS - 1:
                        x.then_inc(x_turned, 1)
            pe.wait_ge(x_copied, 3)
            for k in range(KD):
                x = pe.transpose(ps[2][:, 0, k * META:(k + 1) * META], meta_rows[:, k * P:(k + 1) * P],
                                 ident[0:META, 0:META])
            x.then_inc(meta_turned, 1)

            def norm_sum(s, tokens):
                n, width = pieces(tokens)
                pe.wait_ge(*s.at("acc", KD + 1))
                for c in range(n):
                    x = pe.matmul(ps[2][0:width, 0, c:c + 1], acc[:, c * width:(c + 1) * width], ones[:, 0:1],
                                  start=True, stop=True)
                x.then_inc(s["sum"], 1)

            def norm_spread(s, tokens):
                n, width = pieces(tokens)
                pe.wait_ge(*s.at("inv", 6))
                for c in range(n):
                    b, lo = divmod(c * width, HALF) if tokens == T1 else (0, c * width)
                    x = pe.matmul(ps[3][:, b, lo:lo + width], stat[0:width, 5, c:c + 1].to_broadcast([width, P]),
                                  ident[0:width, 0:width], start=True, stop=True)
                x.then_inc(s["wide"], 1)

            pe.wait_ge(x_copied, 5)
            pe.wait_ge(x_copied_odd, 4)
            norm_sum(n1, T1)
            norm_spread(n1, T1)

            gemm("qf", T1, HEADS, z_hi, z_lo, KD, z_tile(n1))
            uses = [HEADS, HEADS]

            n = UNITS["v"]
            pe.wait_ge(ps_free[0], uses[0] + 1)
            pe.wait_ge(ps_free[1], uses[1] + 1)
            into = [(ps[0], 0, META), (ps[0], 1, META + P), (ps[1], 0, META + 2 * P), (ps[1], 1, META + 3 * P),
                    (ps[2], 0, 0)]
            for i in range(4):
                pe.wait_ge(lo_done, n + i + 3)
                s = i % 2
                for kk_ in range(2):
                    k = 2 * i + kk_
                    for zz, ww, a, b in ((z_hi, w_hi, k == 0, False), (z_lo, w_hi, False, False),
                                         (z_hi, w_lo, False, k == KD - 1)):
                        for buf, bank, lo in into:
                            x = pe.matmul(buf[:, bank, :], zz[:, k, lo:lo + P], ww[s][:, kk_ * 512:(kk_ + 1) * 512],
                                          start=a, stop=b)
                x.then_inc(used, 1)
            uses = [uses[0] + 1, uses[1]]

            pe.wait_ge(vs["dve"], 1)
            gemm("pinog", T1, 4, z_hi, z_lo)
            uses = [uses[0] + 4, uses[1] + 4]

            pe.wait_ge(late_loaded, 32)
            for g in range(4):
                pe.wait_ge(pools["ready"], g + 1)
                pe.wait_ge(ps_free[g % 2], uses[g % 2] + 1)
                uses[g % 2] += 1
                for b in range(2):
                    x = pe.matmul(ps[g % 2][:, b, 0:HALF], pool_w[:, g, :],
                                  pin[:, g, PADC + b * HALF:PADC + (b + 1) * HALF], start=True, stop=True)
                x.then_inc(pools["sum"], 1)

            n = UNITS["gates"]
            base = list(uses)
            pe.wait_ge(vs["act"], 1)

            def head(h, j):
                def gate(i, k):
                    if k == 0:
                        pe.wait_ge(ps_free[i], base[i] + 1 + h)
                        pe.wait_ge(lo_done, n + 2 * h + i + 3)
                    for kq in (k, k + 1):
                        x = products(i, kq, 0, z_hi[:, kq, :], z_lo[:, kq, :], outs528(i), kq == 0, kq == KD - 1)
                    if k + 2 == KD:
                        x.then_inc(used, 1)

                def scores(tt, x, l=None):
                    if x is None:
                        lhs, rhs = kk, qf[:, 2 * h, :]
                    else:
                        lhs, rhs = x, x[:, :]
                    bank = ps[2][:, tt % 2, :]
                    if tt <= 4:
                        pe.matmul(ps[3][0:META, 1, tt * META:(tt + 1) * META], lhs[:, 0:META], rhs[:, 0:META],
                                  start=True, stop=True)
                    for c in range(CHUNKS):
                        lo = META + c * P
                        if x is None:
                            out, queries = bank[:, c * P:(c + 1) * P], rhs[:, lo:lo + P]
                        else:
                            out = bank[:, c * P // 2:(c + 1) * P // 2].rearrange("p (n h) -> p n h", h=2 ** l)
                            queries = right_halves(rhs[:, lo:lo + P], l)
                        x_ = pe.matmul(out, lhs[:, lo:lo + P], queries, start=True, stop=True)
                    x_.then_inc(mx["turn"], 1)

                def level(l):
                    pe.wait_ge(mx["mul_r"], h * LEVELS + l + 1)
                    pe.wait_ge(mx["mul_l"], h * LEVELS + l + 1)
                    scores(turn_of(l), X[l % 3], l)

                gate(0, 0)
                if j == 0:
                    pe.wait_ge(mx["o_read"], h + 1)
                pe.wait_ge(mx["k"], h + 1)
                pe.wait_ge(mx["score_read"], 9 * h + 1)
                scores(0, None)
                gate(0, 2)
                pe.wait_ge(mx["score_read"], 9 * h + 2)
                level(0)
                gate(0, 4)
                pe.wait_ge(mx["score_read"], 9 * h + 3)
                level(1)
                gate(0, 6)
                pe.wait_ge(mx["score_read"], 9 * h + 4)
                level(2)
                gate(1, 0)
                pe.wait_ge(mx["score_read"], 9 * h + 5)
                level(3)
                gate(1, 2)
                pe.wait_ge(mx["kd"], h + 1)
                pe.wait_ge(mx["score_read"], 9 * h + 6)
                pe.transpose(ps[2][0:META, 1, 0:P], kd[:, 0:META], ident)
                for c in range(1, 4):
                    x = pe.transpose(ps[2][:, 1, c * P:(c + 1) * P], kd[:, META + (c - 1) * P:META + c * P], ident)
                x.then_inc(mx["turn"], 1)
                gate(1, 4)
                pe.wait_ge(mx["kdt"], 2 * h + 2)
                pe.wait_ge(mx["vh"], 2 * h + 2)
                pe.wait_ge(mx["score_read"], 9 * h + 7)
                for c in range(4):
                    lhs = kdt[0:META, 0, :] if c == 0 else kdt[:, c, :]
                    rhs = vh0[:, :] if c == 0 else vh[:, c - 1, :]
                    x = pe.matmul(ps[2][:, 0, c * VD:(c + 1) * VD], lhs, rhs, start=True, stop=True)
                x.then_inc(mx["turn"], 1)
                gate(1, 6)
                level(4)
                pe.wait_ge(mx["score_read"], 9 * h + 8)
                level(5)
                pe.wait_ge(mx["score_read"], 9 * h + 9)
                level(6)
                pe.wait_ge(mx["meta"], 5 * h + 5)
                pe.wait_ge(mx["score_read"], 9 * h + 11)
                pe.wait_ge(mx["qe"], h + 1)
                rows = slice(j * VD, (j + 1) * VD)
                pe.matmul(ps[3][rows, 1, 96:96 + META], vh0[:, :], sc0[:, :], start=True, stop=True)
                for c in range(CHUNKS):
                    cs = slice(c * P, (c + 1) * P)
                    pe.matmul(ps[3][rows, 0, cs], vh[:, c, :], sc[:, cs], start=True, stop=False)
                    x = pe.matmul(ps[3][rows, 0, cs], st[:, c, :], qe[:, cs], start=False, stop=True)
                x.then_inc(mx["o"], 1)

            with pe.Fori(0, HEADS // 2) as p:
                head(2 * p, 0)
                head(2 * p + 1, 1)

            for p in range(4):
                pe.wait_ge(oas["sq"], p + 1)
                pe.wait_ge(ps_free[p % 2], FREED["oa"][p % 2] + 1 + p // 2)
                for b in range(2):
                    x = pe.matmul(ps[p % 2][:, b, 0:HALF], pair_ones, sq[p % 2][:, b * HALF:(b + 1) * HALF],
                                  start=True, stop=True)
                x.then_inc(oas["sum"], 1)

            n = UNITS["branch"]
            pe.wait_ge(ps_free[0], FREED["out"][0] + 1)
            pe.wait_ge(ps_free[1], FREED["out"][1] + 1)

            def branch_pair(i, first):
                for s in range(2):
                    m = 2 * i + s
                    pe.wait_ge(lo_done, n + m + 3)
                    pe.wait_ge(brs["mixed"], m + 1)
                    for k in (4, 5, 6, 7, 0, 1, 2, 3):
                        if first and s == 0:
                            if k >= 4:
                                pe.wait_ge(oas["pin_lo"], k - 3)
                            else:
                                pe.wait_ge(oas["lo"], k + 1)
                        x = products(s, k, 0, z_hi[:, k, :], z_lo[:, k, :], outs528(2 * s + k // 4),
                                     k % 4 == 0, k % 4 == 3)
                    x.then_inc(used, 1)
            branch_pair(0, True)
            with pe.Fori(0, 3) as i:
                branch_pair(i + 1, False)

            pe.wait_ge(brs["mixed"], 9)
            gemm("out", T1, 4, mix_hi, mix_lo, KD, lambda k: pe.wait_ge(brs["lo"], k + 3))

            def ffn(tag, tokens, s, norm, between=None):
                for b, half in enumerate("ab"):
                    gemm(f"up{tag}_{half}", tokens, FH, z_hi, z_lo, KD, None if b else z_tile(norm),
                         None if tag else conv_outs)
                    if b and between:
                        between()
                    gemm(f"down{tag}_{half}", tokens, 4, g_hi, g_lo, FH,
                         lambda k: pe.wait_ge(*s.at("lo", 2 + b * FH + k)))
            def memory_turned():
                pe.wait_ge(mem_step, 6)
                for k in range(KD):
                    for c in range(2):
                        x = pe.transpose(turned_memory(k)[:, c * P:(c + 1) * P], mem_rows[:, c, k * P:(k + 1) * P],
                                         ident)
                x.then_inc(mem_turned, 1)

            norm_sum(n2, T1)
            norm_spread(n2, T1)
            ffn("", SEQ, f1, n2, memory_turned)

            n, freed = UNITS["mem"], FREED["mem"]
            pe.wait_ge(mem_lo, KD)
            for l in range(2):
                for s in range(2):
                    pe.wait_ge(ps_free[s], freed[s] + 1 + (2 * l, l)[s])
                    pe.wait_ge(lo_done, n + 4 * l + s + 3)
                    for k in range(KD):
                        x = products(s, k, 0, mz_hi[:, k, :], mz_lo[:, k, :], [(ps[s][:, 0, 0:NMEM], 0, NMEM)],
                                     k == 0, k == KD - 1)
                    x.then_inc(used, 1)
                pe.wait_ge(ps_free[0], freed[0] + 2 + 2 * l)
                for s in range(2):
                    pe.wait_ge(lo_done, n + 4 * l + s + 5)
                    for kk_ in range(4):
                        k = 4 * s + kk_
                        for zz, ww, a, b in ((mz_hi, w_hi, k == 0, False), (mz_lo, w_hi, False, False),
                                             (mz_hi, w_lo, False, k == KD - 1)):
                            for c in range(2):
                                x = pe.matmul(ps[0][:, c, 0:NMEM], zz[:, k, c * P:(c + 1) * P],
                                              ww[s][:, kk_ * NMEM:(kk_ + 1) * NMEM], start=a, stop=b)
                    x.then_inc(used, 1)
                if l == 0:
                    norm_sum(fin, SEQ)
                    norm_spread(fin, SEQ)

            def layer(l):
                norm_sum(norm_a[l], SEQ)
                norm_spread(norm_a[l], SEQ)
                gemm(f"qk{l}", SEQ, (5, 7)[l], z_hi, z_lo, KD, z_tile(norm_a[l]))

                n, freed = UNITS[f"v{l}"], FREED[f"v{l}"]
                count, kt, width = ((2, 4, KVA * HD), (4, 2, 384))[l]
                for half in range((1, 2)[l]):
                    for i in range(count):
                        s, m = i % 2, n + count * half + i
                        if i == 0:
                            pe.wait_ge(ps_free[0], freed[0] + 1 + half)
                            pe.wait_ge(ps_free[1], freed[1] + 1 + half)
                        pe.wait_ge(lo_done, m + 3)
                        for kk_ in range(kt):
                            k = kt * i + kk_
                            for zz, ww, a, b in ((z_hi, w_hi, k == 0, False), (z_lo, w_hi, False, False),
                                                 (z_hi, w_lo, False, k == KD - 1)):
                                for c in range(4):
                                    x = pe.matmul(ps[c // 2][:, c % 2, 0:width], zz[:, k, c * P:(c + 1) * P],
                                                  ww[s][:, kk_ * width:(kk_ + 1) * width], start=a, stop=b)
                        x.then_inc(used, 1)

                s = atts[l]
                pe.wait_ge(ps_free[0], FREED[f"turn{l}"][0] + 1)
                pe.wait_ge(ps_free[1], FREED[f"turn{l}"][1] + 1)

                def scores(h, r, n_, b, kv):
                    memory = n_ >= QH
                    _, width = span(memory, b)
                    if memory:
                        q, keys = q_heads[:, n_, b * P:(b + 1) * P], mk[:, MH * l + n_ - QH, :]
                    else:
                        lo = key_block(False, b, 0) * P
                        q, keys = q_now[r][:, b * P:(b + 1) * P], k_heads[:, bass.ds(kv, 1), lo:lo + width]
                    pe.matmul(banks(r + b)[:, 0:width], q, keys, start=True, stop=True).then_inc(s["s"], 1)

                def turn(h, r, memory, b):
                    _, width = span(memory, b)
                    lo = span(memory, b)[0]
                    pe.wait_ge(*s.at("exp", 4 * h + (b + 1)))
                    pe.wait_ge(*(s.at("pd", h) if b == 1 else s.at("pa", 3 * h + (0, 0, 1, 2)[b])))
                    for j in range(width // P):
                        x = pe.transpose(ps[3][:, b % 2, j * P:(j + 1) * P],
                                         ls[r][:, b, lo + j * P:lo + (j + 1) * P], ident)
                    x.then_inc(s["t"], 1)

                def values(h, r, memory, b, kv, n_):
                    _, width = span(memory, b)
                    if b == 0:
                        pe.wait_ge(*s.at("out", h - 2))
                    pe.wait_ge(*(s.at("pd", h + 1) if b == 3 else s.at("pa", 3 * h + (b + 1))))
                    for j in range(width // P):
                        block = key_block(memory, b, j)
                        if memory:
                            v = mv[:, 2 * l + block, (n_ - QH) * HD:(n_ - QH + 1) * HD]
                        else:
                            v = v_tok[:, block, bass.ds(kv * HD, HD)]
                        x = pe.matmul(y_bank(r)[:, b * HD:(b + 1) * HD], pts[b % 2][:, j * P:(j + 1) * P], v,
                                      start=j == 0, stop=j == width // P - 1)
                    x.then_inc(s["y"], 1)

                def step(h, r, n_, g):
                    front, back = n_ < AH, 2 <= n_ < AH + 2
                    kv, back_kv, last_kv = (h, h - 2, h - 3) if l else (g, g - 1 if r < 2 else g, g - 1)
                    rb, memory = (r + 1) % 3, n_ - 2 >= QH
                    for b in range(4):
                        if front:
                            pe.wait_ge(*s.at("ls", 4 * h + (b - 2)))
                            if n_ < QH:
                                pe.wait_ge(*s.at("q", h + 1))
                        if back:
                            turn(h - 2, rb, memory, b)
                        if front:
                            scores(h, r, n_, b, kv)
                        if b == 0 and n_ >= 3:
                            values(h - 3, r, n_ - 3 >= QH, 3, last_kv, n_ - 3)
                        elif b and back:
                            values(h - 2, rb, memory, b - 1, back_kv, n_ - 2)

                head_steps(pe, step)

                pe.wait_ge(*s.at("out", AH))
                for k in range(KD):
                    pe.wait_ge(ps_free[k % 2], FREED[f"turn{l}"][k % 2] + 1 + k // 2)
                    for c in range(4):
                        x = pe.transpose(ps[k % 2][:, 0, c * P:(c + 1) * P], y_tok[:, c, k * P:(k + 1) * P], ident)
                    x.then_inc(s["turned"], 1)
                pe.wait_ge(ps_free[1], FREED[f"out{l}"][1] + 1)
                gemm(f"out{l}", SEQ, 4, z_hi, z_lo)
                norm_sum(norm_f[l], SEQ)
                norm_spread(norm_f[l], SEQ)
                ffn(str(l), SEQ, ffn2[l], norm_f[l])
            layer(0)
            layer(1)

            pe.wait_ge(ps_free[0], so_far[0] + 1)
            pe.wait_ge(ps_free[1], so_far[1] + 1)
            norm_sum(norm_o, SEQ)
            norm_spread(norm_o, SEQ)
            def out_turn(c, k):
                return pe.transpose(ps[c][:, k // 4, k % 4 * P:(k % 4 + 1) * P],
                                    H[:, k, META + c * P:META + (c + 1) * P], ident)
            for k in range(KD):
                pe.wait_ge(*norm_o.at("z", k + 1))
                for c in range(CHUNKS):
                    if c < 3 or k >= 4:
                        x = out_turn(c, k)
                if k == 3:
                    x.then_inc(out_turned, 1)
            for k in range(4):
                x = out_turn(3, k)
            x.then_inc(out_turned, 1)


def constants():
    import numpy as np

    cc = constant_columns()
    c = np.zeros((P, cc["all"]), np.float32)
    c[:, cc["ident"]:cc["ident"] + P] = np.eye(P)
    c[:, cc["ones"]:cc["ones"] + P] = 1
    c[:, cc["pair_ones"]:cc["pair_ones"] + P] = np.kron(np.eye(2), np.ones((VD, VD)))
    restart = np.ones(T1)
    restart[[0] + [META + P * i for i in range(CHUNKS)]] = 0
    c[:, cc["restart"]:cc["restart"] + T1] = restart
    counts = np.array([[1 / min(i + 1, w) for i in range(16)] for w in WINDOWS])
    c[:, cc["first_counts"]:cc["first_counts"] + 64] = counts.reshape(-1)
    c[:, cc["eps"]] = EPS
    c[:, cc["slopes"]:cc["slopes"] + QH] = -2.0 ** (-8.0 * np.arange(1, QH + 1) / QH)
    s, q = np.arange(P)[:, None], np.arange(P)[None, :]
    masks = np.zeros((P, LEVELS, P), np.float32)
    for l in range(LEVELS):
        h = 2 ** l
        masks[:, l] = (s // (2 * h) == q // (2 * h)) & (s % (2 * h) < h) & (q % (2 * h) >= h)
    return c, masks.reshape(P, -1)


def attention_constants():
    import numpy as np

    a = np.zeros((P, 3 * P + 3 * 48), np.float32)
    distance = np.abs(np.arange(P)[:, None] + P - np.arange(3 * P)[None, :])
    a[:, 0:3 * P] = np.where(distance <= P, distance, -1e3 * NEG)
    x = np.arange(48)[None, :]
    for v, b in enumerate((0, 1, 3)):
        column = BC * b + np.arange(P)[:, None] % BC
        start = np.clip(column - BC // 2, 0, GRID_C - BC)
        key = BC * (b - 1) + x
        a[:, 3 * P + 48 * v:3 * P + 48 * (v + 1)] = np.where((key >= start) & (key < start + BC), 0, NEG)
    return a


def laid_out(inputs):
    import numpy as np

    a = {k: np.asarray(v) for k, v in inputs.items()}
    pc = columns()
    par = np.zeros((P, pc["all"]), np.float32)

    def put(name, v):
        v = v.reshape(-1, P).T
        par[:, pc[name]:pc[name] + v.shape[1]] = v
    put("lb0", a["lb_logits"][0])
    put("lb1", a["lb_logits"][1])
    put("norm1", a["norm1_g"])
    put("b_f", a["b_f"])
    put("head_g", a["head_norm_g"])
    put("pool_scale", a["pool_scale"])
    put("norm2", a["norm2_g"])
    put("conv_w", a["conv_w"])
    put("conv_b", a["conv_b"])
    put("final_g", a["final_norm_g"])
    put("mix_g", a["norm_mix_2"])
    put("ffn_g", a["norm_ffn_2"])
    put("mem_g", a["norm_mem_2"])
    put("out_g", a["norm_final_2"])
    par[:, pc["sink"]:pc["sink"] + QH] = a["sink_a_2"][0][None]
    out = {k: a[k] for k in ("x", "meta_tokens", "w_in", "w_pool", "w_out", "w_up", "w_down")}
    out["w_branch"] = np.concatenate([a["w_branch_a"][0], a["w_branch_b"][0]])
    out["parameters"] = par
    out["constants"], out["level_masks"] = constants()
    for k in ("mem_2", "w_in_a_2", "w_in_b_2", "w_mem_kv_2", "w_out_2", "w_gate_up_2", "w_down_2"):
        out[k] = a[k]
    padded = np.pad(a["rpb_b_2"][0], ((0, 0), (0, 0), (BC, BC + 1)))
    out["rpb"] = np.stack([padded[:, :, BC - 1 - c:4 * BC - 1 - c] for c in range(BC)], axis=1)
    out["attention_constants"] = attention_constants()
    return {k: np.ascontiguousarray(v) for k, v in out.items()}


def kernel(**inputs):
    import concourse.bacc as bacc
    import numpy as np
    from concourse.bass_utils import run_bass_kernel_spmd

    arrays = laid_out(inputs)
    nc = bacc.Bacc("TRN2", target_bir_lowering=False, num_devices=1)
    t = {k: nc.dram_tensor(k, v.shape, mybir.dt.from_np(v.dtype), kind="ExternalInput").ap()
         for k, v in arrays.items()}
    t["out"] = nc.dram_tensor("out", (1, SEQ, D), F32, kind="ExternalOutput").ap()
    build(nc, t)
    return run_bass_kernel_spmd(nc, [arrays], core_ids=[0]).results[0]["out"]
```
